# Optimizing a Trainium2 kernel written in Bass

```python
import math
import jax, jax.numpy as jnp
from jax import lax
import numpy as np

D_MODEL = 1024
BATCH = 1
SEQ = 1024
DEPTH = 1

HEAD_DIM = 64
SWA_Q_HEADS = 8
SWA_KV_HEADS = 2
SWA_GROUP = SWA_Q_HEADS // SWA_KV_HEADS
WINDOW = 128
FOX_HEADS = 4
MLA_HEADS = 4
MLA_Q_RANK = 256
MLA_KV_RANK = 128
MLA_NOPE_DIM = 64
MLA_ROPE_DIM = 32
MLA_V_DIM = 64
ROPE_THETA = 10000.0
REL_BUCKETS = 32
REL_MAX_DIST = 128
D_FF = 2816
CONV_WIDTH = 3
Q_BLOCK = 128
EPS = 1e-6
NEG_INF = -1e30

SWA_WIDTH = SWA_Q_HEADS * HEAD_DIM
FOX_WIDTH = FOX_HEADS * HEAD_DIM
MLA_WIDTH = MLA_HEADS * MLA_V_DIM
MIX_WIDTH = SWA_WIDTH + FOX_WIDTH + MLA_WIDTH
SWA_COLS = (SWA_Q_HEADS + 2 * SWA_KV_HEADS) * HEAD_DIM
FOX_COLS = 3 * FOX_HEADS * HEAD_DIM + FOX_HEADS
MLA_COLS = MLA_Q_RANK + MLA_KV_RANK + MLA_ROPE_DIM
IN_COLS = SWA_COLS + FOX_COLS + MLA_COLS
MLA_QK_DIM = MLA_NOPE_DIM + MLA_ROPE_DIM


def rmsnorm(x, g):
    xf = x.astype(jnp.float32)
    y = xf * lax.rsqrt(jnp.mean(xf * xf, axis=-1, keepdims=True) + EPS) * g.astype(jnp.float32)
    return y.astype(x.dtype)

def t5_causal_bucket(dist):
    max_exact = REL_BUCKETS // 2
    d = jnp.maximum(dist, 0)
    log_ratio = jnp.log(jnp.maximum(d, 1).astype(jnp.float32) / max_exact) / math.log(REL_MAX_DIST / max_exact)
    large = max_exact + (log_ratio * (REL_BUCKETS - max_exact)).astype(jnp.int32)
    large = jnp.minimum(large, REL_BUCKETS - 1)
    return jnp.where(d < max_exact, d, large)

def apply_rope(t, cos, sin):
    t1, t2 = jnp.split(t, 2, axis=-1)
    return jnp.concatenate([t1 * cos - t2 * sin, t1 * sin + t2 * cos], axis=-1)

def swa_sink_attention(q, k, v, sinks, rel_bias):
    B, S = q.shape[0], q.shape[1]
    nb = S // WINDOW
    qb = q.reshape(B, nb, WINDOW, SWA_KV_HEADS, SWA_GROUP, HEAD_DIM)

    def band(t):
        tb = t.reshape(B, nb, WINDOW, SWA_KV_HEADS, HEAD_DIM)
        prev = jnp.pad(tb, ((0, 0), (1, 0), (0, 0), (0, 0), (0, 0)))[:, :-1]
        return jnp.concatenate([prev, tb], axis=2)

    kb, vb = band(k), band(v)
    qi = jnp.arange(WINDOW, dtype=jnp.int32)[:, None] + WINDOW
    kj = jnp.arange(2 * WINDOW, dtype=jnp.int32)[None, :]
    dist = qi - kj
    in_band = (dist >= 0) & (dist < WINDOW)
    valid_key = (jnp.arange(nb)[:, None, None] > 0) | (kj >= WINDOW)[None]
    mask = in_band[None] & valid_key
    bias = rel_bias.astype(jnp.float32)[t5_causal_bucket(dist)]
    bias = bias.transpose(2, 0, 1).reshape(SWA_KV_HEADS, SWA_GROUP, WINDOW, 2 * WINDOW)
    s = jnp.einsum('bnqhgd,bnkhd->bnhgqk', qb, kb, preferred_element_type=jnp.float32)
    s = s * (HEAD_DIM ** -0.5) + bias
    s = jnp.where(mask[None, :, None, None], s, NEG_INF)
    sink = sinks.astype(jnp.float32).reshape(1, 1, SWA_KV_HEADS, SWA_GROUP, 1, 1)
    sink = jnp.broadcast_to(sink, s.shape[:-1] + (1,))
    p = jax.nn.softmax(jnp.concatenate([s, sink], axis=-1), axis=-1)[..., :-1]
    o = jnp.einsum('bnhgqk,bnkhd->bnqhgd', p.astype(v.dtype), vb)
    return o.reshape(B, S, SWA_Q_HEADS * HEAD_DIM)

def blocked_causal_attention(q, k, v, scale, log_forget_cum=None):
    B, S, H = q.shape[0], q.shape[1], q.shape[2]
    nb = S // Q_BLOCK
    q_blocks = q.reshape(B, nb, Q_BLOCK, H, q.shape[-1]).swapaxes(0, 1)
    k_pos = jnp.arange(S, dtype=jnp.int32)
    if log_forget_cum is None:
        f_blocks, f_keys = None, None
    else:
        f_t = log_forget_cum.transpose(0, 2, 1)
        f_blocks = f_t.reshape(B, H, nb, Q_BLOCK).transpose(2, 0, 1, 3)
        f_keys = f_t

    def one_block(args):
        qb, fb, i = args
        s = jnp.einsum('bqhd,bkhd->bhqk', qb, k, preferred_element_type=jnp.float32) * scale
        if fb is not None:
            s = s + (fb[..., :, None] - f_keys[..., None, :])
        q_pos = i * Q_BLOCK + jnp.arange(Q_BLOCK, dtype=jnp.int32)
        s = jnp.where(k_pos[None, :] <= q_pos[:, None], s, NEG_INF)
        p = jax.nn.softmax(s, axis=-1)
        return jnp.einsum('bhqk,bkhd->bqhd', p.astype(v.dtype), v)

    out = lax.map(one_block, (q_blocks, f_blocks, jnp.arange(nb, dtype=jnp.int32)))
    return out.swapaxes(0, 1).reshape(B, S, H * v.shape[-1])

def causal_depthwise_conv(u, w, b):
    S = u.shape[1]
    up = jnp.pad(u, ((0, 0), (CONV_WIDTH - 1, 0), (0, 0)))
    y = b.astype(u.dtype)
    for tap in range(CONV_WIDTH):
        y = y + w[tap].astype(u.dtype) * up[:, tap:tap + S]
    return y

def first_inputs(seed: int = 0) -> dict:
    key = jax.random.key(seed)
    ks = jax.random.split(key, 20)
    L, D = DEPTH, D_MODEL
    f32 = jnp.float32

    def nrm(k, shape, scale):
        return jax.random.normal(k, shape, f32) * scale

    def gain(k, shape):
        return 1.0 + 0.05 * jax.random.normal(k, shape, f32)

    return {
        "x": jax.random.normal(ks[0], (BATCH, SEQ, D), f32),
        "attn_pre_norm": gain(ks[1], (L, D)),
        "w_in": nrm(ks[2], (L, D, IN_COLS), D ** -0.5),
        "forget_bias": 2.0 + 0.5 * jax.random.normal(ks[3], (L, FOX_HEADS), f32),
        "swa_sinks": nrm(ks[4], (L, SWA_Q_HEADS), 0.5),
        "rel_bias": nrm(ks[5], (REL_BUCKETS, SWA_Q_HEADS), 0.5),
        "q_latent_norm": gain(ks[6], (L, MLA_Q_RANK)),
        "w_uq": nrm(ks[7], (L, MLA_Q_RANK, MLA_HEADS * MLA_QK_DIM), MLA_Q_RANK ** -0.5),
        "kv_latent_norm": gain(ks[8], (L, MLA_KV_RANK)),
        "w_ukv": nrm(ks[9], (L, MLA_KV_RANK, MLA_HEADS * (MLA_NOPE_DIM + MLA_V_DIM)), MLA_KV_RANK ** -0.5),
        "group_norm": gain(ks[10], (L, MIX_WIDTH)),
        "w_out": nrm(ks[11], (L, MIX_WIDTH, D), MIX_WIDTH ** -0.5),
        "attn_post_norm": gain(ks[12], (L, D)),
        "ffn_pre_norm": gain(ks[13], (L, D)),
        "w_up": nrm(ks[14], (L, D, 2 * D_FF), D ** -0.5),
        "conv_w": nrm(ks[15], (L, CONV_WIDTH, 2 * D_FF), CONV_WIDTH ** -0.5),
        "conv_b": nrm(ks[16], (L, 2 * D_FF), 0.02),
        "w_down": nrm(ks[17], (L, D_FF, D), D_FF ** -0.5),
        "ffn_post_norm": gain(ks[18], (L, D)),
    }

def first_block(x, attn_pre_norm, w_in, forget_bias, swa_sinks, rel_bias, q_latent_norm, w_uq,
              kv_latent_norm, w_ukv, group_norm, w_out, attn_post_norm, ffn_pre_norm, w_up,
              conv_w, conv_b, w_down, ffn_post_norm):
    B, S, _ = x.shape
    pos = jnp.arange(S, dtype=jnp.float32)
    inv_freq = ROPE_THETA ** (-(jnp.arange(MLA_ROPE_DIM // 2, dtype=jnp.float32) * 2.0 / MLA_ROPE_DIM))
    ang = pos[:, None] * inv_freq[None, :]
    cos = jnp.cos(ang)[:, None, :].astype(x.dtype)
    sin = jnp.sin(ang)[:, None, :].astype(x.dtype)

    for l in range(DEPTH):
        h = rmsnorm(x, attn_pre_norm[l])
        proj = h @ w_in[l]
        a_cols, f_cols, m_cols = jnp.split(proj, [SWA_COLS, SWA_COLS + FOX_COLS], axis=-1)

        qa, ka, va = jnp.split(a_cols, [SWA_WIDTH, SWA_WIDTH + SWA_KV_HEADS * HEAD_DIM], axis=-1)
        out_a = swa_sink_attention(qa.reshape(B, S, SWA_Q_HEADS, HEAD_DIM),
                                   ka.reshape(B, S, SWA_KV_HEADS, HEAD_DIM),
                                   va.reshape(B, S, SWA_KV_HEADS, HEAD_DIM),
                                   swa_sinks[l], rel_bias)

        qf, kf, vf, f_logit = jnp.split(f_cols, [FOX_WIDTH, 2 * FOX_WIDTH, 3 * FOX_WIDTH], axis=-1)
        log_f = jax.nn.log_sigmoid(f_logit.astype(jnp.float32) + forget_bias[l].astype(jnp.float32))
        F = jnp.cumsum(log_f, axis=1)
        out_b = blocked_causal_attention(qf.reshape(B, S, FOX_HEADS, HEAD_DIM),
                                         kf.reshape(B, S, FOX_HEADS, HEAD_DIM),
                                         vf.reshape(B, S, FOX_HEADS, HEAD_DIM),
                                         HEAD_DIM ** -0.5, log_forget_cum=F)

        c_q, c_kv, k_rope = jnp.split(m_cols, [MLA_Q_RANK, MLA_Q_RANK + MLA_KV_RANK], axis=-1)
        qm = (rmsnorm(c_q, q_latent_norm[l]) @ w_uq[l]).reshape(B, S, MLA_HEADS, MLA_QK_DIM)
        q_nope, q_rope = jnp.split(qm, [MLA_NOPE_DIM], axis=-1)
        kv = (rmsnorm(c_kv, kv_latent_norm[l]) @ w_ukv[l]).reshape(B, S, MLA_HEADS, MLA_NOPE_DIM + MLA_V_DIM)
        k_nope, vm = jnp.split(kv, [MLA_NOPE_DIM], axis=-1)
        q_rope = apply_rope(q_rope, cos, sin)
        k_rope = jnp.broadcast_to(apply_rope(k_rope[:, :, None, :], cos, sin), (B, S, MLA_HEADS, MLA_ROPE_DIM))
        out_c = blocked_causal_attention(jnp.concatenate([q_nope, q_rope], axis=-1),
                                         jnp.concatenate([k_nope, k_rope], axis=-1),
                                         vm, MLA_QK_DIM ** -0.5)

        g_a, g_b, g_c = jnp.split(group_norm[l], [SWA_WIDTH, SWA_WIDTH + FOX_WIDTH])
        mixed = jnp.concatenate([rmsnorm(out_a, g_a), rmsnorm(out_b, g_b), rmsnorm(out_c, g_c)], axis=-1)
        x = x + rmsnorm(mixed @ w_out[l], attn_post_norm[l])

        h = rmsnorm(x, ffn_pre_norm[l])
        u = causal_depthwise_conv(h @ w_up[l], conv_w[l], conv_b[l])
        gate, up = jnp.split(u, 2, axis=-1)
        y = (jax.nn.gelu(gate, approximate=True) * up) @ w_down[l]
        x = x + rmsnorm(y, ffn_post_norm[l])
    return x


GRID_W = 64
CTX_LEN = 256
N_HEADS = 8
N_KV_HEADS = 2
GQA_GROUP = N_HEADS // N_KV_HEADS
ATT_WIDTH = N_HEADS * HEAD_DIM
KV_WIDTH = N_KV_HEADS * HEAD_DIM
CONV_WIDTH_2 = D_MODEL - ATT_WIDTH
CONV_GROUPS = 8
CONV_K = 3
BLOCK = 128
N_EXPERTS = 16
EC_CAPACITY_FACTOR = 2
D_EXPERT = 1024
IN_WIDTH = ATT_WIDTH + 2 * KV_WIDTH + 3 * CONV_WIDTH_2
SPLIT_POINTS = [ATT_WIDTH, ATT_WIDTH + KV_WIDTH, ATT_WIDTH + 2 * KV_WIDTH,
                ATT_WIDTH + 2 * KV_WIDTH + CONV_WIDTH_2, ATT_WIDTH + 2 * KV_WIDTH + 2 * CONV_WIDTH_2]


def rmsnorm_2(x, g):
    xf = x.astype(jnp.float32)
    r = xf * lax.rsqrt(jnp.mean(xf * xf, axis=-1, keepdims=True) + EPS)
    return (r * g.astype(jnp.float32)).astype(x.dtype)

def modulate(h, shift, scale):
    return h * (1 + scale) + shift

def axial_rope_tables(seq_len):
    rows = seq_len // GRID_W
    row = jnp.repeat(jnp.arange(rows), GRID_W, total_repeat_length=rows * GRID_W)
    col = jnp.tile(jnp.arange(GRID_W), rows)
    n_freq = HEAD_DIM // 4
    inv = ROPE_THETA ** (-jnp.arange(n_freq, dtype=jnp.float32) / n_freq)
    ang = jnp.concatenate([row.astype(jnp.float32)[:, None] * inv,
                           col.astype(jnp.float32)[:, None] * inv], axis=-1)
    return jnp.cos(ang), jnp.sin(ang)

def apply_rope_2(x, cos, sin):
    xf = x.astype(jnp.float32)
    half = HEAD_DIM // 2
    x1, x2 = xf[..., :half], xf[..., half:]
    cs, sn = cos[None, :, None, :], sin[None, :, None, :]
    return jnp.concatenate([x1 * cs - x2 * sn, x1 * sn + x2 * cs], axis=-1).astype(x.dtype)

def windowed_attention(q, k, v, k_ctx, v_ctx, sink):
    bsz, seq, _, hd = q.shape
    nb = seq // BLOCK
    scale = hd ** -0.5
    qb = q.reshape(bsz, nb, BLOCK, N_KV_HEADS, GQA_GROUP, hd)
    pad = ((0, 0), (BLOCK, BLOCK), (0, 0), (0, 0))
    kp = jnp.pad(k, pad).reshape(bsz, nb + 2, BLOCK, N_KV_HEADS, hd)
    vp = jnp.pad(v, pad).reshape(bsz, nb + 2, BLOCK, N_KV_HEADS, hd)
    kb = jnp.concatenate([kp[:, :-2], kp[:, 1:-1], kp[:, 2:]], axis=2)
    vb = jnp.concatenate([vp[:, :-2], vp[:, 1:-1], vp[:, 2:]], axis=2)
    s_loc = jnp.einsum('bnqkgd,bnjkd->bnkgqj', qb, kb).astype(jnp.float32) * scale
    s_ctx = jnp.einsum('bnqkgd,bjkd->bnkgqj', qb, k_ctx).astype(jnp.float32) * scale
    i = jnp.arange(BLOCK)[None, :, None]
    j = jnp.arange(3 * BLOCK)[None, None, :]
    kpos = jnp.arange(nb)[:, None, None] * BLOCK + j - BLOCK
    valid = (jnp.abs(j - BLOCK - i) <= WINDOW) & (kpos >= 0) & (kpos < seq)
    s_loc = jnp.where(valid[None, :, None, None], s_loc, -jnp.inf)
    sk = jnp.broadcast_to(sink.astype(jnp.float32).reshape(N_KV_HEADS, GQA_GROUP)[None, None, :, :, None, None],
                          s_loc.shape[:-1] + (1,))
    p = jax.nn.softmax(jnp.concatenate([sk, s_ctx, s_loc], axis=-1), axis=-1)
    n_ctx = k_ctx.shape[1]
    p_ctx = p[..., 1:1 + n_ctx].astype(v.dtype)
    p_loc = p[..., 1 + n_ctx:].astype(v.dtype)
    out = (jnp.einsum('bnkgqj,bjkd->bnqkgd', p_ctx, v_ctx)
           + jnp.einsum('bnkgqj,bnjkd->bnqkgd', p_loc, vb))
    return out.reshape(bsz, seq, N_HEADS * hd)

def context_attention(q, k, v, sink):
    bsz, n, _, hd = q.shape
    qg = q.reshape(bsz, n, N_KV_HEADS, GQA_GROUP, hd)
    s = jnp.einsum('bqkgd,bjkd->bkgqj', qg, k).astype(jnp.float32) * hd ** -0.5
    sk = jnp.broadcast_to(sink.astype(jnp.float32).reshape(N_KV_HEADS, GQA_GROUP)[None, :, :, None, None],
                          s.shape[:-1] + (1,))
    p = jax.nn.softmax(jnp.concatenate([sk, s], axis=-1), axis=-1)[..., 1:].astype(v.dtype)
    return jnp.einsum('bkgqj,bjkd->bqkgd', p, v).reshape(bsz, n, N_HEADS * hd)

def short_conv_mixer(bg, cg, hv, conv_w):
    u = cg * hv
    up = jnp.pad(u, ((0, 0), (1, 1), (0, 0)))
    y = conv_w[0] * up[:, :-2] + conv_w[1] * up[:, 1:-1] + conv_w[2] * up[:, 2:]
    return bg * y

def expert_choice_ffn(h, w_router, w_gate, w_up, w_down):
    bsz, n, d = h.shape
    cap = EC_CAPACITY_FACTOR * n // N_EXPERTS
    aff = jax.nn.softmax((h @ w_router).astype(jnp.float32), axis=-1)
    g, idx = lax.top_k(jnp.swapaxes(aff, 1, 2), cap)
    xs = jax.vmap(lambda hb, ib: hb[ib])(h, idx)
    a = jnp.einsum('becd,edf->becf', xs, w_gate)
    u = jnp.einsum('becd,edf->becf', xs, w_up)
    y = jnp.einsum('becf,efd->becd', jax.nn.silu(a) * u, w_down) * g[..., None].astype(h.dtype)
    flat = (idx + (jnp.arange(bsz) * n)[:, None, None]).reshape(-1)
    out = jax.ops.segment_sum(y.reshape(-1, d), flat, num_segments=bsz * n)
    return out.reshape(bsz, n, d)

def second_inputs(seed: int = 0) -> dict:
    key = jax.random.key(seed)
    ks = jax.random.split(key, 17)
    D = D_MODEL
    nrm = jax.random.normal
    f32 = jnp.float32
    return {
        "x": nrm(ks[0], (BATCH, SEQ, D), f32),
        "c": nrm(ks[1], (BATCH, D), f32),
        "ctx": nrm(ks[2], (BATCH, CTX_LEN, D), f32),
        "c_ctx": nrm(ks[3], (D,), f32),
        "w_ada": nrm(ks[4], (DEPTH, D, 6 * D), f32) * (0.5 * D ** -0.5),
        "b_ada": nrm(ks[5], (DEPTH, 6 * D), f32) * 0.01,
        "g_mix": 1.0 + 0.1 * nrm(ks[6], (DEPTH, D), f32),
        "w_in": nrm(ks[7], (DEPTH, D, IN_WIDTH), f32) * D ** -0.5,
        "conv_w": nrm(ks[8], (DEPTH, CONV_K, CONV_WIDTH_2), f32) * CONV_K ** -0.5,
        "sink": nrm(ks[9], (DEPTH, N_HEADS), f32),
        "w_out": nrm(ks[10], (DEPTH, D, D), f32) * D ** -0.5,
        "g_ffn": 1.0 + 0.1 * nrm(ks[11], (DEPTH, D), f32),
        "w_router": nrm(ks[12], (DEPTH, D, N_EXPERTS), f32) * D ** -0.5,
        "w_gate": nrm(ks[13], (DEPTH, N_EXPERTS, D, D_EXPERT), f32) * D ** -0.5,
        "w_up": nrm(ks[14], (DEPTH, N_EXPERTS, D, D_EXPERT), f32) * D ** -0.5,
        "w_down": nrm(ks[15], (DEPTH, N_EXPERTS, D_EXPERT, D), f32) * D_EXPERT ** -0.5,
        "g_final": 1.0 + 0.1 * nrm(ks[16], (D,), f32),
    }

def second_block(x, c, ctx, c_ctx, w_ada, b_ada, g_mix, w_in, conv_w, sink, w_out, g_ffn,
              w_router, w_gate, w_up, w_down, g_final):
    bsz, seq, _ = x.shape
    cos, sin = axial_rope_tables(seq)
    for l in range(DEPTH):
        last = l == DEPTH - 1
        mod = jax.nn.silu(c) @ w_ada[l] + b_ada[l]
        sh1, sc1, gt1, sh2, sc2, gt2 = [m[:, None, :] for m in jnp.split(mod, 6, axis=-1)]
        mod_c = jax.nn.silu(c_ctx) @ w_ada[l] + b_ada[l]
        csh1, csc1, cgt1, csh2, csc2, cgt2 = jnp.split(mod_c, 6, axis=-1)

        hc = modulate(rmsnorm_2(ctx, g_mix[l]), csh1, csc1)
        n_ctx = ctx.shape[1]
        if last:
            kv_c = hc @ w_in[l][:, ATT_WIDTH:ATT_WIDTH + 2 * KV_WIDTH]
            k_c, v_c = jnp.split(kv_c, 2, axis=-1)
            k_c = k_c.reshape(bsz, n_ctx, N_KV_HEADS, HEAD_DIM)
            v_c = v_c.reshape(bsz, n_ctx, N_KV_HEADS, HEAD_DIM)
        else:
            q_c, k_c, v_c, bg_c, cg_c, hv_c = jnp.split(hc @ w_in[l], SPLIT_POINTS, axis=-1)
            q_c = q_c.reshape(bsz, n_ctx, N_HEADS, HEAD_DIM)
            k_c = k_c.reshape(bsz, n_ctx, N_KV_HEADS, HEAD_DIM)
            v_c = v_c.reshape(bsz, n_ctx, N_KV_HEADS, HEAD_DIM)
            att_c = context_attention(q_c, k_c, v_c, sink[l])
            conv_c = short_conv_mixer(bg_c, cg_c, hv_c, conv_w[l])
            ctx_new = ctx + cgt1 * (jnp.concatenate([att_c, conv_c], axis=-1) @ w_out[l])
            hc2 = modulate(rmsnorm_2(ctx_new, g_ffn[l]), csh2, csc2)
            ctx_new = ctx_new + cgt2 * expert_choice_ffn(hc2, w_router[l], w_gate[l], w_up[l], w_down[l])

        h = modulate(rmsnorm_2(x, g_mix[l]), sh1, sc1)
        q, k, v, bg, cg, hv = jnp.split(h @ w_in[l], SPLIT_POINTS, axis=-1)
        q = apply_rope_2(q.reshape(bsz, seq, N_HEADS, HEAD_DIM), cos, sin)
        k = apply_rope_2(k.reshape(bsz, seq, N_KV_HEADS, HEAD_DIM), cos, sin)
        v = v.reshape(bsz, seq, N_KV_HEADS, HEAD_DIM)
        att = windowed_attention(q, k, v, k_c, v_c, sink[l])
        conv = short_conv_mixer(bg, cg, hv, conv_w[l])
        x = x + gt1 * (jnp.concatenate([att, conv], axis=-1) @ w_out[l])

        h2 = modulate(rmsnorm_2(x, g_ffn[l]), sh2, sc2)
        x = x + gt2 * expert_choice_ffn(h2, w_router[l], w_gate[l], w_up[l], w_down[l])

        if not last:
            ctx = ctx_new
    return rmsnorm_2(x, g_final)


def setup_inputs(seed=0):
    out = dict(first_inputs(seed))
    for name, value in second_inputs(seed + 1).items():
        if name != "x":
            out[name + "_2"] = value
    return out


def reference(
    x, attn_pre_norm, w_in, forget_bias, swa_sinks, rel_bias, q_latent_norm, w_uq,
    kv_latent_norm, w_ukv, group_norm, w_out, attn_post_norm, ffn_pre_norm, w_up, conv_w,
    conv_b, w_down, ffn_post_norm, c_2, ctx_2, c_ctx_2, w_ada_2, b_ada_2, g_mix_2, w_in_2,
    conv_w_2, sink_2, w_out_2, g_ffn_2, w_router_2, w_gate_2, w_up_2, w_down_2, g_final_2,
):
    x = first_block(
        x, attn_pre_norm, w_in, forget_bias, swa_sinks, rel_bias, q_latent_norm, w_uq,
        kv_latent_norm, w_ukv, group_norm, w_out, attn_post_norm, ffn_pre_norm, w_up, conv_w,
        conv_b, w_down, ffn_post_norm,
    )
    return second_block(
        x, c_2, ctx_2, c_ctx_2, w_ada_2, b_ada_2, g_mix_2, w_in_2, conv_w_2, sink_2, w_out_2,
        g_ffn_2, w_router_2, w_gate_2, w_up_2, w_down_2, g_final_2,
    )


_drawn_inputs = setup_inputs


def setup_inputs(seed=0):
    import zlib

    import numpy as np

    out = dict(_drawn_inputs(seed))
    spreads = {}
    factors = {'swa_sinks': 7.949,
     'conv_b': 3.275,
     'ctx_2': 6.707,
     'c_ctx_2': 3.308,
     'b_ada_2': 7.706,
     'sink_2': 8.0,
     'g_ffn_2': 5.123}
    for name, (base, spread) in spreads.items():
        noise = np.random.default_rng([zlib.crc32(name.encode()), seed]).standard_normal(out[name].shape)
        drawn = base * np.exp(spread * noise) if base else spread * noise
        out[name] = __import__('jax').numpy.asarray(drawn.astype(out[name].dtype))
    for name, factor in factors.items():
        out[name] = (out[name] * factor).astype(out[name].dtype)
    return out
```

```python
import math
from contextlib import ExitStack

import numpy as np
import concourse.bass as bass
from concourse import mybir

F32 = mybir.dt.float32
BF16 = mybir.dt.bfloat16
U32 = mybir.dt.uint32
ALU = mybir.AluOpType
ACT = mybir.ActivationFunctionType
AX_X = mybir.AxisListType.X

P = 128
S = 1024
D = 1024
KT = D // P
NT = S // P
HALF = 512
HD = 64
EPS = 1e-6
NEG = -1e30
SWA_H = 8
CH = 8
QK = 96
FF = 2816
FT = FF // P
CTX = 256
NE = 16
CAP = 2 * S // NE
ROW = D + NE
ITEM = 2048

COLS = {}
_at = 0
for _n, _w in (("attn_pre", 8), ("group", 8), ("attn_post", 8), ("ffn_pre", 8), ("conv_w", 3 * 2 * FT),
               ("conv_b", 2 * FT), ("ffn_post", 8), ("qlat", 2), ("kvlat", 1), ("cvec", 8), ("cctx", 8),
               ("b_ada", 48), ("g_mix", 8), ("conv2", 12), ("g_ffn", 8)):
    COLS[_n] = (_at, _w)
    _at += _w
NCOLS = _at
CONST = {}
_at = 0
for _n, _w in (("ident", P), ("causal", P), ("left", P), ("ones", P), ("swap16", QK), ("swap32", P), ("flip", P), ("slot", 1)):
    CONST[_n] = (_at, _w)
    _at += _w
NCONST = _at

STOP = 99


def bass_two_blocks(nc, T):
    with ExitStack() as ctx:
        def sem(name):
            return ctx.enter_context(nc.semaphore(name))

        arena = ctx.enter_context(nc.sbuf_tensor("arena", [P, 51200], F32))
        cols = ctx.enter_context(nc.sbuf_tensor("cols", [P, NCOLS], F32))
        const = ctx.enter_context(nc.sbuf_tensor("const", [P, NCONST], F32))
        tiny = ctx.enter_context(nc.sbuf_tensor("tiny", [P, 480], F32))
        maskbf = ctx.enter_context(nc.sbuf_tensor("maskbf", [P, 3, P], BF16))
        ps = ctx.enter_context(nc.psum_tensor("ps", [P, 8, 512], F32))

        def view(kb, n):
            at = int(kb * 256)
            return arena[:, at:at + n]

        def view3(kb, a, b):
            return view(kb, a * b).rearrange("p (a b) -> p a b", a=a)

        def col(name, j=0, n=1):
            return cols[:, COLS[name][0] + j:COLS[name][0] + j + n]

        def con(name):
            return const[:, CONST[name][0]:CONST[name][0] + CONST[name][1]]

        def bank(b, n=512):
            return ps[:, b, 0:n]

        def banks(b, n):
            return ps[:, b:b + (n + 511) // 512, :].rearrange("p a b -> p (a b)")[:, 0:n]

        slot = [view(8 * s, ITEM) for s in range(12)]
        hT = view3(32, KT, S)
        mixed = view3(32, NT, D)
        QH = view3(64, CH, S)
        KH = view3(96, CH, S)
        xT = view3(96, KT, S)
        wv = view3(64, KT, 384)
        VH = view3(128, NT, 512)
        swaq = view3(144, 4, S)
        swak = view(160, S)
        swav = view3(164, NT, 128)
        swab = view3(168, SWA_H, 256)
        mflip = view3(76, SWA_H, 256)
        sq = [view(176, S), view(180, S)]
        ssq = view(184, S)
        rstdB = view(188, S)
        probs = [view(176, S), view(180, S)]
        probsT = [view(184, S), view(188, S)]
        cq = view3(176, 2, S)
        ckv = view(184, S)
        krope = view(188, S)
        rope1 = view3(192, 2, S)
        qstage = [view(32, S), view(36, S)]
        qs = view3(192, 4, P)
        ks = view(194, 384)
        qh = view(196, S)
        flog = view(24, S)
        ftmp = view(28, S)
        lat_sq = [view(32, S), view(36, S)]
        lat_ssq = view(40, S)
        lat_rstd = view(44, S)
        ropet = view(48, S)
        wuq = view3(52, 2, 4 * QK)
        wukv = view(56, 512)
        mixedT = view3(64, KT, S)
        zT = view3(128, KT, S)
        act = view3(128, FT, HALF)
        yT = view3(64, KT, HALF)
        convy = [[view(80 + 4 * b + 2 * g, HALF) for g in range(2)] for b in range(2)]
        gelu = [view(88 + 2 * b, HALF) for b in range(2)]
        carry = view(92, 2 * FT * 2).rearrange("p (a b) -> p a b", b=2)
        ctxT = view3(64, KT, CTX)
        hcT = view3(152, KT, CTX)
        q2 = view3(128, 4, S)
        k2 = view(144, S)
        v2 = view3(148, NT, 128)
        kc = view(160, CTX)
        vc = view3(161, 2, 128)
        rope2 = view3(162, 2, S)
        ropet2 = view(170, S)
        convu = view(192, S)
        convo = view(196, S)
        gt1o = [view(196 + 2 * b, HALF) for b in range(2)]
        att2 = view3(32, NT, 512)
        tok = [view(176, ROW), view(180.5, ROW)]
        aff = tiny[:, 0:128].rearrange("p (a b) -> p a b", a=NT)
        affT = view(128, S)[0:NE]
        work = view(132, S)[0:NE]
        pos = view(136, S)[0:NE]
        posbf = view(140, 512)[0:NE].bitcast(BF16)
        wr = view(142, KT * NE).rearrange("p (k e) -> p k e", k=KT)
        cntj = view(144, S)
        xs = [view(96, ROW), view(100.5, ROW)]
        xsT = [view3(106, KT, P), view3(110, KT, P)]
        sgate = view(114, S)
        actx = view(118, S)
        actT = view3(122, KT, P)
        yx = [view(148, S), view(152, S)]
        gt2B = view(156, D)
        g_fin = view(160, D)
        silu_b = view3(164, KT, P)
        fin = [view(96 + 4 * i, D) for i in range(8)]
        fsq = view(176, D)
        mod = tiny[:, 128:208].rearrange("p (a b) -> p a b", b=2)
        scT = tiny[:, 208:224].rearrange("p (k b) -> p k b", b=2)
        gsc = tiny[:, 224:248].rearrange("p (a b) -> p a b", b=8)
        sinkB = tiny[:, 248:264].rearrange("p (a b) -> p a b", b=8)
        epst = tiny[:, 264:265]
        nmax = tiny[:, 266:270]
        den = tiny[:, 270:274]
        esnk = tiny[:, 274:278]
        rec = tiny[:, 278:282]
        rmax = tiny[:, 282:286]
        gss = tiny[:, 286:310].rearrange("p (a b) -> p a b", b=3)
        grs = tiny[:, 310:334].rearrange("p (a b) -> p a b", b=3)
        fbias = tiny[:, 334:335]
        top8 = tiny[:, 336:344]
        rsum = tiny[:, 344:352]
        rmx = tiny[:, 352:360]
        idxf = tiny[:, 360:376]
        idxu = tiny[:, 376:392].bitcast(U32)
        idxs = [tiny[:, 392 + b:393 + b].bitcast(U32) for b in range(2)]
        gslot = [tiny[:, 396 + b:397 + b] for b in range(2)]
        fss = tiny[:, 400:408]
        pad = tiny[:, 416:417]
        gpad = tiny[:, 417:418]
        frs = tiny[:, 408:416]
        relb = view(192, 8)[0:32]
        onehot = view(193, 384)[0:32]
        extm = view(195, 384)[0:8]
        exts = view(197, 384)[0:8]

        ident, ones = con("ident"), con("ones")
        identb, causalb, leftb = maskbf[:, 0, :], maskbf[:, 1, :], maskbf[:, 2, :]

        ext_d = nc.dram_tensor("bias_line", (8, 384), F32, kind="Internal")
        h_d = nc.dram_tensor("routed_rows", (S, ROW), F32, kind="Internal").ap()
        acc_d = nc.dram_tensor("residual_rows", (S, D), F32, kind="Internal").ap()

        par = sem("params_loaded")
        xld = sem("x_loaded")
        wl = [sem(f"slot{s}_loaded") for s in range(12)]
        wu = [sem(f"slot{s}_used_by_expert") for s in range(12)]
        extra = sem("extra_loaded")
        s_bf = sem("masks_cast")
        s_sq = sem("square_done")
        s_add = sem("square_added")
        s_ssq = sem("squares_summed")
        s_stat = sem("sum_broadcast")
        s_rt = sem("root_done")
        s_h = sem("normalised")
        s_hb = sem("shifted")
        s_zn = sem("branch_scaled")
        s_x = sem("residual_added")
        tps = sem("tile_half_computed")
        evv = sem("tile_evacuated_dve")
        eva = sem("tile_evacuated_act")
        vch = sem("dve_chain")
        ach = sem("act_chain")
        gch = sem("pool_chain")
        s_f = sem("forget_abs_ready")
        s_fe = sem("forget_log_ready")
        s_fd = sem("forget_sum_ready")
        s_frow = sem("forget_row_placed")
        s_aug = sem("extra_rows_set")
        s_krc = sem("rope_key_copied")
        s_sw = sem("swapped_computed")
        s_rot = sem("rotated")
        s_bl = sem("bias_line_computed")
        s_bls = sem("bias_line_ready")
        s_bld = sem("bias_line_stored")
        s_bias = sem("bias_loaded")
        s_flip = sem("bias_in_order")
        s_rope = sem("rope1_loaded")
        s_lat = sem("latent_weights_loaded")
        s_stage = sem("query_staged")
        s_S = sem("scores_done")
        s_max = sem("max_done")
        s_exp = sem("exp_done")
        s_T = sem("probs_transposed")
        s_pt = sem("probs_evacuated")
        s_pv = sem("pv_done")
        s_o = sem("head_out_done")
        s_gq = sem("group_root")
        s_gn = sem("group_normalised")
        s_u = sem("ffn_pair_computed")
        s_ua = sem("conv_started")
        s_uv = sem("conv_done")
        s_gl = sem("gelu_done")
        s_act = sem("gated")
        s_silu = sem("silu_done")
        s_mod = sem("mod_computed")
        s_modv = sem("mod_evacuated")
        s_gsc = sem("mod_ready")
        s_cl = sem("context_loaded")
        s_cx = sem("context_proj")
        s_cxe = sem("context_evacuated")
        s_rp = sem("rope2_loaded")
        s_cv = sem("conv2_done")
        s_x3 = sem("gated_half_added")
        s_late = sem("late_params_loaded")
        s_lg = sem("logits_done")
        s_rm = sem("logits_shifted")
        s_re = sem("router_exp")
        s_aff = sem("affinity_done")
        s_tkst = [sem("rows_stored0"), sem("rows_stored1")]
        s_at = sem("affinity_transposed")
        s_pos = sem("positions_done")
        s_pb = sem("positions_broadcast")
        s_cnt = sem("positions_counted")
        s_idx = sem("indices_done")
        s_sb = sem("silu_columns_ready")
        s_g2 = sem("gate2_computed")
        s_g2e = sem("gate2_ready")
        s_gat = [sem("gathered0"), sem("gathered1")]
        s_xt = sem("rows_to_columns")
        s_xe = sem("columns_evacuated")
        s_sg = sem("silu_gate_done")
        s_ga = sem("expert_gated")
        s_at2 = sem("gated_transposed")
        s_ae = sem("gated_evacuated")
        s_ys = sem("expert_out_scaled")
        s_sc = [sem("scattered0"), sem("scattered1")]
        s_fl = [sem(f"final_loaded{i}") for i in range(8)]
        s_frt = sem("final_root")
        s_fo = sem("final_ready")
        s_out = sem("stored")

        block = ctx.enter_context(nc.Block())

        NPAR = 8
        NORM_K = [8, 2, 1, 8, 8, 8, 8, 8, 8, 8]
        NORM_N = [S, S, S, S, S, HALF, HALF, CTX, S, S]
        NORM_AT = [(sq, ssq, rstdB)] + [(lat_sq, lat_ssq, lat_rstd)] * 2 + [(sq, ssq, rstdB)] * 7

        class Chain:
            def __init__(self, eng, s):
                self.eng, self.s, self.base, self.k = eng, s, 0, 0

            def mark(self, ins):
                ins.then_inc(self.s, 1)
                self.k += 1

            def need(self):
                self.eng.wait_ge(self.s, self.base + self.k)

            def link(self, ins):
                self.mark(ins)
                self.need()

            def enter(self, it, per):
                self.static, self.per = self.base + self.k, per
                self.base, self.k = it * per + self.static, 0

            def leave(self, n):
                assert self.k == self.per, (self.k, self.per)
                self.base, self.k = self.static + n * self.per, 0

        PH = ["w_in", "w_out", "up0", "down0", "up1", "down1", "ada", "w_in2", "w_out2", "gate2", "expert"]
        USE = {"w_in": [2, 2, 2, 1], "w_out": [4, 4, 0, 0], "up0": [11, 11, 0, 0], "down0": [4, 4, 4, 4],
               "up1": [11, 11, 0, 0], "down1": [4, 4, 4, 4], "ada": [10, 10, 0, 0], "w_in2": [3, 2, 2, 2],
               "w_out2": [4, 4, 0, 0], "gate2": [1, 1, 1, 1], "expert": [16] * 12}

        def loads_before(ph, s):
            return sum(USE[p][s] if s < len(USE[p]) else 0 for p in PH[:PH.index(ph)])

        U_SWA, U_DENSE, U_ATT2, U_END = 0, 64, 128, 192
        T_V, T_IN, T_UQ, T_UKV, T_LV, T_MT, T_OUT, T_DN = 0, 4, 17, 21, 25, 29, 37, 45
        T_V2, T_IN2, T_AT, T_OUT2, T_XR, T_HR = 53, 57, 74, 78, 86, 94

        @block.sync
        def _(sp):
            sp.dma_start(cols[:], T["cols"]).then_inc(par, 16)
            sp.dma_start(const[:], T["const"]).then_inc(par, 16)
            sp.dma_start(fbias[0:4], T["forget_bias"].rearrange("a (h o) -> (a h) o", o=1)).then_inc(par, 16)
            sp.dma_start(sinkB[:, 0, :], T["swa_sinks"].to_broadcast([P, 8])).then_inc(par, 16)
            sp.dma_start(sinkB[:, 1, :], T["sink_2"].to_broadcast([P, 8])).then_inc(par, 16)
            sp.dma_start(relb, T["rel_bias"]).then_inc(par, 16)
            sp.dma_start(onehot, T["onehot"]).then_inc(par, 16)
            sp.dma_start(extm, T["extmask"]).then_inc(par, 16)
            sp.dma_start(xT, T["xT"]).then_inc(xld, 16)
            sp.dma_start(wv, T["w_in_v"]).then_inc(extra, 16)

            def load(s, src, n=ITEM, free=None):
                if free:
                    sp.wait_ge(*free)
                sp.dma_start(slot[s][:, 0:n], src).then_inc(wl[s], 16)

            for i in range(7):
                n = 2048 if i < 6 else 8 * QK
                if i == 4:
                    sp.wait_ge(s_bls, 1)
                    sp.dma_start(ext_d.ap(), exts).then_inc(s_bld, 16)
                    sp.wait_ge(s_bld, 16)
                    sp.dma_start(mflip, bass.AP(ext_d, 0, [[1, P], [384, 8], [1, 256]])).then_inc(s_bias, 16)
                    sp.dma_start(rope1[64:96], T["rope1"]).then_inc(s_rope, 16)
                load(i % 4, T["w_in"][:, i * ITEM:i * ITEM + n], n, (tps, 2 * (T_IN + 2 * (i - 4) + 2)) if i >= 4 else None)
            sp.wait_ge(tps, 2 * T_UQ)
            sp.dma_start(wuq, T["w_uq"]).then_inc(s_lat, 16)
            sp.dma_start(wukv, T["w_ukv"]).then_inc(s_lat, 16)
            sp.wait_ge(s_fd, 1)
            sp.wait_ge(s_aug, 2)
            sp.dma_start(KH[64:65, 0:4, :], flog[0:4, :]).then_inc(s_frow, 16)
            sp.wait_ge(s_frow, 16)
            wot = T["w_out"].rearrange("p (j b n) -> p j b n", j=4, b=2)
            for b in range(2):
                load(b, wot[:, 0, b, :], 8 * P)
            sp.wait_ge(s_S, U_ATT2)
            sp.dma_start(xT, T["xT"]).then_inc(xld, 16)
            with sp.Fori(1, 4) as j:
                for b in range(2):
                    load(b, wot[:, j, b, :], 8 * P, (tps, (j - 1) * 4 + 2 * (T_OUT + b + 1)))
            wup = T["w_up"].rearrange("p (j b n) -> p j b n", j=FT // 2, b=2)
            wdn = T["w_down"].rearrange("p (j b n) -> p j b n", j=4, b=4)
            for half in range(2):
                p0 = half * FT
                for b in range(2):
                    load(b, wup[:, 0, b, :], ITEM, (tps, 2 * (T_OUT + 6 + b + 1)) if half == 0 else (tps, 2 * (T_DN + 4)))
                with sp.Fori(1, FT // 2) as j:
                    for b in range(2):
                        load(b, wup[:, j, b, :], ITEM, (s_u, 2 * j + (p0 + b - 1)))
                for b in range(4):
                    free = (s_u, p0 + FT) if half == 0 or b < 2 else (tps, 2 * (T_DN + 4))
                    load(b, wdn[:, 0, b, :], 11 * P, free)
                with sp.Fori(1, 4) as j:
                    for b in range(4):
                        load(b, wdn[:, j, b, :], 11 * P, (tps, 2 * j + (2 * (T_DN + 4 * half - 1) + 1 + b // 2)))
            if STOP > 1:
                wad = T["w_ada"].rearrange("p (j b n) -> p j b n", j=10, b=2)
                for b in range(2):
                    load(b, wad[:, 0, b, :], ITEM, (tps, 2 * (T_DN + 8)))
                with sp.Fori(1, 10) as j:
                    for b in range(2):
                        load(b, wad[:, j, b, :], ITEM, (s_mod, 2 * j + (b - 1)))
                sp.wait_ge(s_x, 24)
                sp.dma_start(ctxT, T["ctxT"]).then_inc(s_cl, 16)
                sp.dma_start(rope2, T["rope2"]).then_inc(s_rp, 16)
                for i in range(9):
                    if i < 4:
                        free = (s_mod, 20) if i < 2 else (tps, 2 * (T_DN + 8))
                    else:
                        free = (tps, 2 * (T_IN2 + 1 + 2 * (i - 4)))
                    load(i % 4, T["w_in2"][:, i * ITEM:(i + 1) * ITEM], ITEM, free)
                wo2 = T["w_out2"].rearrange("p (j b n) -> p j b n", j=4, b=2)
                for b in range(2):
                    load(b, wo2[:, 0, b, :], 8 * P, (tps, 2 * T_AT))
                with sp.Fori(1, 4) as j:
                    for b in range(2):
                        load(b, wo2[:, j, b, :], 8 * P, (tps, (j - 1) * 4 + 2 * (T_OUT2 + b + 1)))
            if STOP > 2:
                wga = T["w_ada_2"].rearrange("l (k a p) n -> l k p a n", a=2, p=P)[0]
                sp.wait_ge(tps, 2 * (T_OUT2 + 8))
                for i in range(4):
                    sp.dma_start(slot[i].rearrange("p (a n) -> p a n", a=2), wga[i][:, :, 5 * D:6 * D]).then_inc(wl[i], 16)
                sp.wait_ge(evv, T_OUT2 + 8)
                sp.dma_start(gt2B, T["b_ada_2"][:, 5 * D:6 * D].to_broadcast([P, D])).then_inc(s_late, 16)
                sp.dma_start(g_fin, T["g_final_2"].rearrange("(a d) -> a d", a=1).to_broadcast([P, D])).then_inc(s_late, 16)
                sp.dma_start(wr, T["w_router_2"][0].rearrange("(k p) e -> p k e", p=P)).then_inc(s_late, 16)
                for i in range(2 * NT):
                    sp.wait_ge(evv, T_XR + i + 1)
                    sp.wait_ge(eva, T_XR + i + 1)
                    dst, n, t = (acc_d, D, i) if i < NT else (h_d, ROW, i - NT)
                    sp.dma_start(dst[t * P:(t + 1) * P, :], tok[i % 2][:, 0:n]).then_inc(s_tkst[i % 2], 16)
                wx = [T[n].rearrange("l e (j a p) n -> (l e) j p a n", a=2, p=P) for n in ("w_gate_2", "w_up_2", "w_down_2")]
                sp.wait_ge(tps, 2 * (T_HR + 8))
                sp.wait_ge(s_g2, 1)
                for s in range(12):
                    sp.dma_start(slot[s].rearrange("p (a n) -> p a n", a=2), wx[s // 4][0, s % 4]).then_inc(wl[s], 16)
                with sp.Fori(1, NE) as e:
                    for s in range(12):
                        sp.wait_ge(wu[s], e)
                        sp.dma_start(slot[s].rearrange("p (a n) -> p a n", a=2), wx[s // 4][e, s % 4]).then_inc(wl[s], 16)
                for b in range(2):
                    sp.wait_ge(s_sc[b], 16 * NE // 2)
                for i in range(NT):
                    sp.dma_start(fin[i], acc_d[i * P:(i + 1) * P, :]).then_inc(s_fl[i], 16)
                for i in range(NT):
                    sp.wait_ge(s_fo, i + 1)
                    sp.dma_start(T["out"][0, i * P:(i + 1) * P, :], fin[i]).then_inc(s_out, 16)
                sp.wait_ge(s_out, 16 * NT)
            if STOP <= 2:
                sp.wait_ge(s_x, 24)
                if STOP == 2:
                    sp.wait_ge(evv, T_OUT2 + 8)
                    sp.wait_ge(s_x3, 8)
                sp.dma_start(T["out"].rearrange("p (k s) -> p k s", k=KT), xT).then_inc(s_out, 16)
                sp.wait_ge(s_out, 16)

        @block.tensor
        def _(pe):
            def stat(i):
                pe.wait_ge(s_ssq, i + 1)
                n, s = NORM_N[i], NORM_AT[i][1]
                for c in range((n + 511) // 512):
                    m = pe.matmul(ps[:, 6 + c, 0:min(n, 512)], ones, s[:, c * 512:c * 512 + min(n, 512)], start=True, stop=True)
                m.then_inc(s_stat, 1)

            def tile_free(t, h):
                if not isinstance(t, int) or t >= 2:
                    pe.wait_ge(evv if h == 0 else eva, t - 1)

            def tile(t, b, lhs, rhs, nk, m=P, n=512):
                for h in range(2):
                    tile_free(t, h)
                    for k in range(nk):
                        i = pe.matmul(ps[0:m, 2 * b + h, 0:n], lhs(k, h), rhs(k, h), start=(k == 0), stop=(k == nk - 1))
                    i.then_inc(tps, 1)

            def turn(t, src):
                for h in range(2):
                    tile_free(t, h)
                    for j in range(4):
                        i = pe.transpose(ps[:, 2 * (t % 2) + h, j * P:(j + 1) * P], src(h, j), ident)
                    i.then_inc(tps, 1)

            def loaded(ph, s, j):
                pe.wait_ge(wl[s], j * 16 + 16 * (loads_before(ph, s) + 1))

            def wtile(s, a):
                return lambda k, h: slot[s][:, (a * KT + k) * P:(a * KT + k + 1) * P]

            def tokens(src):
                return lambda k, h: src[:, k, h * HALF:(h + 1) * HALF]

            def units(n, g, scores, cols_of, values, wait_stage):
                def after(s, v, u, least):
                    if not isinstance(g, int) or g + u >= least:
                        pe.wait_ge(s, g + (u + v))
                for u in range(n + 2):
                    if u < n:
                        after(s_exp, -1, u, 2)
                        scores(u).then_inc(s_S, 1)
                    if 1 <= u <= n:
                        w = u - 1
                        pe.wait_ge(s_exp, g + (w + 1))
                        after(s_pt, 0, w, 1)
                        for j in range(cols_of(w) // P):
                            i = pe.transpose(ps[:, 4 + j // 4, (j % 4) * P:(j % 4 + 1) * P], probs[w % 2][:, j * P:(j + 1) * P], ident)
                        i.then_inc(s_T, 1)
                    if u >= 2:
                        w = u - 2
                        pe.wait_ge(s_pt, g + (w + 1))
                        after(s_o, -1, w, 2)
                        nb = cols_of(w) // P
                        for j in range(nb):
                            i = pe.matmul(ps[:, 6 + w % 2, 0:HD], probsT[w % 2][:, j * P:(j + 1) * P], values(w, j),
                                          start=(j == 0), stop=(j == nb - 1))
                        i.then_inc(s_pv, 1)

            pe.wait_ge(par, 16 * NPAR)
            pe.matmul(ps[0:8, 4, 0:384], relb, onehot, start=True, stop=True).then_inc(s_bl, 1)
            stat(0)
            pe.wait_ge(s_h, 8)
            pe.wait_ge(extra, 16)
            pe.wait_ge(s_bias, 16)
            for c in range(4):
                m = pe.matmul(ps[:, 4 + c, :], con("flip"), mflip.rearrange("p a b -> p (a b)")[:, c * 512:(c + 1) * 512], start=True, stop=True)
            m.then_inc(s_flip, 1)
            for t in range(4):
                tile(T_V + t, t % 2, lambda k, h: hT[:, k, (2 * t + h) * P:(2 * t + h + 1) * P], lambda k, h: wv[:, k, :], KT, P, 384)
            for t in range(13):
                i, a = t // 2, t % 2
                if a == 0:
                    loaded("w_in", i % 4, i // 4)
                if t < 12:
                    tile(T_IN + t, (T_IN + t) % 2, wtile(i % 4, a), tokens(hT), KT)
                else:
                    tile(T_IN + t, (T_IN + t) % 2, lambda k, h: slot[i % 4][:, k * QK:(k + 1) * QK], tokens(hT), KT, QK)

            def swapped(i, src):
                if i:
                    pe.wait_ge(s_rot, i)
                for h in range(2):
                    m = pe.matmul(ps[0:QK, 4 + h, :], con("swap16")[64:96], src[64:96, h * HALF:(h + 1) * HALF], start=True, stop=True)
                m.then_inc(s_sw, 1)

            pe.wait_ge(eva, T_UQ)
            pe.wait_ge(evv, T_UQ)
            pe.wait_ge(s_bls, 1)
            swapped(0, krope)
            stat(1)
            stat(2)
            pe.wait_ge(s_lat, 32)
            pe.wait_ge(s_h, 8 + 2 + 1)
            for h in range(4):
                tile(T_UQ + h, (T_UQ + h) % 2, lambda k, hf: wuq[:, k, h * QK:(h + 1) * QK], tokens(cq), 2, QK)
                pe.wait_ge(evv, T_UQ + h + 1)
                pe.wait_ge(eva, T_UQ + h + 1)
                swapped(1 + h, QH[:, 4 + h, :])
            for h in range(4):
                tile(T_UKV + h, (T_UKV + h) % 2, lambda k, hf: wukv[:, h * P:h * P + HD],
                     lambda k, hf: ckv[:, hf * HALF:(hf + 1) * HALF], 1, HD)
            wuv = wukv.rearrange("p (h c) -> p h c", c=P)[:, :, HD:P]
            for t in range(4):
                tile(T_LV + t, (T_LV + t) % 2, lambda k, h: ckv[:, (2 * t + h) * P:(2 * t + h + 1) * P], lambda k, h: wuv, 1, P, 256)

            pe.wait_ge(evv, T_MT)
            pe.wait_ge(eva, T_MT)
            pe.wait_ge(s_rot, 5)
            pe.wait_ge(s_krc, 1)
            pe.wait_ge(s_frow, 16)

            def swa(n, g):
                nk = P if isinstance(n, int) else 2 * P

                def scores(u):
                    r = HD * (u % 2)
                    if u == 0:
                        pe.wait_ge(s_stage, n + 1)
                    return pe.matmul(ps[:, 2 * (u % 2), 0:nk], qs[r:r + HD, u // 2, :], ks[r:r + HD, 0:nk], start=True, stop=True)

                def values(u, j):
                    c = HD * (u % 2)
                    if isinstance(n, int):
                        return swav[:, 0, c:c + HD]
                    return swav[:, bass.ds(n + (j - 1), 1), c:c + HD].rearrange("p a c -> p (a c)")
                units(8, g, scores, lambda u: nk, values, None)

            swa(0, 0)
            with pe.Fori(1, NT) as n:
                swa(n, n * 8)

            with pe.Fori(0, CH) as h:
                def scores(u):
                    if u == 0:
                        pe.wait_ge(s_stage, h + (NT + 1))
                    n = (u + 1) * P
                    for c in range((n + 511) // 512):
                        m = min(512, n - c * 512)
                        pe.matmul(ps[:, 2 * (u % 2) + c, 0:m], qh[0:QK, u * P:(u + 1) * P],
                                  KH[0:QK, bass.ds(h, 1), c * 512:c * 512 + m].rearrange("p a c -> p (a c)"), start=True, stop=(c * 512 + m < n))
                    return pe.matmul(ps[:, 2 * (u % 2) + u // 4, (u % 4) * P:(u % 4 + 1) * P], identb, causalb, start=False, stop=True)

                def values(u, j):
                    return VH[:, j, bass.ds(h * HD, HD)]
                units(8, h * 8 + U_DENSE, scores, lambda u: (u + 1) * P, values, None)

            pe.wait_ge(s_gn, 8)
            for k in range(KT):
                turn(T_MT + k, lambda h, j: mixed[:, 4 * h + j, k * P:(k + 1) * P])
            pe.wait_ge(evv, T_OUT)
            pe.wait_ge(eva, T_OUT)
            with pe.Fori(0, 4) as j:
                for b in range(2):
                    loaded("w_out", b, j)
                    tile(2 * j + (T_OUT + b), (T_OUT + b) % 2, wtile(b, 0), tokens(mixedT), KT)
            stat(3)
            stat(4)
            pe.wait_ge(s_h, 8 + 2 + 1 + 8)
            for half in range(2):
                p0 = half * FT
                with pe.Fori(0, FT // 2) as j:
                    for b in range(2):
                        loaded(f"up{half}", b, j)
                        pe.wait_ge(s_uv, 2 * j + (p0 + b + 1))
                        for g in range(2):
                            for k in range(KT):
                                i = pe.matmul(ps[:, 2 * b + g, :], wtile(b, g)(k, 0), hT[:, k, half * HALF:(half + 1) * HALF],
                                              start=(k == 0), stop=(k == KT - 1))
                        i.then_inc(s_u, 1)
                pe.wait_ge(s_act, p0 + FT + 1)
                with pe.Fori(0, 4) as j:
                    for h in range(2):
                        pe.wait_ge(evv if h == 0 else eva, j + (T_DN + 4 * half))
                        for q in range(2):
                            loaded(f"down{half}", 2 * h + q, j)
                            for k in range(11):
                                i = pe.matmul(ps[:, 4 + h, :], slot[2 * h + q][:, k * P:(k + 1) * P], act[:, 11 * q + k, :],
                                              start=(q == 0 and k == 0), stop=(q == 1 and k == 10))
                        i.then_inc(tps, 1)
                stat(5 + half)
            if STOP <= 1:
                return
            pe.wait_ge(s_silu, 1)
            pe.wait_ge(evv, T_V2)
            pe.wait_ge(eva, T_V2)
            with pe.Fori(0, 10) as j:
                for b in range(2):
                    loaded("ada", b, j)
                    pe.wait_ge(s_modv, 2 * j + (b + 1))
                    for a in range(2):
                        for k in range(KT):
                            i = pe.matmul(ps[:, 4 + b, 2 * a:2 * a + 2], wtile(b, a)(k, 0), scT[:, k, :], start=(k == 0), stop=(k == KT - 1))
                    i.then_inc(s_mod, 1)
            stat(7)
            stat(8)
            loaded("w_in2", 0, 0)
            pe.wait_ge(s_hb, KT)
            for k in range(KT):
                pe.matmul(ps[:, 4, 0:CTX], wtile(0, 0)(k, 0), hcT[:, k, :], start=(k == 0), stop=(k == KT - 1))
            for t in range(2):
                for k in range(KT):
                    i = pe.matmul(ps[:, 5, t * P:(t + 1) * P], hcT[:, k, t * P:(t + 1) * P], wtile(0, 1)(k, 0), start=(k == 0), stop=(k == KT - 1))
            i.then_inc(s_cx, 1)
            pe.wait_ge(s_hb, 2 * KT)
            for t in range(4):
                tile(T_V2 + t, (T_V2 + t) % 2, lambda k, h: hT[:, k, (2 * t + h) * P:(2 * t + h + 1) * P], lambda k, h: wtile(0, 1)(k, 0), KT, P, P)

            def swapped2(i, src):
                pe.wait_ge(s_rot, 5 + i)
                for h in range(2):
                    m = pe.matmul(ps[:, 4 + h, :], con("swap32"), src[:, h * HALF:(h + 1) * HALF], start=True, stop=True)
                m.then_inc(s_sw, 1)

            pe.wait_ge(s_cxe, 2)
            for t in range(17):
                i, a = (t + 1) // 2, (t + 1) % 2
                if t == 0:
                    i, a = 0, 0
                elif a == 0:
                    loaded("w_in2", i % 4, i // 4)
                tile(T_IN2 + t, (T_IN2 + t) % 2, wtile(i % 4, a), tokens(hT), KT)
                if t < 5:
                    pe.wait_ge(evv, T_IN2 + t + 1)
                    pe.wait_ge(eva, T_IN2 + t + 1)
                    swapped2(t, k2 if t == 0 else q2[:, t - 1, :])
            pe.wait_ge(s_rot, 10)
            pe.wait_ge(s_cv, 4)

            def att(n, g, lo, hi, it):
                nl = (hi - lo + 1) * P
                at = 512 - nl

                def scores(u):
                    r, b = HD * (u % 2), 2 * (u % 2)
                    if u == 0:
                        pe.wait_ge(s_stage, it + (NT + CH + 1))
                    pe.matmul(ps[:, b, at:512], qs[r:r + HD, u // 2, :], ks[r:r + HD, 0:nl], start=True, stop=False)
                    if lo < 0:
                        pe.matmul(ps[:, b, at:at + P], identb, leftb, start=False, stop=(hi < 1))
                    if hi > 0:
                        pe.matmul(ps[:, b, 512 - P:512], identb, causalb, start=False, stop=True)
                    return pe.matmul(ps[:, b + 1, 0:CTX], qs[r:r + HD, u // 2, :], kc[r:r + HD, :], start=True, stop=True)

                def values(u, j):
                    c = HD * (u % 2)
                    if j >= nl // P:
                        return vc[:, j - nl // P, c:c + HD]
                    return v2[:, n + (lo + j), c:c + HD]
                units(8, g, scores, lambda u: nl + CTX, values, None)

            att(0, U_ATT2, 0, 1, 0)
            with pe.Fori(1, NT - 1) as n:
                att(n, n * 8 + U_ATT2, -1, 1, n)
            att(NT - 1, U_ATT2 + 8 * (NT - 1), -1, 0, NT - 1)
            pe.wait_ge(s_o, U_END)
            for k in range(4):
                turn(T_AT + k, lambda h, j: att2[:, 4 * h + j, k * P:(k + 1) * P])
            pe.wait_ge(evv, T_OUT2)
            pe.wait_ge(eva, T_OUT2)
            with pe.Fori(0, 4) as j:
                for b in range(2):
                    loaded("w_out2", b, j)
                    tile(2 * j + (T_OUT2 + b), (T_OUT2 + b) % 2, wtile(b, 0), tokens(mixedT), KT)
            if STOP <= 2:
                return
            stat(9)
            for i in range(NT):
                turn(T_XR + i, lambda h, j: xT[:, 4 * h + j, i * P:(i + 1) * P])
            pe.wait_ge(s_hb, 3 * KT)
            pe.wait_ge(s_late, 48)
            for i in range(NT):
                for k in range(KT):
                    m = pe.matmul(ps[:, 4, i * NE:(i + 1) * NE], hT[:, k, i * P:(i + 1) * P], wr[:, k, :], start=(k == 0), stop=(k == KT - 1))
            m.then_inc(s_lg, 1)
            for i in range(NT):
                turn(T_HR + i, lambda h, j: hT[:, 4 * h + j, i * P:(i + 1) * P])
            pe.wait_ge(s_aff, 1)
            for i in range(NT):
                m = pe.transpose(ps[0:NE, 5 + i // 4, (i % 4) * P:(i % 4 + 1) * P], aff[:, i, :], ident)
            m.then_inc(s_at, 1)
            pe.wait_ge(s_sb, 1)
            pe.wait_ge(evv, T_HR + 8)
            pe.wait_ge(eva, T_HR + 8)
            for k in range(KT):
                if k % 2 == 0:
                    loaded("gate2", k // 2, 0)
                for c in range(2):
                    m = pe.matmul(ps[:, 2 + c, :], silu_b[:, k, :], slot[k // 2][:, (k % 2) * D + c * 512:(k % 2) * D + (c + 1) * 512],
                                  start=(k == 0), stop=(k == KT - 1))
            m.then_inc(s_g2, 1)
            pe.wait_ge(s_pos, 1)
            for e in range(NE):
                if e >= 2:
                    pe.wait_ge(s_cnt, e - 1)
                for c in range(2):
                    b = 4 + 2 * (e % 2) + c
                    m = pe.matmul(ps[:, b, :], identb[0:NE, e:e + 1].to_broadcast([NE, P]), posbf[:, c * 512:(c + 1) * 512], start=True, stop=True)
                m.then_inc(s_pb, 1)
            pe.wait_ge(s_cnt, NE)
            pe.wait_ge(s_g2e, 1)
            with pe.Fori(0, NE // 2) as q:
                for b in range(2):
                    pe.wait_ge(s_gat[b], q * 16 + 16)
                    for k in range(KT):
                        m = pe.transpose(ps[:, 4 + k // 4, (k % 4) * P:(k % 4 + 1) * P], xs[b][:, k * P:(k + 1) * P], ident)
                    m.then_inc(s_xt, 1)
                    pe.wait_ge(s_xe, 2 * q + (b + 1))
                    for s in range(8):
                        pe.wait_ge(wl[s], q * 32 + 16 * (loads_before("expert", s) + b + 1))
                        for a in range(2):
                            k = 2 * (s % 4) + a
                            for c in range(2):
                                m = pe.matmul(ps[:, 2 * (s // 4) + c, :], xsT[b][:, k, :], slot[s][:, a * D + c * 512:a * D + (c + 1) * 512],
                                              start=(k == 0), stop=(k == KT - 1))
                        m.then_inc(wu[s], 1)
                    pe.wait_ge(s_ga, 2 * q + (b + 1))
                    for k in range(KT):
                        m = pe.transpose(ps[:, 4 + k // 4, (k % 4) * P:(k % 4 + 1) * P], actx[:, k * P:(k + 1) * P], ident)
                    m.then_inc(s_at2, 1)
                    pe.wait_ge(s_ae, 2 * q + (b + 1))
                    pe.wait_ge(s_ys, 2 * q + (b + 1))
                    for s in range(8, 12):
                        pe.wait_ge(wl[s], q * 32 + 16 * (loads_before("expert", s) + b + 1))
                        for a in range(2):
                            k = 2 * (s % 4) + a
                            for c in range(2):
                                m = pe.matmul(ps[:, 6 + c, :], actT[:, k, :], slot[s][:, a * D + c * 512:a * D + (c + 1) * 512],
                                              start=(k == 0), stop=(k == KT - 1))
                        m.then_inc(wu[s], 1)

        @block.scalar
        def _(act_e):
            ac = Chain(act_e, ach)
            sqn = [0, 0]

            def squares(i, src, ready):
                sqs, sm, _ = NORM_AT[i]
                n = NORM_N[i]
                for k in range(NORM_K[i]):
                    for w in (ready(k) or ()):
                        act_e.wait_ge(*w)
                    if k >= 3:
                        act_e.wait_ge(s_add, sqn[1] + k - 2)
                    act_e.activation(sm[:, 0:n] if k == 0 else sqs[k % 2][:, 0:n], src(k), ACT.Square).then_inc(s_sq, 1)
                sqn[1] += NORM_K[i] - 1

            def root(i):
                act_e.wait_ge(s_stat, i + 1)
                n = NORM_N[i]
                act_e.activation(NORM_AT[i][2][:, 0:n], banks(6, n), ACT.Sqrt, bias=epst, scale=1.0 / (P * NORM_K[i])).then_inc(s_rt, 1)

            act_e.wait_ge(par, 16 * NPAR)
            act_e.wait_ge(s_bf, 1)
            act_e.wait_ge(xld, 16)
            squares(0, lambda k: xT[:, k, :], lambda k: None)
            root(0)

            def half1(t, out, scale=None):
                act_e.wait_ge(tps, 2 * t + 2)
                return act_e.activation(out[0], out[1], ACT.Copy, scale=scale) if scale else act_e.activation(out[0], out[1], ACT.Copy)

            def b1(t):
                return 2 * (t % 2) + 1
            hi = slice(HALF, S)
            for t in range(4):
                g = T_V + t
                half1(g, (swav[:, 2 * t + 1, :], ps[:, b1(g), 0:P]))
                act_e.activation(VH[:, 2 * t + 1, 0:256], ps[:, b1(g), P:384], ACT.Copy).then_inc(eva, 1)
            for t in range(13):
                g = T_IN + t
                src = ps[:, b1(g), :]
                if t < 4:
                    half1(g, (swaq[:, t, hi], src), HD ** -0.5).then_inc(eva, 1)
                elif t == 4:
                    half1(g, (swak[:, hi], src)).then_inc(eva, 1)
                elif t < 9:
                    dst, h = (QH, 2 * (t - 5)) if t < 7 else (KH, 2 * (t - 7))
                    half1(g, (dst[0:HD, h, hi], src[0:HD]), HD ** -0.5 if t < 7 else None)
                    act_e.activation(dst[0:HD, h + 1, hi], src[HD:P], ACT.Copy, scale=HD ** -0.5 if t < 7 else 1.0).then_inc(eva, 1)
                elif t < 11:
                    half1(g, (cq[:, t - 9, hi], src)).then_inc(eva, 1)
                elif t == 11:
                    half1(g, (ckv[:, hi], src)).then_inc(eva, 1)
                else:
                    half1(g, (krope[64:96, hi], src[64:96]))
                    act_e.activation(flog[0:4, hi], src[0:4], ACT.Identity, bias=fbias[0:4]).then_inc(eva, 1)
            act_e.wait_ge(s_f, 1)
            ac.link(act_e.activation(ftmp[0:4], ftmp[0:4], ACT.Exp, scale=-1.0))
            act_e.activation(ftmp[0:4], ftmp[0:4], ACT.Ln, bias=1.0).then_inc(s_fe, 1)
            squares(1, lambda k: cq[:, k, :], lambda k: [(evv, T_UQ), (eva, T_UQ)])
            root(1)
            squares(2, lambda k: ckv, lambda k: [(s_h, 8 + 2)])
            root(2)
            for h in range(4):
                g = T_UQ + h
                half1(g, (QH[0:QK, 4 + h, hi], ps[0:QK, b1(g), :]), QK ** -0.5).then_inc(eva, 1)
            for h in range(4):
                g = T_UKV + h
                half1(g, (KH[0:HD, 4 + h, hi], ps[0:HD, b1(g), :])).then_inc(eva, 1)
            for t in range(4):
                g = T_LV + t
                half1(g, (VH[:, 2 * t + 1, 256:512], ps[:, b1(g), 0:256])).then_inc(eva, 1)

            def exps(n, g, cols_of, src, sink, prob_free=True):
                for u in range(n):
                    act_e.wait_ge(s_max, g + (u + 1))
                    if not isinstance(g, int) or g + u >= 2:
                        act_e.wait_ge(s_T, g + (u - 1))
                    w, c = cols_of(u), u % 4
                    last = act_e.activation(probs[u % 2][:, 0:w], src(u), ACT.Exp, bias=nmax[:, c:c + 1], accum_out=den[:, c:c + 1])
                    if sink is not None:
                        hd = u // 2 + 4 * (u % 2)
                        last = act_e.activation(esnk[:, c:c + 1], sinkB[:, sink, hd:hd + 1], ACT.Exp, bias=nmax[:, c:c + 1])
                    last.then_inc(s_exp, 1)

            def swa(n, g):
                w = P if isinstance(n, int) else 2 * P
                exps(8, g, lambda u: w, lambda u: probs[u % 2][:, 0:w], 0)
            swa(0, 0)
            with act_e.Fori(1, NT) as n:
                swa(n, n * 8)
            with act_e.Fori(0, CH) as h:
                exps(8, h * 8 + U_DENSE, lambda u: (u + 1) * P, lambda u: banks(2 * (u % 2), (u + 1) * P), None)
            act_e.wait_ge(s_o, U_ATT2)
            groups = ((0, 512), (512, 256), (768, 256))
            for i in range(NT):
                for j, (c, w) in enumerate(groups):
                    ac.mark(act_e.activation(sq[0][:, c:c + w], mixed[:, i, c:c + w], ACT.Square, accum_out=gss[:, i, j:j + 1]))
                ac.need()
            for j, (c, w) in enumerate(groups):
                last = act_e.activation(grs[:, :, j:j + 1], gss[:, :, j:j + 1], ACT.Sqrt, bias=epst, scale=1.0 / w)
                last.then_inc(s_gq, 1)
            for k in range(KT):
                g = T_MT + k
                act_e.wait_ge(tps, 2 * g + 2)
                act_e.activation(mixedT[:, k, hi], ps[:, b1(g), :], ACT.Copy, scale=col("group", k)).then_inc(eva, 1)
            with act_e.Fori(0, 4) as j:
                for b in range(2):
                    act_e.wait_ge(tps, 4 * j + (2 * (T_OUT + b) + 2))
                    act_e.activation(zT[:, 2 * j + b, hi], ps[:, b1(T_OUT + b), :], ACT.Copy).then_inc(eva, 1)
            squares(3, lambda k: zT[:, k, :], lambda k: [(evv, T_DN), (eva, T_DN)])
            root(3)
            squares(4, lambda k: xT[:, k, :], lambda k: [(s_x, k + 1)])
            root(4)
            for half in range(2):
                p0 = half * FT
                with act_e.Fori(0, FT // 2) as j:
                    for b in range(2):
                        g = 2 * j + (p0 + b)
                        act_e.wait_ge(s_u, g + 1)
                        act_e.wait_ge(s_act, g + 1)
                        for q in range(2):
                            t = 2 * j + (q * FT + b)
                            act_e.activation(convy[b][q], ps[:, 2 * b + q, :], ACT.Identity, bias=cols[:, bass.ds(t + COLS["conv_b"][0], 1)],
                                             scale=cols[:, bass.ds(t + (COLS["conv_w"][0] + 2 * 2 * FT), 1)]).then_inc(s_ua, 1)
                        act_e.wait_ge(s_uv, g + 3)
                        act_e.activation(gelu[b], convy[b][0], ACT.Gelu_apprx_tanh).then_inc(s_gl, 1)
                act_e.wait_ge(s_x, 8 + 8 * half)
                with act_e.Fori(0, 4) as j:
                    act_e.wait_ge(tps, 2 * j + (2 * (T_DN + 4 * half) + 2))
                    act_e.activation(yT[:, 2 * j + 1, :], ps[:, 5, :], ACT.Copy).then_inc(eva, 1)
                d = T_DN + 4 * half + 4
                squares(5 + half, lambda k: yT[:, k, :], lambda k: [(evv, d), (eva, d)])
                root(5 + half)
            if STOP <= 1:
                return
            act_e.activation(scT[:, :, 0:1], col("cvec", 0, 8), ACT.Silu)
            act_e.activation(scT[:, :, 1:2], col("cctx", 0, 8), ACT.Silu).then_inc(s_silu, 1)
            squares(7, lambda k: ctxT[:, k, :], lambda k: [(s_cl, 16)])
            root(7)
            squares(8, lambda k: xT[:, k, :], lambda k: [(s_x, 24), (s_h, 8 + 2 + 1 + 8 + 8)])
            root(8)

            def shift(i, base, dst, row, b):
                for k in range(KT):
                    act_e.wait_ge(s_h, base + k + 1)
                    act_e.activation(dst[:, k, :], dst[:, k, :], ACT.Identity, bias=mod[:, row + k, b:b + 1]).then_inc(s_hb, 1)
            shift(7, 19, hcT, 0, 1)
            shift(8, 27, hT, 0, 0)
            act_e.wait_ge(s_cx, 1)
            act_e.activation(vc[:, :, :], ps[:, 5, 0:2 * P].rearrange("p (a b) -> p a b", a=2), ACT.Copy).then_inc(s_cxe, 1)
            for t in range(4):
                g = T_V2 + t
                half1(g, (v2[:, 2 * t + 1, :], ps[:, b1(g), 0:P])).then_inc(eva, 1)
            for t in range(17):
                g = T_IN2 + t
                src = ps[:, b1(g), :]
                if t == 0:
                    half1(g, (k2[:, hi], src)).then_inc(eva, 1)
                elif t < 5:
                    half1(g, (q2[:, t - 1, hi], src), HD ** -0.5).then_inc(eva, 1)
                else:
                    act_e.wait_ge(evv, g + 1)
                    act_e.nop().then_inc(eva, 1)

            def att(g, nl):
                at = 512 - nl
                exps(8, g, lambda u: nl + CTX, lambda u: banks(2 * (u % 2), 1024)[:, at:512 + CTX], 1)
            att(U_ATT2, 2 * P)
            with act_e.Fori(1, NT - 1) as n:
                att(n * 8 + U_ATT2, 3 * P)
            att(U_ATT2 + 8 * (NT - 1), 2 * P)
            for k in range(4):
                half1(T_AT + k, (mixedT[:, k, hi], ps[:, b1(T_AT + k), :])).then_inc(eva, 1)
            with act_e.Fori(0, 4) as j:
                for b in range(2):
                    act_e.wait_ge(tps, 4 * j + (2 * (T_OUT2 + b) + 2))
                    act_e.wait_ge(s_x3, 2 * j + b + 1)
                    act_e.activation(gt1o[b], ps[:, b1(T_OUT2 + b), :], ACT.Copy, scale=mod[:, 2 * j + (16 + b), 0:1]).then_inc(eva, 1)
            if STOP <= 2:
                return
            squares(9, lambda k: xT[:, k, :], lambda k: [(evv, T_XR), (s_x3, 9)])
            root(9)
            shift(9, 35, hT, 24, 0)

            def rows(i):
                g = T_XR + i
                if i >= 2:
                    act_e.wait_ge(s_tkst[i % 2], 16 * (i // 2))
                half1(g, (tok[i % 2][:, HALF:D], ps[:, b1(g), :])).then_inc(eva, 1)
            for i in range(NT):
                rows(i)
            act_e.wait_ge(s_rm, 1)
            act_e.activation(aff, aff, ACT.Exp).then_inc(s_re, 1)
            for i in range(NT):
                rows(NT + i)
            with act_e.Fori(0, NE // 2) as q:
                for b in range(2):
                    act_e.wait_ge(s_xt, 2 * q + (b + 1))
                    act_e.activation(xsT[b].rearrange("p a b -> p (a b)"), banks(4, D), ACT.Copy).then_inc(s_xe, 1)
                    act_e.wait_ge(wu[3], 2 * q + (b + 1))
                    act_e.activation(sgate, banks(0, D), ACT.Silu).then_inc(s_sg, 1)
                    act_e.wait_ge(s_at2, 2 * q + (b + 1))
                    act_e.activation(actT.rearrange("p a b -> p (a b)"), banks(4, D), ACT.Copy).then_inc(s_ae, 1)
            for i in range(NT):
                act_e.wait_ge(s_fl[i], 16)
                ac.mark(act_e.activation(fsq, fin[i], ACT.Square, accum_out=fss[:, i:i + 1]))
                ac.need()
                act_e.activation(frs[:, i:i + 1], fss[:, i:i + 1], ACT.Sqrt, bias=epst, scale=1.0 / D).then_inc(s_frt, 1)

        @block.vector
        def _(v):
            vc_ = Chain(v, vch)
            done = [0, 0]

            def sums(i):
                sqs, sm, rs = NORM_AT[i]
                n = NORM_N[i]
                for k in range(1, NORM_K[i]):
                    v.wait_ge(s_sq, done[0] + k + 1)
                    if k > 1:
                        v.wait_ge(s_add, done[1] + k - 1)
                    v.tensor_tensor(sm[:, 0:n], sm[:, 0:n], sqs[k % 2][:, 0:n], ALU.add).then_inc(s_add, 1)
                done[0] += NORM_K[i]
                done[1] += NORM_K[i] - 1
                v.wait_ge(s_sq, done[0])
                if done[1]:
                    v.wait_ge(s_add, done[1])
                v.tensor_copy(rmax[:, 1:2], epst).then_inc(s_ssq, 1)

            def inverse(i):
                v.wait_ge(s_rt, i + 1)
                rs = NORM_AT[i][2][:, 0:NORM_N[i]]
                vc_.link(v.reciprocal(rs, rs))
                return rs

            vc_.mark(v.memset(epst, EPS))
            v.wait_ge(par, 16 * NPAR)
            vc_.mark(v.tensor_copy(identb, ident))
            vc_.mark(v.tensor_copy(causalb, con("causal")))
            vc_.mark(v.tensor_copy(leftb, con("left")))
            vc_.need()
            v.tensor_copy(rmax[:, 3:4], epst).then_inc(s_bf, 1)
            v.wait_ge(s_bl, 1)
            v.tensor_tensor(exts, ps[0:8, 4, 0:384], extm, ALU.add).then_inc(s_bls, 1)
            sums(0)
            rs = inverse(0)
            for k in range(KT):
                v.scalar_tensor_tensor(hT[:, k, :], xT[:, k, :], col("attn_pre", k), rs, ALU.mult, ALU.mult).then_inc(s_h, 1)

            def b0(t):
                return 2 * (t % 2)
            lo = slice(0, HALF)

            def half0(t, dst, src, scale=None):
                v.wait_ge(tps, 2 * t + 1)
                return v.tensor_scalar(dst, src, scale, None, ALU.mult) if scale else v.tensor_copy(dst, src)

            v.wait_ge(s_flip, 1)
            v.tensor_copy(swab.rearrange("p a b -> p (a b)"), banks(4, 2048))
            for t in range(4):
                g = T_V + t
                half0(g, swav[:, 2 * t, :], ps[:, b0(g), 0:P])
                v.tensor_copy(VH[:, 2 * t, 0:256], ps[:, b0(g), P:384]).then_inc(evv, 1)
            for t in range(13):
                g = T_IN + t
                src = ps[:, b0(g), :]
                if t < 4:
                    half0(g, swaq[:, t, lo], src, HD ** -0.5).then_inc(evv, 1)
                elif t == 4:
                    half0(g, swak[:, lo], src).then_inc(evv, 1)
                elif t < 9:
                    dst, h = (QH, 2 * (t - 5)) if t < 7 else (KH, 2 * (t - 7))
                    half0(g, dst[0:HD, h, lo], src[0:HD], HD ** -0.5 if t < 7 else None)
                    v.tensor_scalar(dst[0:HD, h + 1, lo], src[HD:P], HD ** -0.5 if t < 7 else 1.0, None, ALU.mult).then_inc(evv, 1)
                elif t < 11:
                    half0(g, cq[:, t - 9, lo], src).then_inc(evv, 1)
                elif t == 11:
                    half0(g, ckv[:, lo], src).then_inc(evv, 1)
                else:
                    half0(g, krope[64:96, lo], src[64:96])
                    v.tensor_scalar(flog[0:4, lo], src[0:4], fbias[0:4], None, ALU.add).then_inc(evv, 1)
            v.wait_ge(evv, T_UQ)
            v.wait_ge(eva, T_UQ)
            v.scalar_tensor_tensor(ftmp[0:4], flog[0:4], -1.0, flog[0:4], ALU.mult, ALU.max).then_inc(s_f, 1)
            v.wait_ge(s_fe, 1)
            vc_.link(v.tensor_scalar(flog[0:4], flog[0:4], 0.0, None, ALU.min))
            vc_.link(v.tensor_tensor(ftmp[0:4], flog[0:4], ftmp[0:4], ALU.subtract))
            vc_.link(v.tensor_tensor_scan(flog[0:4], ftmp[0:4], ftmp[0:4], 0.0, ALU.add, ALU.min))
            v.tensor_scalar(flog[0:4], flog[0:4], -1.0, None, ALU.mult).then_inc(s_fd, 1)
            sums(1)
            rs = inverse(1)
            for k in range(2):
                v.scalar_tensor_tensor(cq[:, k, :], cq[:, k, :], col("qlat", k), rs, ALU.mult, ALU.mult).then_inc(s_h, 1)
            sums(2)
            rs = inverse(2)
            v.scalar_tensor_tensor(ckv, ckv, col("kvlat"), rs, ALU.mult, ALU.mult).then_inc(s_h, 1)

            def rotate(i, x, c, s, tmp, r):
                v.wait_ge(s_sw, i + 1)
                vc_.mark(v.tensor_tensor(tmp[r], banks(4, S)[r], s[r], ALU.mult))
                vc_.link(v.tensor_tensor(x[r], x[r], c[r], ALU.mult))
                v.tensor_tensor(x[r], x[r], tmp[r], ALU.add).then_inc(s_rot, 1)

            r32 = slice(64, 96)
            v.wait_ge(s_rope, 16)
            rotate(0, krope, rope1[:, 0, :], rope1[:, 1, :], ropet, r32)
            for h in range(4):
                g = T_UQ + h
                half0(g, QH[0:QK, 4 + h, lo], ps[0:QK, b0(g), :], QK ** -0.5).then_inc(evv, 1)
                rotate(1 + h, QH[:, 4 + h, :], rope1[:, 0, :], rope1[:, 1, :], ropet, r32)
            for h in range(4):
                g = T_UKV + h
                half0(g, KH[0:HD, 4 + h, lo], ps[0:HD, b0(g), :]).then_inc(evv, 1)
            for t in range(4):
                g = T_LV + t
                half0(g, VH[:, 2 * t, 256:512], ps[:, b0(g), 0:256]).then_inc(evv, 1)

            def units(n, g, cols_of, maximum, sink, out):
                def after(s, d, u, least):
                    if not isinstance(g, int) or g + u >= least:
                        v.wait_ge(s, g + (u + d))
                for u in range(n + 2):
                    if u < n:
                        c = u % 4
                        v.wait_ge(s_S, g + (u + 1))
                        maximum(u, c, after)
                        if sink is not None:
                            hd = u // 2 + 4 * (u % 2)
                            v.tensor_scalar(nmax[:, c:c + 1], rmax[:, c:c + 1], sinkB[:, sink, hd:hd + 1], -1.0, ALU.max, ALU.mult).then_inc(s_max, 1)
                    if 1 <= u <= n:
                        w = u - 1
                        v.wait_ge(s_T, g + (w + 1))
                        after(s_pv, -1, w, 2)
                        v.tensor_copy(probsT[w % 2][:, 0:cols_of(w)], banks(4, cols_of(w))).then_inc(s_pt, 1)
                    if u >= 2:
                        w = u - 2
                        c = w % 4
                        v.wait_ge(s_pv, g + (w + 1))
                        if sink is not None:
                            vc_.link(v.tensor_tensor(den[:, c:c + 1], den[:, c:c + 1], esnk[:, c:c + 1], ALU.add))
                        vc_.link(v.reciprocal(rec[:, c:c + 1], den[:, c:c + 1]))
                        v.tensor_scalar(out(w), ps[:, 6 + w % 2, 0:HD], rec[:, c:c + 1], None, ALU.mult).then_inc(s_o, 1)

            def swa(n, g):
                w = P if isinstance(n, int) else 2 * P

                def maximum(u, c, after):
                    hd = u // 2 + 4 * (u % 2)
                    after(s_T, -1, u, 2)
                    v.memset(pad, 0.0)
                    vc_.link(v.tensor_tensor_reduce(probs[u % 2][:, 0:w], ps[:, 2 * (u % 2), 0:w], swab[:, hd, 256 - w:256], 1.0, -3e38,
                                                    ALU.add, ALU.max, rmax[:, c:c + 1]))
                hd = lambda u: u // 2 + 4 * (u % 2)
                units(8, g, lambda u: w, maximum, 0, lambda u: mixed[:, n, hd(u) * HD:(hd(u) + 1) * HD])
            swa(0, 0)
            with v.Fori(1, NT) as n:
                vc_.enter(n - 1, 24)
                swa(n, n * 8)
                vc_.leave(NT - 1)
            with v.Fori(0, CH) as h:
                vc_.enter(h, 8)

                def maximum(u, c, after):
                    v.tensor_reduce(nmax[:, c:c + 1], banks(2 * (u % 2), (u + 1) * P), AX_X, ALU.max, negate=True).then_inc(s_max, 1)
                units(8, h * 8 + U_DENSE, lambda u: (u + 1) * P, maximum, None, lambda u: mixed[:, u, bass.ds(h * HD + 512, HD)])
                vc_.leave(CH)
            v.wait_ge(s_gq, 3)
            vc_.link(v.reciprocal(grs, grs))
            for i in range(NT):
                for j, (c, w) in enumerate(((0, 512), (512, 256), (768, 256))):
                    last = v.tensor_scalar(mixed[:, i, c:c + w], mixed[:, i, c:c + w], grs[:, i, j:j + 1], None, ALU.mult)
                last.then_inc(s_gn, 1)
            for k in range(KT):
                g = T_MT + k
                v.wait_ge(tps, 2 * g + 1)
                v.tensor_scalar(mixedT[:, k, lo], ps[:, b0(g), :], col("group", k), None, ALU.mult).then_inc(evv, 1)
            with v.Fori(0, 4) as j:
                for b in range(2):
                    v.wait_ge(tps, 4 * j + (2 * (T_OUT + b) + 1))
                    v.tensor_copy(zT[:, 2 * j + b, lo], ps[:, b0(T_OUT + b), :]).then_inc(evv, 1)
            sums(3)
            rs = inverse(3)
            for k in range(KT):
                v.scalar_tensor_tensor(zT[:, k, :], zT[:, k, :], col("attn_post", k), rs, ALU.mult, ALU.mult).then_inc(s_zn, 1)
            sums(4)
            rs = inverse(4)
            for k in range(KT):
                v.scalar_tensor_tensor(hT[:, k, :], xT[:, k, :], col("ffn_pre", k), rs, ALU.mult, ALU.mult).then_inc(s_h, 1)
            v.memset(rmax[:, 0:1], 0.0).then_inc(s_uv, 1)
            v.memset(rmax[:, 1:2], 0.0).then_inc(s_uv, 1)
            v.memset(rmax[:, 2:3], 0.0).then_inc(s_act, 1)
            for half in range(2):
                p0 = half * FT
                per = (8 if half else 4) + 0
                with v.Fori(0, FT // 2) as j:
                    vc_.enter(j, 2 * per)
                    for b in range(2):
                        g = 2 * j + (p0 + b)
                        w0, w1 = COLS["conv_w"][0], COLS["conv_w"][0] + 2 * FT
                        v.wait_ge(s_ua, 2 * g + 2)
                        for q in range(2):
                            t = 2 * j + (q * FT + b)
                            vc_.mark(v.scalar_tensor_tensor(convy[b][q][:, 1:HALF], ps[:, 2 * b + q, 0:HALF - 1], cols[:, bass.ds(t + w1, 1)],
                                                            convy[b][q][:, 1:HALF], ALU.mult, ALU.add))
                            if half:
                                vc_.mark(v.scalar_tensor_tensor(convy[b][q][:, 0:1], carry[:, t, 1:2], cols[:, bass.ds(t + w1, 1)],
                                                                convy[b][q][:, 0:1], ALU.mult, ALU.add))
                        vc_.need()
                        for q in range(2):
                            t = 2 * j + (q * FT + b)
                            if half:
                                vc_.mark(v.scalar_tensor_tensor(convy[b][q][:, 0:2], carry[:, t, 0:2], cols[:, bass.ds(t + w0, 1)],
                                                                convy[b][q][:, 0:2], ALU.mult, ALU.add))
                            else:
                                vc_.mark(v.tensor_copy(carry[:, t, :], ps[:, 2 * b + q, HALF - 2:HALF]))
                            last = v.scalar_tensor_tensor(convy[b][q][:, 2:HALF], ps[:, 2 * b + q, 0:HALF - 2], cols[:, bass.ds(t + w0, 1)],
                                                          convy[b][q][:, 2:HALF], ALU.mult, ALU.add)
                            if half:
                                vc_.mark(last) if q == 0 else last.then_inc(s_uv, 1)
                            elif q == 1:
                                last.then_inc(s_uv, 1)
                        if half:
                            vc_.mark(v.memset(rmax[:, 3:4], 0.0))
                        v.wait_ge(s_gl, g + 1)
                        v.tensor_tensor(act[:, 2 * j + b, :], gelu[b], convy[b][1], ALU.mult).then_inc(s_act, 1)
                    vc_.leave(FT // 2)
                v.wait_ge(s_x, 8 + 8 * half)
                with v.Fori(0, 4) as j:
                    v.wait_ge(tps, 2 * j + (2 * (T_DN + 4 * half) + 1))
                    v.tensor_copy(yT[:, 2 * j, :], ps[:, 4, :]).then_inc(evv, 1)
                sums(5 + half)
                rs = inverse(5 + half)
                for k in range(KT):
                    v.scalar_tensor_tensor(yT[:, k, :], yT[:, k, :], col("ffn_post", k), rs, ALU.mult, ALU.mult).then_inc(s_zn, 1)
            if STOP <= 1:
                return
            v.memset(rmax[:, 0:1], 0.0).then_inc(s_modv, 1)
            v.memset(rmax[:, 1:2], 0.0).then_inc(s_modv, 1)
            with v.Fori(0, 10) as j:
                for b in range(2):
                    v.wait_ge(s_mod, 2 * j + (b + 1))
                    v.tensor_copy(mod[:, bass.ds(4 * j + 2 * b, 2), :], ps[:, 4 + b, 0:4].rearrange("p (a b) -> p a b", a=2)).then_inc(s_modv, 1)
            v.wait_ge(s_modv, 22)
            for b in range(2):
                vc_.mark(v.tensor_tensor(mod[:, :, b], mod[:, :, b], col("b_ada", 0, 40), ALU.add))
            vc_.need()
            for i, (row, b, g) in enumerate(((8, 0, "g_mix"), (8, 1, "g_mix"), (32, 0, "g_ffn"))):
                vc_.mark(v.scalar_tensor_tensor(gsc[:, i, :], mod[:, row:row + 8, b], 1.0, col(g, 0, 8), ALU.add, ALU.mult))
            vc_.need()
            sums(7)
            rs = inverse(7)
            for k in range(KT):
                v.scalar_tensor_tensor(hcT[:, k, :], ctxT[:, k, :], gsc[:, 1, k:k + 1], rs, ALU.mult, ALU.mult).then_inc(s_h, 1)
            sums(8)
            rs = inverse(8)
            for k in range(KT):
                v.scalar_tensor_tensor(hT[:, k, :], xT[:, k, :], gsc[:, 0, k:k + 1], rs, ALU.mult, ALU.mult).then_inc(s_h, 1)
            v.wait_ge(s_cx, 1)
            v.tensor_copy(kc, ps[:, 4, 0:CTX]).then_inc(s_cxe, 1)
            for t in range(4):
                g = T_V2 + t
                half0(g, v2[:, 2 * t, :], ps[:, b0(g), 0:P]).then_inc(evv, 1)
            v.wait_ge(s_rp, 16)
            for t in range(17):
                g = T_IN2 + t
                src = ps[:, b0(g), :]
                if t < 5:
                    x = k2 if t == 0 else q2[:, t - 1, :]
                    half0(g, x[:, lo], src, HD ** -0.5 if t else None).then_inc(evv, 1)
                    rotate(5 + t, x, rope2[:, 0, :], rope2[:, 1, :], ropet2, slice(0, P))
                    continue
                c, part = (t - 5) // 3, (t - 5) % 3
                both = banks(b0(g), S)
                v.wait_ge(tps, 2 * g + 2)
                if part == 0:
                    if c:
                        v.wait_ge(s_cv, c)
                    vc_.mark(v.tensor_copy(convu, both))
                    last = None
                    v.tensor_copy(rmax[:, 0:1], epst).then_inc(evv, 1)
                elif part == 1:
                    vc_.need()
                    vc_.link(v.tensor_tensor(convu, both, convu, ALU.mult))
                    v.tensor_copy(rmax[:, 0:1], epst).then_inc(evv, 1)
                    vc_.link(v.tensor_scalar(convo, convu, col("conv2", 4 + c), None, ALU.mult))
                    vc_.link(v.scalar_tensor_tensor(convo[:, 1:S], convu[:, 0:S - 1], col("conv2", c), convo[:, 1:S], ALU.mult, ALU.add))
                    vc_.link(v.scalar_tensor_tensor(convo[:, 0:S - 1], convu[:, 1:S], col("conv2", 8 + c), convo[:, 0:S - 1], ALU.mult, ALU.add))
                else:
                    vc_.link(v.tensor_tensor(mixedT[:, 4 + c, :], both, convo, ALU.mult))
                    v.tensor_copy(rmax[:, 0:1], epst).then_inc(evv, 1)
                    v.tensor_copy(rmax[:, 1:2], epst).then_inc(s_cv, 1)

            def att(n, g, nl):
                at = 512 - nl

                def maximum(u, c, after):
                    vc_.link(v.tensor_reduce(rmax[:, c:c + 1], banks(2 * (u % 2), 1024)[:, at:512 + CTX], AX_X, ALU.max))
                hd = lambda u: u // 2 + 4 * (u % 2)
                units(8, g, lambda u: nl + CTX, maximum, 1, lambda u: att2[:, n, hd(u) * HD:(hd(u) + 1) * HD])
            att(0, U_ATT2, 2 * P)
            with v.Fori(1, NT - 1) as n:
                vc_.enter(n - 1, 24)
                att(n, n * 8 + U_ATT2, 3 * P)
                vc_.leave(NT - 2)
            att(NT - 1, U_ATT2 + 8 * (NT - 1), 2 * P)
            for k in range(4):
                half0(T_AT + k, mixedT[:, k, lo], ps[:, b0(T_AT + k), :]).then_inc(evv, 1)
            with v.Fori(0, 4) as j:
                for b in range(2):
                    m = 2 * j + b
                    v.wait_ge(tps, 4 * j + (2 * (T_OUT2 + b) + 1))
                    v.scalar_tensor_tensor(xT[:, m, lo], ps[:, b0(T_OUT2 + b), :], mod[:, m + 16, 0:1], xT[:, m, lo], ALU.mult, ALU.add).then_inc(evv, 1)
            if STOP <= 2:
                return
            sums(9)
            rs = inverse(9)
            for k in range(KT):
                v.scalar_tensor_tensor(hT[:, k, :], xT[:, k, :], gsc[:, 2, k:k + 1], rs, ALU.mult, ALU.mult).then_inc(s_h, 1)

            def rows(i):
                if i >= 2:
                    v.wait_ge(s_tkst[i % 2], 16 * (i // 2))
                g = T_XR + i
                if i >= NT:
                    half0(g, tok[i % 2][:, 0:HALF], ps[:, b0(g), :])
                    v.tensor_copy(tok[i % 2][:, D:ROW], aff[:, i - NT, :]).then_inc(evv, 1)
                else:
                    half0(g, tok[i % 2][:, 0:HALF], ps[:, b0(g), :]).then_inc(evv, 1)
            for i in range(NT):
                rows(i)
            v.wait_ge(s_lg, 1)
            lg = ps[:, 4, 0:NT * NE].rearrange("p (a b) -> p a b", a=NT)
            vc_.link(v.tensor_reduce(rmx, lg, AX_X, ALU.max))
            v.tensor_tensor(aff, lg, rmx.unsqueeze(2).to_broadcast([P, NT, NE]), ALU.subtract).then_inc(s_rm, 1)
            v.wait_ge(s_re, 1)
            vc_.link(v.tensor_reduce(rsum, aff, AX_X, ALU.add))
            vc_.link(v.reciprocal(rsum, rsum))
            vc_.link(v.tensor_tensor(aff, aff, rsum.unsqueeze(2).to_broadcast([P, NT, NE]), ALU.mult))
            v.tensor_copy(rmax[:, 0:1], epst).then_inc(s_aff, 1)
            for i in range(NT):
                rows(NT + i)
            for k in range(KT):
                last = v.tensor_scalar(silu_b[:, k, :], ones, scT[:, k, 0:1], None, ALU.mult)
            last.then_inc(s_sb, 1)
            v.wait_ge(s_at, 1)
            vc_.link(v.tensor_copy(work, ps[0:NE, 5:7, :].rearrange("p a b -> p (a b)")))
            for _ in range(CAP // 8):
                vc_.link(v.max(top8[0:NE], work))
                vc_.link(v.match_replace(work, top8[0:NE], work, -1.0))
            vc_.link(v.tensor_scalar(work, work, 0.0, None, ALU.is_lt))
            vc_.link(v.tensor_tensor_scan(pos, work, work, 0.0, ALU.add, ALU.max))
            v.tensor_copy(posbf, pos).then_inc(s_pos, 1)
            v.wait_ge(s_g2, 1)
            v.wait_ge(s_late, 48)
            v.tensor_tensor(gt2B, banks(2, D), gt2B, ALU.add).then_inc(s_g2e, 1)
            for e in range(NE):
                if e:
                    v.wait_ge(s_cnt, e)
                v.wait_ge(s_pb, e + 1)
                v.tensor_scalar(cntj, banks(4 + 2 * (e % 2), S), con("slot"), None, ALU.is_le, ALU.add, accum_out=idxf[:, e:e + 1]).then_inc(s_cnt, 1)
            v.wait_ge(s_cnt, NE)
            v.tensor_copy(idxu, idxf).then_inc(s_idx, 1)
            v.memset(rmax[:, 0:1], 0.0).then_inc(s_ys, 1)
            with v.Fori(0, NE // 2) as q:
                for b in range(2):
                    v.wait_ge(s_gat[b], q * 16 + 16)
                    v.wait_ge(s_sg, 2 * q + (b + 1))
                    v.wait_ge(wu[7], 2 * q + (b + 1))
                    v.tensor_tensor(actx, banks(2, D), sgate, ALU.mult).then_inc(s_ga, 1)
                    v.tensor_copy(gslot[b], xs[b][:, bass.ds(2 * q + (D + b), 1)]).then_inc(vch, 1)
                    vc_.enter(q, 2) if b == 0 else None
                    vc_.k += 1
                    vc_.need()
                    v.wait_ge(wu[11], 2 * q + (b + 1))
                    v.scalar_tensor_tensor(yx[b], banks(6, D), gslot[b], gt2B, ALU.mult, ALU.mult).then_inc(s_ys, 1)
                vc_.leave(NE // 2)
            for i in range(NT):
                v.wait_ge(s_frt, i + 1)
                vc_.link(v.reciprocal(frs[:, i:i + 1], frs[:, i:i + 1]))
                v.scalar_tensor_tensor(fin[i], fin[i], frs[:, i:i + 1], g_fin, ALU.mult, ALU.mult).then_inc(s_fo, 1)

        @block.gpsimd
        def _(gp):
            gp.wait_ge(tps, 2 * T_IN)
            gp.memset(QH[64:96, 0:4, :], 1.0).then_inc(s_aug, 1)
            gp.wait_ge(s_h, 8)
            gp.memset(KH[64:96, 0:4, :], 0.0).then_inc(s_aug, 1)
            gp.wait_ge(s_aug, 2)
            gp.wait_ge(s_rot, 1)
            for h in range(4):
                last = gp.tensor_copy(KH[64:96, 4 + h, :], krope[64:96])
            last.then_inc(s_krc, 1)
            gp.wait_ge(s_krc, 1)
            gp.wait_ge(evv, T_MT)
            gp.wait_ge(eva, T_MT)
            gp.wait_ge(s_rot, 5)
            gp.tensor_copy(qs, swaq[:, :, 0:P])
            gp.tensor_copy(ks[:, 0:P], swak[:, 0:P]).then_inc(s_stage, 1)
            with gp.Fori(1, NT) as n:
                gp.wait_ge(s_S, n * 8)
                gp.tensor_copy(qs, swaq[:, :, bass.ds(n * P, P)])
                gp.tensor_copy(ks[:, 0:2 * P], swak[:, bass.ds(n * P - P, 2 * P)]).then_inc(s_stage, 1)
            gp.wait_ge(s_frow, 16)
            with gp.Fori(0, CH) as h:
                gp.wait_ge(s_S, h * 8 + U_DENSE)
                gp.tensor_copy(qh[0:QK], QH[0:QK, h, :]).then_inc(s_stage, 1)
            gp.wait_ge(xld, 32)
            for k in range(KT):
                gp.wait_ge(s_zn, k + 1)
                gp.tensor_tensor(xT[:, k, :], xT[:, k, :], zT[:, k, :], ALU.add).then_inc(s_x, 1)
            for half in range(2):
                hs = slice(half * HALF, (half + 1) * HALF)
                for k in range(KT):
                    gp.wait_ge(s_zn, KT * (1 + half) + k + 1)
                    gp.tensor_tensor(xT[:, k, hs], xT[:, k, hs], yT[:, k, :], ALU.add).then_inc(s_x, 1)
            if STOP <= 1:
                return
            gp.wait_ge(s_rot, 10)
            gp.wait_ge(s_cv, 4)
            n0 = NT + CH

            def stage(q0, k0, w):
                gp.tensor_copy(qs, q2[:, :, q0])
                gp.tensor_copy(ks[:, 0:w], k2[:, k0]).then_inc(s_stage, 1)
            stage(slice(0, P), slice(0, 2 * P), 2 * P)
            with gp.Fori(1, NT - 1) as n:
                gp.wait_ge(s_S, n * 8 + U_ATT2)
                stage(bass.ds(n * P, P), bass.ds(n * P - P, 3 * P), 3 * P)
            gp.wait_ge(s_S, U_ATT2 + 8 * (NT - 1))
            stage(slice(S - P, S), slice(S - 2 * P, S), 2 * P)
            gp.memset(gpad, 0.0).then_inc(s_x3, 1)
            with gp.Fori(0, 4) as j:
                for b in range(2):
                    m = 2 * j + b
                    gp.wait_ge(eva, 2 * j + (T_OUT2 + b + 1))
                    gp.tensor_tensor(xT[:, m, HALF:S], xT[:, m, HALF:S], gt1o[b], ALU.add).then_inc(s_x3, 1)
            if STOP <= 2:
                return
            gp.wait_ge(s_idx, 1)
            gp.wait_ge(s_tkst[0], 16 * NT)
            gp.wait_ge(s_tkst[1], 16 * NT)
            gc = Chain(gp, gch)

            def gather(e):
                b = e % 2
                gc.link(gp.tensor_copy(idxs[b], idxu[:, e:e + 1]))
                gp.indirect_dma_start(out=xs[b], out_offset=None, in_=h_d,
                                      in_offset=bass.IndirectOffsetOnAxis(ap=idxs[b], axis=0)).then_inc(s_gat[b], 16)
            for e in range(2):
                gather(e)
            for e in range(NE):
                b = e % 2
                gp.wait_ge(s_ys, e + 2)
                gp.indirect_dma_start(out=acc_d, out_offset=bass.IndirectOffsetOnAxis(ap=idxs[b], axis=0), in_=yx[b], in_offset=None,
                                      compute_op=ALU.add).then_inc(s_sc[b], 16)
                gp.wait_ge(s_sc[b], 16 * (e // 2 + 1))
                if e + 2 < NE:
                    gather(e + 2)


def _tiles(w, tile=P):
    k, n = w.shape
    return w.reshape(k // P, P, n // tile, tile).transpose(1, 2, 0, 3).reshape(P, -1)


def _cols(v):
    return np.asarray(v).reshape(-1, P).T


def _constants():
    r = np.arange(P)
    c = np.zeros((P, NCONST), np.float32)

    def put(name, a):
        c[:, CONST[name][0]:CONST[name][0] + CONST[name][1]] = a
    put("ident", np.eye(P))
    put("causal", np.where(r[None, :] <= r[:, None], 0.0, NEG))
    put("left", np.where(r[None, :] >= r[:, None], 0.0, NEG))
    put("ones", np.ones((P, P)))
    s16 = np.zeros((P, QK))
    for i in range(32):
        s16[64 + i, 64 + (i + 16) % 32] = 1.0
    put("swap16", s16)
    s32 = np.zeros((P, P))
    for i in range(P):
        s32[i, i // 64 * 64 + (i + 32) % 64] = 1.0
    put("swap32", s32)
    put("flip", np.eye(P)[::-1])
    put("slot", r[:, None])
    pos = np.arange(S, dtype=np.float32)
    inv = (np.float32(10000.0) ** (-(np.arange(16, dtype=np.float32) * np.float32(2.0) / np.float32(32)))).astype(np.float32)
    ang = pos[None, :] * inv[:, None]
    rope1 = np.stack([np.concatenate([np.cos(ang)] * 2), np.concatenate([-np.sin(ang), np.sin(ang)])], 1)
    inv2 = (np.float32(10000.0) ** (-np.arange(16, dtype=np.float32) / np.float32(16))).astype(np.float32)
    grid = np.arange(S)
    ang2 = np.concatenate([(grid // 64).astype(np.float32)[None] * inv2[:, None], (grid % 64).astype(np.float32)[None] * inv2[:, None]])
    rope2 = np.stack([np.concatenate([np.cos(ang2)] * 4), np.concatenate([-np.sin(ang2), np.sin(ang2)] * 2)], 1)
    dist = 255 - np.arange(384)
    d = np.maximum(dist, 0)
    ratio = np.log(np.maximum(d, 1).astype(np.float32) / np.float32(16)) / np.float32(math.log(128 / 16))
    large = np.minimum(16 + (ratio * np.float32(16)).astype(np.int32), 31)
    bucket = np.where(d < 16, d, large)
    onehot = (np.arange(32)[:, None] == bucket[None, :]).astype(np.float32)
    extmask = np.broadcast_to(np.where((dist >= 0) & (dist < P), 0.0, NEG), (8, 384))
    f = lambda a: np.ascontiguousarray(a, np.float32)
    return {"const": c, "rope1": f(rope1), "rope2": f(rope2), "onehot": onehot, "extmask": f(extmask)}


def _layout(x):
    a = {k: np.asarray(v) for k, v in x.items()}
    w = a["w_in"][0]
    pair = np.concatenate([np.r_[t * HD:(t + 1) * HD, (t + 4) * HD:(t + 5) * HD] for t in range(4)])
    sw, fx, ml = 0, 768, 768 + 772
    rope = ml + 384 + np.arange(32)
    order = np.concatenate([pair, 512 + np.arange(128), fx + np.arange(512), ml + np.arange(384)])
    last = np.concatenate([fx + 768 + np.arange(4), rope, rope[:28], rope])
    w2 = a["w_in_2"][0]
    conv = np.concatenate([768 + np.arange(c * P, (c + 1) * P) + o for c in range(4) for o in (512, 1024, 0)])
    order2 = np.concatenate([512 + np.arange(256), pair, conv])
    wup = a["w_up"][0].reshape(KT, P, 2, FT, P).transpose(1, 3, 2, 0, 4).reshape(P, -1)
    wdn = a["w_down"][0].reshape(FT, P, KT, P).transpose(1, 2, 0, 3).reshape(P, -1)
    cols = np.concatenate([_cols(v) for v in (
        a["attn_pre_norm"], a["group_norm"], a["attn_post_norm"], a["ffn_pre_norm"], a["conv_w"], a["conv_b"], a["ffn_post_norm"],
        a["q_latent_norm"], a["kv_latent_norm"], a["c_2"], a["c_ctx_2"], a["b_ada_2"], a["g_mix_2"], a["conv_w_2"], a["g_ffn_2"])], 1)
    out = {
        "xT": a["x"][0].T.reshape(KT, P, S).transpose(1, 0, 2), "ctxT": a["ctx_2"][0].T.reshape(KT, P, CTX).transpose(1, 0, 2),
        "w_in": np.concatenate([_tiles(w[:, order]), _tiles(w[:, last], QK)], 1),
        "w_in_v": w[:, np.r_[640:768, fx + 512:fx + 768]].reshape(KT, P, 384).transpose(1, 0, 2),
        "w_uq": a["w_uq"][0].reshape(2, P, 4 * QK).transpose(1, 0, 2), "w_ukv": a["w_ukv"][0],
        "w_out": _tiles(a["w_out"][0]), "w_up": wup, "w_down": wdn, "w_ada": _tiles(a["w_ada_2"][0][:, :5 * D]),
        "w_in2": _tiles(w2[:, order2]), "w_out2": _tiles(a["w_out_2"][0]), "cols": cols,
    }
    for n in ("forget_bias", "swa_sinks", "sink_2", "rel_bias", "w_ada_2", "b_ada_2", "g_final_2", "w_router_2", "w_gate_2", "w_up_2", "w_down_2"):
        out[n] = a[n]
    return out


def kernel(**inputs):
    import concourse.bacc as bacc
    from concourse.bass_utils import run_bass_kernel_spmd as run

    nc = bacc.Bacc("TRN2", target_bir_lowering=False, num_devices=1)
    arrays, T = {}, {}
    for name, x in {**_layout(inputs), **_constants()}.items():
        x = np.ascontiguousarray(x)
        arrays["in_" + name] = x
        T[name] = nc.dram_tensor("in_" + name, x.shape, mybir.dt.from_np(x.dtype), kind="ExternalInput").ap()
    shape = (1, S, D) if STOP > 2 else (P, KT * S)
    T["out"] = nc.dram_tensor("out_rows", shape, F32, kind="ExternalOutput").ap()
    bass_two_blocks(nc, T)
    r = run(nc, [arrays], core_ids=[0])
    return r.results[0]["out_rows"]
```

```python
import math
from contextlib import ExitStack

import numpy as np
import concourse.bass as bass
from concourse import mybir

F32 = mybir.dt.float32
F32R = mybir.dt.float32r
BF16 = mybir.dt.bfloat16
U32 = mybir.dt.uint32
ALU = mybir.AluOpType
ACT = mybir.ActivationFunctionType
AX_X = mybir.AxisListType.X

P = 128
S = 1024
D = 1024
KT = D // P
NT = S // P
HALF = 512
HD = 64
EPS = 1e-6
NEG = -1e30
SWA_H = 8
CH = 8
QK = 96
FF = 2816
FT = FF // P
CTX = 256
NE = 16
CAP = 2 * S // NE
PARTS = 3 * KT
RING = 4
ROW = D + NE
ADA = 3 * D // 2
ITEM = 2048

COLS = {}
_at = 0
for _n, _w in (("attn_pre", 8), ("group", 8), ("attn_post", 8), ("ffn_pre", 8), ("conv_w", 3 * 2 * FT),
               ("conv_b", 2 * FT), ("ffn_post", 8), ("qlat", 2), ("kvlat", 1), ("cvec", 8), ("cctx", 8),
               ("b_ada", 48), ("g_mix", 8), ("conv2", 12), ("g_ffn", 8)):
    COLS[_n] = (_at, _w)
    _at += _w
NCOLS = _at
CONST = {}
_at = 0
for _n, _w in (("ident", P), ("causal", P), ("left", P), ("mean", P), ("swap16", QK), ("swap32", P), ("flip", P), ("slot", 1)):
    CONST[_n] = (_at, _w)
    _at += _w
NCONST = _at

STOP = 99


def bass_two_blocks(nc, T):
    with ExitStack() as ctx:
        def sem(name):
            return ctx.enter_context(nc.semaphore(name))

        def split_views(*parts):
            out, at = [], 0
            with ExitStack() as early:
                for name, kb, shape in parts:
                    if kb * 256 > at:
                        early.enter_context(nc.sbuf_tensor(f"before_{name}", [P, kb * 256 - at], F32))
                    out.append(early.enter_context(nc.sbuf_tensor(name, [P] + shape, F32R)))
                    at = kb * 256 + int(np.prod(shape))
            return out

        w_hi, w_lo, h_hi, h_lo, a_hi, a_lo = split_views(("w_hi", 16, [2, D]), ("w_lo", 24, [2, D]), ("h_hi", 32, [KT, HALF]), ("h_lo", 48, [KT, HALF]),
                                                         ("a_hi", 192, [2, HALF]), ("a_lo", 196, [2, HALF]))
        g_hi, g_lo = split_views(("g_hi", 32, [KT, S]), ("g_lo", 64, [KT, S]))
        m_hi, m_lo = split_views(("m_hi", 64, [KT, S]), ("m_lo", 128, [KT, S]))
        x_hi, t_hi, x_lo, t_lo, e_hi, e_lo = split_views(("x_hi", 106, [2, KT, P]), ("t_hi", 122, [KT, P]), ("x_lo", 128, [2, KT, P]), ("t_lo", 136, [KT, P]),
                                                         ("e_hi", 168, [RING, D]), ("e_lo", 184, [RING, D]))
        arena = [ctx.enter_context(nc.sbuf_tensor(f"arena{i}", [P, n], F32)) for i, n in enumerate((96 * 256, 104 * 256))]
        cols = ctx.enter_context(nc.sbuf_tensor("cols", [P, NCOLS], F32))
        const = ctx.enter_context(nc.sbuf_tensor("const", [P, NCONST], F32))
        tiny = ctx.enter_context(nc.sbuf_tensor("tiny", [P, 480], F32))
        maskbf = ctx.enter_context(nc.sbuf_tensor("maskbf", [P, 3, P], BF16))
        ps = ctx.enter_context(nc.psum_tensor("ps", [P, 8, 512], F32))

        def view(kb, n):
            at = int(kb * 256)
            a = int(kb >= 96)
            return arena[a][:, at - a * 96 * 256:at - a * 96 * 256 + n]

        def view3(kb, a, b):
            return view(kb, a * b).rearrange("p (a b) -> p a b", a=a)

        def col(name, j=0, n=1):
            return cols[:, COLS[name][0] + j:COLS[name][0] + j + n]

        def con(name):
            return const[:, CONST[name][0]:CONST[name][0] + CONST[name][1]]

        def bank(b, n=512):
            return ps[:, b, 0:n]

        def banks(b, n):
            return ps[:, b:b + (n + 511) // 512, :].rearrange("p a b -> p (a b)")[:, 0:n]

        slot = [view(8 * s, ITEM) for s in range(12)]
        hT = view3(32, KT, S)
        mixed = view3(32, NT, D)
        QH = view3(64, CH, S)
        KH = view3(96, CH, S)
        xT = view3(96, KT, S)
        wv = view3(64, KT, 384)
        VH = view3(128, NT, 512)
        swaq = view3(144, 4, S)
        swak = view(160, S)
        swav = view3(164, NT, 128)
        swab = view3(168, SWA_H, 256)
        mflip = view3(76, SWA_H, 256)
        sq = [view(176, S), view(180, S)]
        ssq = view(184, S)
        rstdB = view(188, S)
        probs = [view(176, S), view(180, S)]
        probsT = [view(184, S), view(188, S)]
        cq = view3(176, 2, S)
        ckv = view(184, S)
        krope = view(188, S)
        rope1 = view3(192, 2, S)
        qstage = [view(32, S), view(36, S)]
        qs = [view3(192 + 4 * b, 4, P) for b in range(2)]
        ks = [view(194 + 4 * b, 384) for b in range(2)]
        qh = [view(192 + 4 * b, S) for b in range(2)]
        flog = view(24, S)
        ftmp = view(28, S)
        lat_sq = [view(32, S), view(36, S)]
        lat_ssq = view(40, S)
        lat_rstd = view(44, S)
        ropet = view(48, S)
        wuq = view3(52, 2, 4 * QK)
        wukv = view(56, 512)
        gsq = view(160, 512)
        attT = view3(48, 4, S)
        convm = view3(176, 4, S)
        late_probs = [view(64, S), view(68, S)]
        late_probsT = [view(72, S), view(76, S)]
        zT = view3(32, KT, S)
        act = view3(128, FT, HALF)
        yT = view3(64, KT, HALF)
        convy = [[view(80 + 4 * b + 2 * g, HALF) for g in range(2)] for b in range(2)]
        gelu = [view(88 + 2 * b, HALF) for b in range(2)]
        carry = view(92, 2 * FT * 2).rearrange("p (a b) -> p a b", b=2)
        adaA = [view(kb, 2 * D) for kb in (128, 136, 144, 152, 160, 84)]
        adaB = [view(kb, ADA) for kb in (160, 166, 192, 128, 134, 140, 146, 152)]
        rowA, rowB = view(176, 2 * D)[0:2], view(64, 2 * ADA)[0:2]
        ctxT = hcT = view3(80, KT, CTX)
        ctx_sq, ctx_ssq, ctx_rstd = [view(88, CTX), view(89, CTX)], view(93, CTX), view(94, CTX)
        q2 = view3(128, 4, S)
        k2 = view(144, S)
        v2 = view3(148, NT, 128)
        kc = view(160, CTX)
        vc = view3(161, 2, 128)
        rope2 = view3(162, 2, S)
        ropet2 = view(170, S)
        convu = view(192, S)
        convo = view(196, S)
        gt1o = [view(196 + 2 * b, HALF) for b in range(2)]
        att2 = view3(32, NT, 512)
        tok = [view(176, ROW), view(180.5, ROW)]
        aff = tiny[:, 0:128].rearrange("p (a b) -> p a b", a=NT)
        affT = view(128, S)[0:NE]
        work = view(132, S)[0:NE]
        lgT = view(128, S)[0:NE]
        pos = view(136, S)[0:NE]
        posbf = view(140, 512)[0:NE].bitcast(BF16)
        wr = view(142, KT * NE).rearrange("p (k e) -> p k e", k=KT)
        cntj = view(144, S)
        xs = [view(96, ROW), view(100.5, ROW)]
        sgate = view(114, S)
        actx = view(118, S)
        yx = [view(148, S), view(152, S)]
        gt2B = view(156, D)
        g_fin = view(160, D)
        silu_b = view3(164, KT, P)
        fin = [view(96 + 4 * i, D) for i in range(8)]
        fsq = view(176, D)
        mod = tiny[:, 128:208].rearrange("p (a b) -> p a b", b=2)
        scT = tiny[:, 208:224].rearrange("p (k b) -> p k b", b=2)
        gsc = tiny[:, 224:248].rearrange("p (a b) -> p a b", b=8)
        sinkB = tiny[:, 248:264].rearrange("p (a b) -> p a b", b=8)
        epst = tiny[:, 264:265]
        nmax = tiny[:, 266:270]
        den = tiny[:, 270:274]
        esnk = tiny[:, 274:278]
        rec = tiny[:, 278:282]
        rmax = tiny[:, 282:286]
        gss = tiny[:, 286:310].rearrange("p (a b) -> p a b", b=3)
        grs = tiny[:, 310:334].rearrange("p (a b) -> p a b", b=3)
        fbias = tiny[:, 334:335]
        top8 = tiny[:, 336:344]
        rsum = tiny[:, 344:352]
        rmx = tiny[:, 352:360]
        idxf = tiny[:, 360:376]
        idxu = tiny[:, 376:392].bitcast(U32)
        idxs = [tiny[:, 392 + b:393 + b].bitcast(U32) for b in range(2)]
        odxs = [tiny[:, 440 + b:441 + b].bitcast(U32) for b in range(2)]
        gslot = [tiny[:, 396 + b:397 + b] for b in range(2)]
        fss = tiny[:, 400:408]
        pad = tiny[:, 416:417]
        apad = tiny[:, 442:454]
        rms = [tiny[:, 420 + 8 * b:428 + 8 * b] for b in range(2)]
        gpad = tiny[:, 417:418]
        frs = tiny[:, 408:416]
        relb = view(192, 8)[0:32]
        onehot = view(193, 384)[0:32]
        extm = view(195, 384)[0:8]
        exts = view(197, 384)[0:8]

        ident = con("ident")
        identb, causalb, leftb = maskbf[:, 0, :], maskbf[:, 1, :], maskbf[:, 2, :]

        ext_d = nc.dram_tensor("bias_line", (8, 384), F32, kind="Internal")
        h_d = nc.dram_tensor("routed_rows", (S, ROW), F32, kind="Internal").ap()
        acc_d = nc.dram_tensor("residual_rows", (S, D), F32, kind="Internal").ap()

        par = sem("params_loaded")
        xld = sem("x_loaded")
        wl = [sem(f"slot{s}_loaded") for s in range(12)]
        s_ehi = sem("expert_weight_high_ready")
        s_elo = sem("expert_weight_low_ready")
        s_eu = sem("expert_weight_used")
        s_xhi = sem("columns_high_ready")
        s_thi = sem("gated_columns_high_ready")
        extra = sem("extra_loaded")
        s_bf = sem("masks_cast")
        s_sq = sem("square_done")
        s_add = sem("square_added")
        s_ssq = sem("squares_summed")
        s_stat = sem("sum_broadcast")
        s_zsq = sem("branch_square_done")
        s_zadd = sem("branch_square_added")
        s_rt = sem("root_done")
        s_dg = sem("inverse_root_on_diagonal")
        s_bc = sem("inverse_root_broadcast")
        s_rs = sem("inverse_root_ready")
        s_h = sem("normalised")
        s_hb = sem("shifted")
        s_zn = sem("branch_scaled")
        s_x = sem("residual_added")
        tps = sem("tile_half_computed")
        evv = sem("tile_evacuated_dve")
        eva = sem("tile_evacuated_act")
        vch = sem("dve_chain")
        ach = sem("act_chain")
        gch = sem("pool_chain")
        s_f = sem("forget_abs_ready")
        s_fe = sem("forget_log_ready")
        s_fd = sem("forget_sum_ready")
        s_frow = sem("forget_row_placed")
        s_aug = sem("extra_rows_set")
        s_krc = sem("rope_key_copied")
        s_sw = sem("swapped_computed")
        s_rot = sem("rotated")
        s_bl = sem("bias_line_computed")
        s_bls = sem("bias_line_ready")
        s_bld = sem("bias_line_stored")
        s_bias = sem("bias_loaded")
        s_flip = sem("bias_in_order")
        s_rope = sem("rope1_loaded")
        s_lat = sem("latent_weights_loaded")
        s_stage = sem("query_staged")
        s_S = sem("scores_done")
        s_max = sem("max_done")
        s_exp = sem("exp_done")
        s_T = sem("probs_transposed")
        s_pt = sem("probs_evacuated")
        s_pv = sem("pv_done")
        s_o = sem("head_out_done")
        s_gq = sem("group_root")
        s_gr = sem("group_inverse_ready")
        s_gn = sem("group_normalised")
        s_gna = sem("window_group_normalised")
        s_wl = [sem("stream_slot0_loaded"), sem("stream_slot1_loaded")]
        s_whi = sem("weight_high_ready")
        s_wlo = sem("weight_low_ready")
        s_wu = sem("weight_parts_used")
        s_ahi = sem("gated_high_ready")
        s_alo = sem("gated_low_ready")
        s_hhi = sem("input_part_ready")
        s_ua = sem("conv_started")
        s_uv = sem("conv_done")
        s_gl = sem("gelu_done")
        s_act = sem("gated")
        s_silu = sem("silu_done")
        s_al = [sem(f"modulation_loaded{i}") for i in range(6)]
        s_bl2 = [sem(f"later_modulation_loaded{i}") for i in range(8)]
        s_au = sem("modulation_weights_used")
        s_ad = sem("modulation_rows_computed")
        s_row = sem("modulation_rows_ready")
        s_mod = sem("modulation_columns_computed")
        xl = [sem(f"x_loaded{i}") for i in range(4)]
        s_cl = sem("context_loaded")
        s_cx = sem("context_proj")
        s_cxe = sem("context_evacuated")
        s_rp = sem("rope2_loaded")
        s_cv = sem("conv2_done")
        s_x3 = sem("gated_half_added")
        s_late = sem("late_params_loaded")
        s_lgT = sem("logits_computed")
        s_lgc = sem("logits_copied")
        s_lg = sem("logits_done")
        s_rm = sem("logits_shifted")
        s_re = sem("router_exp")
        s_aff = sem("affinity_done")
        s_tkst = [sem("rows_stored0"), sem("rows_stored1")]
        s_at = sem("affinity_transposed")
        s_pos = sem("positions_done")
        s_pb = sem("positions_broadcast")
        s_cnt = sem("positions_counted")
        s_idx = sem("indices_done")
        s_sb = sem("silu_columns_ready")
        s_g2 = sem("gate2_computed")
        s_g2e = sem("gate2_ready")
        s_gat = [sem("gathered0"), sem("gathered1")]
        s_yf = sem("expert_output_free")
        s_gs = sem("expert_affinity_kept")
        s_xt = sem("rows_to_columns")
        s_xe = sem("columns_evacuated")
        s_sg = sem("silu_gate_done")
        s_ga = sem("expert_gated")
        s_at2 = sem("gated_transposed")
        s_ae = sem("gated_evacuated")
        s_ys = sem("expert_out_scaled")
        s_sc = [sem("scattered0"), sem("scattered1")]
        s_fl = [sem(f"final_loaded{i}") for i in range(8)]
        s_frt = sem("final_root")
        s_fo = sem("final_ready")
        s_out = sem("stored")

        block = ctx.enter_context(nc.Block())

        NPAR = 8
        NORM_K = [8, 2, 1, 8, 8, 8, 8, 8, 8, 8]
        NORM_N = [S, S, S, S, S, HALF, CTX, HALF, S, S]
        NORM_PS = [6, 6, 6, 6, 6, 6, 5, 6, 6, 6]
        NORM_AT = [(sq, ssq, rstdB)] + [(lat_sq, lat_ssq, lat_rstd)] * 2 + [(sq, ssq, rstdB)] * 3 + [(ctx_sq, ctx_ssq, ctx_rstd)] + [(sq, ssq, rstdB)] * 2 + [(late_probs, late_probsT[0], late_probsT[1])]

        class Chain:
            def __init__(self, eng, s):
                self.eng, self.s, self.base, self.k = eng, s, 0, 0

            def mark(self, ins):
                ins.then_inc(self.s, 1)
                self.k += 1

            def need(self):
                self.eng.wait_ge(self.s, self.base + self.k)

            def link(self, ins):
                self.mark(ins)
                self.need()

            def enter(self, it, per):
                self.static, self.per = self.base + self.k, per
                self.base, self.k = it * per + self.static, 0

            def leave(self, n):
                assert self.k == self.per, (self.k, self.per)
                self.base, self.k = self.static + n * self.per, 0

        PH = ["w_in", "w_in2", "w_out2", "gate2", "expert"]
        USE = {"w_in": [2, 2, 2, 1], "w_in2": [0, 0, 0, 0],
               "w_out2": [4, 4, 0, 0], "gate2": [1, 1, 1, 1], "expert": [16] * 12}

        def loads_before(ph, s):
            return sum(USE[p][s] if s < len(USE[p]) else 0 for p in PH[:PH.index(ph)])

        U_SWA, U_DENSE, U_ATT2, U_END = 0, 64, 128, 192
        T_V, T_IN, T_UQ, T_UKV, T_LV, T_MT, T_OUT, T_DN = 0, 4, 17, 21, 25, 29, 37, 45
        T_V2, T_K2, T_IN2, T_AT, T_OUT2, T_XR, T_HR = (53, 54, 56, 57), 55, 57, 74, 78, 86, 94

        G_OUT, G_UP, G_DN, G_IN2 = 0, (4, 37), (26, 59), 70
        W_UP, W_DN = (0, 2 * FT + FT - 1), (2 * FT, 4 * FT + FT - 1)

        def in2_used(n):
            return tps, 2 * (T_K2 + 1 if n == 0 else T_V2[3] + 1 if n == 1 else T_IN2 + n)

        def parts_used(ph, half, g, q):
            if ph == "out":
                return tps, 4 * g + (2 * (T_OUT + q) + 2)
            if ph == "down" and isinstance(g, int) and g == FT // 2 - 1 and q == 1:
                return tps, 2 * (T_DN + 4 * half) + 8
            return s_wu, 2 * g + ((W_UP if ph == "up" else W_DN)[half] + q + 1)

        def expert_item(e, i):
            return PARTS * e + (KT + i)

        def expert_items(e, last):
            turn = [(1, e), (2, e)] if last else [(1, e), (0, e + 1), (2, e)]
            return [(j * KT + k, 4 * n + k // 2, k % 2, ee) for j, (n, ee) in enumerate(turn) for k in range(KT)]

        @block.sync
        def _(sp):
            sp.dma_start(cols[:], T["cols"]).then_inc(par, 16)
            sp.dma_start(const[:], T["const"]).then_inc(par, 16)
            sp.dma_start(fbias[0:4], T["forget_bias"].rearrange("a (h o) -> (a h) o", o=1)).then_inc(par, 16)
            sp.dma_start(sinkB[:, 0, :], T["swa_sinks"].to_broadcast([P, 8])).then_inc(par, 16)
            sp.dma_start(sinkB[:, 1, :], T["sink_2"].to_broadcast([P, 8])).then_inc(par, 16)
            sp.dma_start(relb, T["rel_bias"]).then_inc(par, 16)
            sp.dma_start(onehot, T["onehot"]).then_inc(par, 16)
            sp.dma_start(extm, T["extmask"]).then_inc(par, 16)
            for i in range(4):
                sp.dma_start(xT[:, 2 * i:2 * i + 2, :], T["xT"][:, 2 * i:2 * i + 2, :]).then_inc(xl[i], 16)
            ada = T["w_ada_2"].rearrange("l (k p) n -> (l k) p n", p=P)
            for k in range(6):
                sp.dma_start(adaA[k], ada[k, :, 0:2 * D]).then_inc(s_al[k], 16)
            sp.dma_start(wv, T["w_in_v"]).then_inc(extra, 16)

            def load(s, src, n=ITEM, free=None):
                if free:
                    sp.wait_ge(*free)
                sp.dma_start(slot[s][:, 0:n], src).then_inc(wl[s], 16)

            for i in range(7):
                if i == 2:
                    for k in range(6, KT):
                        sp.wait_ge(s_au, k - 5)
                        sp.dma_start(adaA[k - 6], ada[k, :, 0:2 * D]).then_inc(s_al[k - 6], 16)
                n = 2048 if i < 6 else 8 * QK
                if i == 4:
                    sp.wait_ge(s_bls, 1)
                    sp.dma_start(ext_d.ap(), exts).then_inc(s_bld, 16)
                    sp.wait_ge(s_bld, 16)
                    sp.dma_start(mflip, bass.AP(ext_d, 0, [[1, P], [384, 8], [1, 256]])).then_inc(s_bias, 16)
                    sp.dma_start(rope1[64:96], T["rope1"]).then_inc(s_rope, 16)
                load(i % 4, T["w_in"][:, i * ITEM:i * ITEM + n], n, (tps, 2 * (T_IN + 2 * (i - 4) + 2)) if i >= 4 else None)
            sp.wait_ge(tps, 2 * T_UQ)
            sp.dma_start(wuq, T["w_uq"]).then_inc(s_lat, 16)
            sp.dma_start(wukv, T["w_ukv"]).then_inc(s_lat, 16)
            sp.wait_ge(s_fd, 1)
            sp.wait_ge(s_aug, 2)
            sp.dma_start(KH[64:65, 0:4, :], flog[0:4, :]).then_inc(s_frow, 16)
            sp.wait_ge(s_frow, 16)
            def stream(g0, n, src):
                if g0 < 2:
                    for g in range(2):
                        sp.dma_start(slot[g], src[:, g, :]).then_inc(s_wl[g], 16)
                    stream(g0 + 2, n - 2, src[:, 2:, :])
                    return
                two = src[:, 0:n // 2 * 2, :].rearrange("p (m c) n -> p m c n", c=2)
                with sp.Fori(0, n // 2) as m:
                    for c in range(2):
                        sp.wait_ge(s_wlo, 4 * m + 2 * (g0 + c) - 2)
                        sp.dma_start(slot[(g0 + c) % 2], two[:, m, c, :]).then_inc(s_wl[(g0 + c) % 2], 16)
                if n % 2:
                    sp.wait_ge(s_wlo, 2 * (g0 + n - 1) - 2)
                    sp.dma_start(slot[(g0 + n - 1) % 2], src[:, n - 1, :]).then_inc(s_wl[(g0 + n - 1) % 2], 16)

            stream(G_OUT, KT // 2, T["w_out"].rearrange("p (g n) -> p g n", n=ITEM))
            sp.wait_ge(s_S, U_ATT2)
            sp.dma_start(xT, T["xT"]).then_inc(xld, 16)
            up0 = T["w_up"].rearrange("p (g n) -> p g n", n=ITEM)
            for g in range(2):
                sp.wait_ge(s_wlo, 2 * (G_UP[0] + g) - 2)
                sp.dma_start(slot[g], up0[:, g, :]).then_inc(s_wl[g], 16)
            for g in range(2):
                for k in range(KT):
                    if g == 0 and k == 3:
                        sp.wait_ge(tps, 2 * T_DN)
                    if g:
                        sp.wait_ge(s_au, KT - 1 + k + 1) if k < KT - 1 else sp.wait_ge(s_ad, 2)
                    sp.dma_start(adaB[k], ada[k, :, 2 * D + g * ADA:2 * D + (g + 1) * ADA]).then_inc(s_bl2[k], 16)
            for half in range(2):
                if half:
                    stream(G_UP[1], FT, up0)
                else:
                    stream(G_UP[0] + 2, FT - 2, up0[:, 2:, :])
                stream(G_DN[half], FT // 2, T["w_down"].rearrange("p (g n) -> p g n", n=ITEM))
            sp.wait_ge(s_act, 2 * FT + 1)
            sp.dma_start(ctxT, T["ctxT"]).then_inc(s_cl, 16)
            if STOP > 1:
                in2 = T["w_in2"].rearrange("p (g n) -> p g n", n=ITEM)
                for g in range(9):
                    sp.wait_ge(s_wlo, 2 * (G_IN2 + g) - 2)
                    if g == 2:
                        sp.wait_ge(s_cx, 1)
                        sp.dma_start(rope2, T["rope2"]).then_inc(s_rp, 16)
                    sp.dma_start(slot[g % 2], in2[:, g, :]).then_inc(s_wl[g % 2], 16)
                wo2 = T["w_out2"].rearrange("p (j b n) -> p j b n", j=4, b=2)
                for b in range(2):
                    load(b, wo2[:, 0, b, :], 8 * P, (tps, 2 * T_AT))
                with sp.Fori(1, 4) as j:
                    for b in range(2):
                        load(b, wo2[:, j, b, :], 8 * P, (tps, (j - 1) * 4 + 2 * (T_OUT2 + b + 1)))
            if STOP > 2:
                wga = T["w_ada_2"].rearrange("l (k a p) n -> l k p a n", a=2, p=P)[0]
                sp.wait_ge(tps, 2 * (T_OUT2 + 8))
                for i in range(4):
                    sp.dma_start(slot[i].rearrange("p (a n) -> p a n", a=2), wga[i][:, :, 5 * D:6 * D]).then_inc(wl[i], 16)
                sp.wait_ge(evv, T_OUT2 + 8)
                sp.dma_start(gt2B, T["b_ada_2"][:, 5 * D:6 * D].to_broadcast([P, D])).then_inc(s_late, 16)
                sp.dma_start(g_fin, T["g_final_2"].rearrange("(a d) -> a d", a=1).to_broadcast([P, D])).then_inc(s_late, 16)
                sp.dma_start(wr, T["w_router_2"][0].rearrange("(k p) e -> p k e", p=P)).then_inc(s_late, 16)
                for i in range(2 * NT):
                    sp.wait_ge(eva, T_XR + i + 1)
                    dst, n, t = (acc_d, D, i) if i < NT else (h_d, ROW, i - NT)
                    sp.dma_start(dst[t * P:(t + 1) * P, :], tok[i % 2][:, 0:n]).then_inc(s_tkst[i % 2], 16)
                wx = [T[n].rearrange("l e (j a p) n -> (l e) j p a n", a=2, p=P) for n in ("w_gate_2", "w_up_2", "w_down_2")]
                sp.wait_ge(tps, 2 * (T_HR + 8))
                sp.wait_ge(s_g2, 1)
                def expert_weights(n, e, used=None):
                    for j in range(4):
                        if used is not None:
                            sp.wait_ge(s_elo, used + (2 * j + 2))
                        src = wx[n][e, j] if isinstance(e, int) else wx[n][bass.ds(e, 1), j].rearrange("o p a n -> p (o a) n")
                        sp.dma_start(slot[4 * n + j].rearrange("p (a n) -> p a n", a=2), src).then_inc(wl[4 * n + j], 16)
                for n in range(3):
                    expert_weights(n, 0)
                expert_weights(0, 1, 0)
                with sp.Fori(0, NE - 2) as e:
                    expert_weights(1, e + 1, expert_item(e, 0))
                    expert_weights(0, e + 2, expert_item(e, KT))
                    expert_weights(2, e + 1, expert_item(e, 2 * KT))
                for n in (1, 2):
                    expert_weights(n, NE - 1, expert_item(NE - 2, (n - 1) * 2 * KT))
                for b in range(2):
                    sp.wait_ge(s_sc[b], 16 * NE // 2)
                for i in range(NT):
                    sp.dma_start(fin[i], acc_d[i * P:(i + 1) * P, :]).then_inc(s_fl[i], 16)
                for i in range(NT):
                    sp.wait_ge(s_fo, i + 1)
                    sp.dma_start(T["out"][0, i * P:(i + 1) * P, :], fin[i]).then_inc(s_out, 16)
                sp.wait_ge(s_out, 16 * NT)
            if STOP <= 2:
                sp.wait_ge(s_x, 24)
                if STOP == 2:
                    sp.wait_ge(evv, T_OUT2 + 8)
                    sp.wait_ge(s_x3, 8)
                sp.dma_start(T["out"].rearrange("p (k s) -> p k s", k=KT), xT).then_inc(s_out, 16)
                sp.wait_ge(s_out, 16)

        @block.tensor
        def _(pe):
            def keep_clock(n):
                for _ in range(n):
                    pe.matmul(ps[:, 7, :], con("mean"), const[:, 0:512], start=True, stop=True)

            def mean(i):
                pe.wait_ge(s_ssq, i + 1)
                for t in range(NORM_N[i] // P):
                    m = pe.matmul(ps[:, NORM_PS[i], t:t + 1], NORM_AT[i][1][:, t * P:(t + 1) * P], con("mean")[:, 0:1], start=True, stop=True)
                m.then_inc(s_stat, 1)

            def spread(i):
                pe.wait_ge(s_dg, i + 1)
                for t in range(NORM_N[i] // P):
                    m = pe.matmul(ps[:, NORM_PS[i] + t // 4, (t % 4) * P:(t % 4 + 1) * P], con("mean"), NORM_AT[i][0][0][:, t * P:(t + 1) * P], start=True, stop=True)
                m.then_inc(s_bc, 1)

            def stat(i):
                mean(i)
                spread(i)

            def tile_free(t, h):
                if not isinstance(t, int) or t >= 2:
                    pe.wait_ge(evv if h == 0 else eva, t - 1)

            def tile(t, b, lhs, rhs, nk, m=P, n=512):
                for h in range(2):
                    tile_free(t, h)
                    for k in range(nk):
                        i = pe.matmul(ps[0:m, 2 * b + h, 0:n], lhs(k, h), rhs(k, h), start=(k == 0), stop=(k == nk - 1))
                    i.then_inc(tps, 1)

            def turn(t, src):
                for h in range(2):
                    tile_free(t, h)
                    for j in range(4):
                        i = pe.transpose(ps[:, 2 * (t % 2) + h, j * P:(j + 1) * P], src(h, j), ident)
                    i.then_inc(tps, 1)

            def loaded(ph, s, j):
                pe.wait_ge(wl[s], j * 16 + 16 * (loads_before(ph, s) + 1))

            def wtile(s, a):
                return lambda k, h: slot[s][:, (a * KT + k) * P:(a * KT + k + 1) * P]

            def tokens(src):
                return lambda k, h: src[:, k, h * HALF:(h + 1) * HALF]

            def units(g, now, before=None, probs=probs, probsT=probsT):
                def after(s, v, u, least):
                    if not isinstance(g, int) or g + u >= least:
                        pe.wait_ge(s, g + (u + v))

                def group(w):
                    return now if w >= 0 else before
                for u in range(8 if now else 2):
                    if now:
                        after(s_exp, -1, u, 2)
                        now[0](u).then_inc(s_S, 1)
                    w = u - 1
                    if (now or u == 0) and group(w):
                        pe.wait_ge(s_exp, g + (w + 1))
                        after(s_pt, 0, w, 1)
                        for j in range(group(w)[1](w % 8) // P):
                            i = pe.transpose(ps[:, 4 + j // 4, (j % 4) * P:(j % 4 + 1) * P], probs[w % 2][:, j * P:(j + 1) * P], ident)
                        i.then_inc(s_T, 1)
                    w = u - 2
                    if group(w):
                        pe.wait_ge(s_pt, g + (w + 1))
                        after(s_o, -1, w, 2)
                        nb = group(w)[1](w % 8) // P
                        for j in range(nb):
                            i = pe.matmul(ps[:, 6 + w % 2, 0:HD], probsT[w % 2][:, j * P:(j + 1) * P], group(w)[2](w % 8, j),
                                          start=(j == 0), stop=(j == nb - 1))
                        i.then_inc(s_pv, 1)

            pe.wait_ge(par, 16 * NPAR)
            pe.matmul(ps[0:8, 4, 0:384], relb, onehot, start=True, stop=True).then_inc(s_bl, 1)

            def modulation(k, w, load, b, n):
                pe.wait_ge(*load)
                for c in range(n):
                    m = pe.matmul(ps[0:2, b + c, :], scT[:, k, :], w[:, c * 512:(c + 1) * 512], start=(k == 0), stop=(k == KT - 1))
                return m

            def columns(row, n, rows):
                pe.wait_ge(s_row, rows)
                for t in range(n):
                    m = pe.transpose(ps[:, 4, 2 * t:2 * t + 2], row[:, t * P:(t + 1) * P], ident[0:2, 0:2])
                m.then_inc(s_mod, 1)

            stat(0)
            pe.wait_ge(s_silu, 1)
            for k in range(KT):
                modulation(k, adaA[k % 6], (s_al[k % 6], 16 * (k // 6 + 1)), 0, 4).then_inc(s_au if k < KT - 1 else s_ad, 1)
            pe.wait_ge(s_row, 1)
            pe.wait_ge(s_h, 8)
            pe.wait_ge(extra, 16)
            pe.wait_ge(s_bias, 16)
            for c in range(4):
                m = pe.matmul(ps[:, 4 + c, :], con("flip"), mflip.rearrange("p a b -> p (a b)")[:, c * 512:(c + 1) * 512], start=True, stop=True)
            m.then_inc(s_flip, 1)
            for t in range(4):
                tile(T_V + t, t % 2, lambda k, h: hT[:, k, (2 * t + h) * P:(2 * t + h + 1) * P], lambda k, h: wv[:, k, :], KT, P, 384)
            pe.wait_ge(evv, T_IN)
            columns(rowA, 2 * KT, 1)
            for t in range(13):
                i, a = t // 2, t % 2
                if a == 0:
                    loaded("w_in", i % 4, i // 4)
                if t < 12:
                    tile(T_IN + t, (T_IN + t) % 2, wtile(i % 4, a), tokens(hT), KT)
                else:
                    tile(T_IN + t, (T_IN + t) % 2, lambda k, h: slot[i % 4][:, k * QK:(k + 1) * QK], tokens(hT), KT, QK)

            def swapped(i, src):
                if i:
                    pe.wait_ge(s_rot, i)
                for h in range(2):
                    m = pe.matmul(ps[0:QK, 4 + h, :], con("swap16")[64:96], src[64:96, h * HALF:(h + 1) * HALF], start=True, stop=True)
                m.then_inc(s_sw, 1)

            def swap_query(h):
                pe.wait_ge(evv, T_UQ + h + 1)
                pe.wait_ge(eva, T_UQ + h + 1)
                swapped(1 + h, QH[:, 4 + h, :])

            pe.wait_ge(eva, T_UQ)
            pe.wait_ge(evv, T_UQ)
            pe.wait_ge(s_bls, 1)
            swapped(0, krope)
            keep_clock(5)
            stat(1)
            pe.wait_ge(s_rs, 2)
            keep_clock(3)
            stat(2)
            pe.wait_ge(s_rs, 3)
            keep_clock(2)
            pe.wait_ge(s_lat, 32)
            pe.wait_ge(s_h, 8 + 2 + 1)
            for h in range(4):
                tile(T_UQ + h, (T_UQ + h) % 2, lambda k, hf: wuq[:, k, h * QK:(h + 1) * QK], tokens(cq), 2, QK)
                if h:
                    swap_query(h - 1)
            for h in range(4):
                tile(T_UKV + h, (T_UKV + h) % 2, lambda k, hf: wukv[:, h * P:h * P + HD],
                     lambda k, hf: ckv[:, hf * HALF:(hf + 1) * HALF], 1, HD)
                if h == 0:
                    swap_query(3)
            wuv = wukv.rearrange("p (h c) -> p h c", c=P)[:, :, HD:P]
            for t in range(4):
                tile(T_LV + t, (T_LV + t) % 2, lambda k, h: ckv[:, (2 * t + h) * P:(2 * t + h + 1) * P], lambda k, h: wuv, 1, P, 256)

            keep_clock(6)
            pe.wait_ge(evv, T_MT)
            pe.wait_ge(eva, T_MT)
            pe.wait_ge(s_rot, 5)
            pe.wait_ge(s_krc, 1)
            pe.wait_ge(s_frow, 16)

            def sink(u, layer, b, at):
                return pe.matmul(ps[:, b, at:at + 1], con("mean")[0:1, :], sinkB[0:1, layer, u // 2 + 4 * (u % 2):u // 2 + 4 * (u % 2) + 1], start=True, stop=True)

            def swa(n, par):
                nk = P if isinstance(n, int) and n == 0 else 2 * P

                def scores(u):
                    r = HD * (u % 2)
                    if u == 0:
                        pe.wait_ge(s_stage, n + 1)
                    pe.matmul(ps[:, 2 * (u % 2), 0:nk], qs[par][r:r + HD, u // 2, :], ks[par][r:r + HD, 0:nk], start=True, stop=False)
                    pe.matmul(ps[:, 2 * (u % 2), 0:nk], ident, swab[:, u // 2 + 4 * (u % 2), 256 - nk:256], start=False, stop=True)
                    return sink(u, 0, 2 * (u % 2), nk)

                def values(u, j):
                    c = HD * (u % 2)
                    if nk == P:
                        return swav[:, 0, c:c + HD]
                    return swav[:, bass.ds(n + (j - 1), 1), c:c + HD].rearrange("p a c -> p (a c)")
                return scores, lambda u: nk, values

            def dense(h, par):
                def scores(u):
                    if u == 0:
                        pe.wait_ge(s_stage, h + (NT + 1))
                    n = (u + 1) * P
                    for c in range((n + 511) // 512):
                        m = min(512, n - c * 512)
                        pe.matmul(ps[:, 2 * (u % 2) + c, 0:m], qh[par][0:QK, u * P:(u + 1) * P],
                                  KH[0:QK, bass.ds(h, 1), c * 512:c * 512 + m].rearrange("p a c -> p (a c)"), start=True, stop=(c * 512 + m < n))
                    return pe.matmul(ps[:, 2 * (u % 2) + u // 4, (u % 4) * P:(u % 4 + 1) * P], identb, causalb, start=False, stop=True)

                def values(u, j):
                    return VH[:, j, bass.ds(h * HD, HD)]
                return scores, lambda u: (u + 1) * P, values

            units(U_SWA, swa(0, 0))
            units(8, swa(1, 1), swa(0, 0))
            with pe.Fori(1, NT // 2) as m:
                for b in range(2):
                    units(m * 16 + 8 * b, swa(2 * m + b, b), swa(2 * m + (b - 1), 1 - b))
            units(U_DENSE, dense(0, 0), swa(NT - 1, 1))
            with pe.Fori(0, CH // 2 - 1) as m:
                for b in range(2):
                    units(m * 16 + (U_DENSE + 8 * (b + 1)), dense(2 * m + (b + 1), 1 - b), dense(2 * m + b, b))
            units(U_ATT2 - 8, dense(CH - 1, 1), dense(CH - 2, 0))
            units(U_ATT2, None, dense(CH - 1, 1))

            pe.wait_ge(s_gn, 8)
            pe.wait_ge(s_gna, 8)
            for k in range(KT):
                turn(T_MT + k, lambda h, j: mixed[:, 4 * h + j, k * P:(k + 1) * P])
            pe.wait_ge(evv, T_OUT)
            pe.wait_ge(eva, T_OUT)
            def passes(out, q, t, hi, lo, start, stop):
                w = slice(t * P, (t + 1) * P)
                pe.matmul(out, w_hi[:, q, w], hi, start=start, stop=False)
                pe.matmul(out, w_hi[:, q, w], lo, start=False, stop=False)
                return pe.matmul(out, w_lo[:, q, w], hi, start=False, stop=stop)

            with pe.Fori(0, 2) as m:
                for c in range(2):
                    for q in range(2):
                        g = 2 * m + c
                        pe.wait_ge(s_wlo, 2 * g + (2 * G_OUT + q + 1))
                        for h in range(2):
                            tile_free(4 * m + (T_OUT + 2 * c + q), h)
                            for k in range(KT):
                                i = passes(ps[:, 2 * ((T_OUT + q) % 2) + h, :], q, k, m_hi[:, k, h * HALF:(h + 1) * HALF], m_lo[:, k, h * HALF:(h + 1) * HALF],
                                           k == 0, k == KT - 1)
                            i.then_inc(tps, 1)
            def parts(g, ks):
                for k in ks:
                    modulation(k, adaB[k], (s_bl2[k], 16 * (g + 1)), 3 * g, 3).then_inc(s_au if k < KT - 1 else s_ad, 1)
            pe.wait_ge(evv, T_DN)
            pe.wait_ge(eva, T_DN)
            mean(3)
            parts(0, range(2))
            spread(3)
            parts(0, range(2, KT))
            mean(4)
            parts(1, range(2))
            spread(4)
            parts(1, range(2, KT))
            pe.wait_ge(s_row, 2)

            def up(half, g, b):
                for q in range(2):
                    pe.wait_ge(s_wlo, 2 * g + (2 * G_UP[half] + q + 1))
                    if q == 0:
                        pe.wait_ge(s_uv, g + (half * FT + 1))
                    for k in range(KT):
                        i = passes(ps[:, 2 * b + q, :], q, k, h_hi[:, k, :], h_lo[:, k, :], k == 0, k == KT - 1)
                    i.then_inc(s_wu, 1)

            def down(half, g, q, first=False, last=False):
                pe.wait_ge(s_wlo, 2 * g + (2 * G_DN[half] + q + 1))
                pe.wait_ge(s_alo, 2 * g + (half * FT + q + 1))
                for t in ((4, 5, 6, 7, 0, 1, 2, 3) if first else range(KT)):
                    if first and t == 0:
                        pe.wait_ge(s_uv, half * FT + FT + 2)
                    i = passes(ps[:, t, :], q, t, a_hi[:, q, :], a_lo[:, q, :], first, last)
                    if last:
                        i.then_inc(tps, 1)
                if not last:
                    i.then_inc(s_wu, 1)

            for half in range(2):
                pe.wait_ge(s_h, 8 + 2 + 1 + 8 + 8 * half)
                pe.wait_ge(evv, T_DN + 4 * half)
                pe.wait_ge(eva, T_DN + 4 * half)
                up(half, 0, 0)
                if half:
                    mean(5)
                else:
                    columns(rowB, 3 * KT, 3)
                up(half, 1, 1)
                if half:
                    spread(5)
                with pe.Fori(1, FT // 2) as j:
                    for b in range(2):
                        up(half, 2 * j + b, b)
                down(half, 0, 0, first=True)
                down(half, 0, 1)
                with pe.Fori(1, FT // 2 - 1) as g:
                    for q in range(2):
                        down(half, g, q)
                down(half, FT // 2 - 1, 0)
                down(half, FT // 2 - 1, 1, last=True)
            if STOP <= 1:
                return
            pe.wait_ge(evv, T_V2[0])
            pe.wait_ge(eva, T_V2[0])
            mean(6)
            mean(7)
            spread(6)
            spread(7)
            pe.wait_ge(s_wl[0], 8 * G_IN2 + 16)
            pe.wait_ge(s_hb, KT)
            for k in range(KT):
                pe.matmul(ps[:, 4, 0:CTX], wtile(0, 0)(k, 0), hcT[:, k, :], start=(k == 0), stop=(k == KT - 1))
            for t in range(2):
                for k in range(KT):
                    i = pe.matmul(ps[:, 5, t * P:(t + 1) * P], hcT[:, k, t * P:(t + 1) * P], wtile(0, 1)(k, 0), start=(k == 0), stop=(k == KT - 1))
            i.then_inc(s_cx, 1)
            stat(8)
            pe.wait_ge(s_rs, 9)
            keep_clock(8)

            def swapped2(i, src):
                pe.wait_ge(s_rot, 5 + i)
                for h in range(2):
                    m = pe.matmul(ps[:, 4 + h, :], con("swap32"), src[:, h * HALF:(h + 1) * HALF], start=True, stop=True)
                m.then_inc(s_sw, 1)

            def input_tile(t, n):
                pe.wait_ge(s_wlo, 2 * G_IN2 + n + 1)
                for h in range(2):
                    tile_free(t, h)
                    if n == 0 and h == 1:
                        pe.wait_ge(s_hhi, 4 * KT)
                    hs = slice(h * HALF, (h + 1) * HALF)
                    for k in range(KT):
                        i = passes(ps[:, 2 * (t % 2) + h, :], n % 2, k, g_hi[:, k, hs], g_lo[:, k, hs], k == 0, k == KT - 1)
                    i.then_inc(tps, 1)

            pe.wait_ge(s_cxe, 2)
            pe.wait_ge(s_wlo, 2 * G_IN2 + 2)
            pe.wait_ge(s_hhi, 3 * KT)
            for t in range(4):
                g = T_V2[t]
                for h in range(2):
                    tile_free(g, h)
                    out, rows = ps[:, 2 * (g % 2) + h, 0:P], slice((2 * t + h) * P, (2 * t + h + 1) * P)
                    for k in range(KT):
                        w = slice(k * P, (k + 1) * P)
                        pe.matmul(out, g_hi[:, k, rows], w_hi[:, 1, w], start=(k == 0), stop=False)
                        pe.matmul(out, g_hi[:, k, rows], w_lo[:, 1, w], start=False, stop=False)
                        i = pe.matmul(out, g_lo[:, k, rows], w_hi[:, 1, w], start=False, stop=(k == KT - 1))
                    i.then_inc(tps, 1)
                if t == 1:
                    input_tile(T_K2, 0)
                if t == 2:
                    pe.wait_ge(evv, T_K2 + 1)
                    pe.wait_ge(eva, T_K2 + 1)
                    swapped2(0, k2)
            for t in range(1, 17):
                input_tile(T_IN2 + t, t + 1)
                if 2 <= t <= 5:
                    pe.wait_ge(evv, T_IN2 + t)
                    pe.wait_ge(eva, T_IN2 + t)
                    swapped2(t - 1, q2[:, t - 2, :])
            keep_clock(6)
            pe.wait_ge(s_rot, 10)
            pe.wait_ge(s_cv, 4)

            def att(n, lo, hi, it, par):
                nl = (hi - lo + 1) * P
                at = 512 - nl

                def scores(u):
                    r, b = HD * (u % 2), 2 * (u % 2)
                    if u == 0:
                        pe.wait_ge(s_stage, it + (NT + CH + 1))
                    pe.matmul(ps[:, b, at:512], qs[par][r:r + HD, u // 2, :], ks[par][r:r + HD, 0:nl], start=True, stop=False)
                    if lo < 0:
                        pe.matmul(ps[:, b, at:at + P], identb, leftb, start=False, stop=(hi < 1))
                    if hi > 0:
                        pe.matmul(ps[:, b, 512 - P:512], identb, causalb, start=False, stop=True)
                    pe.matmul(ps[:, b + 1, 0:CTX], qs[par][r:r + HD, u // 2, :], kc[r:r + HD, :], start=True, stop=True)
                    return sink(u, 1, b + 1, CTX)

                def values(u, j):
                    c = HD * (u % 2)
                    if j >= nl // P:
                        return vc[:, j - nl // P, c:c + HD]
                    return v2[:, n + (lo + j), c:c + HD]
                return scores, lambda u: nl + CTX, values

            def units2(g, now, before=None):
                units(g, now, before, late_probs, late_probsT)
            units2(U_ATT2, att(0, 0, 1, 0, 0))
            units2(U_ATT2 + 8, att(1, -1, 1, 1, 1), att(0, 0, 1, 0, 0))
            with pe.Fori(1, NT // 2 - 1) as m:
                for b in range(2):
                    n = 2 * m + b
                    units2(m * 16 + (U_ATT2 + 8 * b), att(n, -1, 1, n, b), att(n - 1, -1, 1, n - 1, 1 - b))
            units2(U_END - 16, att(NT - 2, -1, 1, NT - 2, 0), att(NT - 3, -1, 1, NT - 3, 1))
            units2(U_END - 8, att(NT - 1, -1, 0, NT - 1, 1), att(NT - 2, -1, 1, NT - 2, 0))
            units2(U_END, None, att(NT - 1, -1, 0, NT - 1, 1))
            pe.wait_ge(s_o, U_END)
            for k in range(4):
                turn(T_AT + k, lambda h, j: att2[:, 4 * h + j, k * P:(k + 1) * P])
            pe.wait_ge(evv, T_OUT2)
            pe.wait_ge(eva, T_OUT2)
            with pe.Fori(0, 4) as j:
                for b in range(2):
                    loaded("w_out2", b, j)
                    tile(2 * j + (T_OUT2 + b), (T_OUT2 + b) % 2, wtile(b, 0),
                         lambda k, h: (attT[:, k, :] if k < 4 else convm[:, k - 4, :])[:, h * HALF:(h + 1) * HALF], KT)
            if STOP <= 2:
                return
            stat(9)
            pe.wait_ge(s_late, 48)
            for k in range(KT):
                pe.wait_ge(s_hb, 3 * KT + k + 1)
                for c in range(2):
                    m = pe.matmul(ps[0:NE, c, :], wr[:, k, :], hT[:, k, c * HALF:(c + 1) * HALF], start=(k == 0), stop=(k == KT - 1))
            m.then_inc(s_lgT, 1)
            pe.wait_ge(s_lgc, 1)
            for i in range(NT):
                m = pe.transpose(ps[:, 4, i * NE:(i + 1) * NE], lgT[:, i * P:(i + 1) * P], ident[0:NE, 0:NE])
            m.then_inc(s_lg, 1)
            pe.wait_ge(s_aff, 1)
            for i in range(NT):
                m = pe.transpose(ps[0:NE, 5 + i // 4, (i % 4) * P:(i % 4 + 1) * P], aff[:, i, :], ident)
            m.then_inc(s_at, 1)
            for i in range(2 * NT):
                src, t, g = (xT, i, T_XR + i) if i < NT else (hT, i - NT, T_XR + i)
                pe.wait_ge(eva, g - 1)
                for k in range(KT):
                    m = pe.transpose(ps[:, 2 * (g % 2) + k // 4, (k % 4) * P:(k % 4 + 1) * P], src[:, k, t * P:(t + 1) * P], ident)
                    if k % 4 == 3:
                        m.then_inc(tps, 1)
            pe.wait_ge(s_sb, 1)
            pe.wait_ge(eva, T_HR + 8)
            for k in range(KT):
                if k % 2 == 0:
                    loaded("gate2", k // 2, 0)
                for c in range(2):
                    m = pe.matmul(ps[:, 2 + c, :], silu_b[:, k, :], slot[k // 2][:, (k % 2) * D + c * 512:(k % 2) * D + (c + 1) * 512],
                                  start=(k == 0), stop=(k == KT - 1))
            m.then_inc(s_g2, 1)
            pe.wait_ge(s_pos, 1)
            for e in range(NE):
                if e >= 2:
                    pe.wait_ge(s_cnt, e - 1)
                for c in range(2):
                    b = 4 + 2 * (e % 2) + c
                    m = pe.matmul(ps[:, b, :], identb[0:NE, e:e + 1].to_broadcast([NE, P]), posbf[:, c * 512:(c + 1) * 512], start=True, stop=True)
                m.then_inc(s_pb, 1)
            pe.wait_ge(s_cnt, NE)
            pe.wait_ge(s_g2e, 1)
            def item(n, k, hi, lo, bank):
                r = k % RING
                pe.wait_ge(s_elo, n + 1)
                for c in range(2):
                    w, out = slice(c * 512, (c + 1) * 512), ps[:, bank + c, :]
                    pe.matmul(out, hi[:, k, :], e_hi[:, r, w], start=(k == 0), stop=False)
                    pe.matmul(out, lo[:, k, :], e_hi[:, r, w], start=False, stop=False)
                    m = pe.matmul(out, hi[:, k, :], e_lo[:, r, w], start=False, stop=(k == KT - 1))
                m.then_inc(s_eu, 1)

            def turn_rows(e, b):
                pe.wait_ge(s_gat[b], 8 * e + (16 - 8 * b))
                for k in range(KT):
                    m = pe.transpose(ps[:, 4 + k // 4, (k % 4) * P:(k % 4 + 1) * P], xs[b][:, k * P:(k + 1) * P], ident)
                m.then_inc(s_xt, 1)

            def gate(n, b, ks):
                for k in ks:
                    item(n + k, k, x_hi[:, b], x_lo[:, b], 0)

            def expert(e, b, last=False):
                if not last:
                    turn_rows(e + 1, 1 - b)
                for k in range(KT):
                    item(expert_item(e, k), k, x_hi[:, b], x_lo[:, b], 2)
                if not last:
                    pe.wait_ge(s_xe, e + 2)
                    pe.wait_ge(s_sg, e + 1)
                    gate(expert_item(e, KT), 1 - b, range(4))
                pe.wait_ge(s_ga, e + 1)
                for k in range(KT):
                    m = pe.transpose(ps[:, 4 + k // 4, (k % 4) * P:(k % 4 + 1) * P], actx[:, k * P:(k + 1) * P], ident)
                m.then_inc(s_at2, 1)
                if not last:
                    gate(expert_item(e, KT), 1 - b, range(4, KT))
                pe.wait_ge(s_ae, e + 1)
                pe.wait_ge(s_ys, e + 1)
                for k in range(KT):
                    item(expert_item(e, (1 if last else 2) * KT + k), k, t_hi, t_lo, 6)

            turn_rows(0, 0)
            pe.wait_ge(s_xe, 1)
            gate(0, 0, range(KT))
            expert(0, 0)
            with pe.Fori(0, NE // 2 - 1) as q:
                for b in range(2):
                    expert(2 * q + (1 + b), 1 - b)
            expert(NE - 1, 1, last=True)

        @block.scalar
        def _(act_e):
            ac = Chain(act_e, ach)
            sqn = [0, 0]

            def squares(i, src, ready):
                sqs, sm, _ = NORM_AT[i]
                n = NORM_N[i]
                for k in range(NORM_K[i]):
                    for w in (ready(k) or ()):
                        act_e.wait_ge(*w)
                    if k >= 3:
                        act_e.wait_ge(s_add, sqn[1] + k - 2)
                    act_e.activation(sm[:, 0:n] if k == 0 else sqs[k % 2][:, 0:n], src(k), ACT.Square).then_inc(s_sq, 1)
                sqn[1] += NORM_K[i] - 1

            def root(i):
                act_e.wait_ge(s_stat, i + 1)
                nt = NORM_N[i] // P
                act_e.activation(rms[i % 2][:, 0:nt], ps[:, NORM_PS[i], 0:nt], ACT.Sqrt, bias=epst, scale=KT / NORM_K[i]).then_inc(s_rt, 1)

            def spread(i):
                act_e.wait_ge(s_bc, i + 1)
                act_e.activation(NORM_AT[i][2][:, 0:NORM_N[i]], banks(NORM_PS[i], NORM_N[i]), ACT.Copy).then_inc(s_rs, 1)

            def norm(i):
                root(i)
                spread(i)

            act_e.wait_ge(par, 16 * NPAR)
            act_e.wait_ge(s_bf, 1)
            act_e.activation(scT[:, :, 0:1], col("cvec", 0, 8), ACT.Silu)
            act_e.activation(scT[:, :, 1:2], col("cctx", 0, 8), ACT.Silu).then_inc(s_silu, 1)
            squares(0, lambda k: xT[:, k, :], lambda k: [(xl[k // 2], 16)])
            norm(0)
            act_e.wait_ge(s_ad, 1)
            act_e.activation(rowA, banks(0, 2 * D)[0:2], ACT.Copy).then_inc(s_row, 1)

            def half1(t, out, scale=None):
                act_e.wait_ge(tps, 2 * t + 2)
                return act_e.activation(out[0], out[1], ACT.Copy, scale=scale) if scale else act_e.activation(out[0], out[1], ACT.Copy)

            def b1(t):
                return 2 * (t % 2) + 1
            hi = slice(HALF, S)
            for t in range(4):
                g = T_V + t
                half1(g, (swav[:, 2 * t + 1, :], ps[:, b1(g), 0:P]))
                act_e.activation(VH[:, 2 * t + 1, 0:256], ps[:, b1(g), P:384], ACT.Copy).then_inc(eva, 1)
            for t in range(13):
                g = T_IN + t
                src = ps[:, b1(g), :]
                if t < 4:
                    half1(g, (swaq[:, t, hi], src), HD ** -0.5).then_inc(eva, 1)
                elif t == 4:
                    half1(g, (swak[:, hi], src)).then_inc(eva, 1)
                elif t < 9:
                    dst, h = (QH, 2 * (t - 5)) if t < 7 else (KH, 2 * (t - 7))
                    half1(g, (dst[0:HD, h, hi], src[0:HD]), HD ** -0.5 if t < 7 else None)
                    act_e.activation(dst[0:HD, h + 1, hi], src[HD:P], ACT.Copy, scale=HD ** -0.5 if t < 7 else 1.0).then_inc(eva, 1)
                elif t < 11:
                    half1(g, (cq[:, t - 9, hi], src)).then_inc(eva, 1)
                elif t == 11:
                    half1(g, (ckv[:, hi], src)).then_inc(eva, 1)
                else:
                    half1(g, (krope[64:96, hi], src[64:96]))
                    act_e.activation(flog[0:4, hi], src[0:4], ACT.Identity, bias=fbias[0:4]).then_inc(eva, 1)
            act_e.wait_ge(s_f, 1)
            ac.link(act_e.activation(ftmp[0:4], ftmp[0:4], ACT.Exp, scale=-1.0))
            act_e.activation(ftmp[0:4], ftmp[0:4], ACT.Ln, bias=1.0).then_inc(s_fe, 1)
            squares(1, lambda k: cq[:, k, :], lambda k: [(evv, T_UQ), (eva, T_UQ)])
            norm(1)
            squares(2, lambda k: ckv, lambda k: [(s_h, 8 + 2)])
            norm(2)
            for h in range(4):
                g = T_UQ + h
                half1(g, (QH[0:QK, 4 + h, hi], ps[0:QK, b1(g), :]), QK ** -0.5).then_inc(eva, 1)
            for h in range(4):
                g = T_UKV + h
                half1(g, (KH[0:HD, 4 + h, hi], ps[0:HD, b1(g), :])).then_inc(eva, 1)
            for t in range(4):
                g = T_LV + t
                half1(g, (VH[:, 2 * t + 1, 256:512], ps[:, b1(g), 0:256])).then_inc(eva, 1)

            def exps(n, g, cols_of, src, probs=probs):
                for u in range(n):
                    act_e.wait_ge(s_max, g + (u + 1))
                    if not isinstance(g, int) or g + u >= 2:
                        act_e.wait_ge(s_T, g + (u - 1))
                    w, c = cols_of(u), u % 4
                    act_e.activation(probs[u % 2][:, 0:w], src(u), ACT.Exp, bias=nmax[:, c:c + 1], accum_out=den[:, c:c + 1]).then_inc(s_exp, 1)

            def swa(n, g):
                w = P if isinstance(n, int) else 2 * P
                exps(8, g, lambda u: w + 1, lambda u: ps[:, 2 * (u % 2), 0:w + 1])
            swa(0, 0)
            with act_e.Fori(1, NT) as n:
                swa(n, n * 8)
            with act_e.Fori(0, CH) as h:
                exps(8, h * 8 + U_DENSE, lambda u: (u + 1) * P, lambda u: banks(2 * (u % 2), (u + 1) * P))
                act_e.wait_ge(s_o, U_DENSE)
                act_e.activation(gsq, mixed[:, bass.ds(h, 1), 0:512].rearrange("p a c -> p (a c)"), ACT.Square,
                                 accum_out=gss[:, bass.ds(h, 1), 0:1].rearrange("p a c -> p (a c)"))
            def weight_high(gg, c, q, free):
                act_e.wait_ge(s_wl[c], 8 * gg + (16 - 8 * c))
                act_e.wait_ge(*free)
                act_e.activation(w_hi[:, q, :], slot[c][:, q * D:(q + 1) * D], ACT.Copy).then_inc(s_whi, 1)

            def gated_high(half, k, q, free):
                act_e.wait_ge(s_act, k + (half * FT + 2))
                act_e.wait_ge(*free)
                act_e.activation(a_hi[:, q, :], act[:, k, :], ACT.Copy).then_inc(s_ahi, 1)

            for q in range(2):
                weight_high(G_OUT, 0, q, (tps, 2 * T_UQ))
            act_e.wait_ge(s_o, U_ATT2)
            groups = ((0, 512), (512, 256), (768, 256))
            for i in range(NT):
                for j, (c, w) in list(enumerate(groups))[1:]:
                    ac.mark(act_e.activation(sq[0][:, c:c + w], mixed[:, i, c:c + w], ACT.Square, accum_out=gss[:, i, j:j + 1]))
                ac.need()
            for j, (c, w) in enumerate(groups):
                act_e.activation(grs[:, :, j:j + 1], gss[:, :, j:j + 1], ACT.Sqrt, bias=epst, scale=1.0 / w).then_inc(s_gq, 1)
            act_e.wait_ge(s_gr, 1)
            for i in range(NT):
                act_e.activation(mixed[:, i, 0:512], mixed[:, i, 0:512], ACT.Copy, scale=grs[:, i, 0:1]).then_inc(s_gna, 1)
            for k in range(KT):
                g = T_MT + k
                act_e.wait_ge(tps, 2 * g + 2)
                act_e.activation(m_hi[:, k, :], banks(2 * (g % 2), S), ACT.Copy, scale=col("group", k)).then_inc(eva, 1)
            act_e.wait_ge(tps, 2 * T_OUT)
            with act_e.Fori(0, 2) as m:
                for c in range(2):
                    for q in range(2):
                        g = 2 * m + c
                        act_e.wait_ge(tps, 4 * g + (2 * (T_OUT + q) + 2))
                        weight_high(g + (G_OUT + 1), 1 - c, q, parts_used("out", 0, g, q))
                        act_e.activation(zT[:, 2 * g + q, hi], ps[:, b1(T_OUT + q), :], ACT.Copy).then_inc(eva, 1)
                        act_e.wait_ge(evv, 2 * g + (T_OUT + q + 1))
                        act_e.wait_ge(eva, 2 * g + (T_OUT + q + 1))
                        act_e.wait_ge(s_zadd, 2 * g + (q + 1))
                        act_e.activation(sq[q], zT[:, bass.ds(2 * g + q, 1), :].rearrange("p a b -> p (a b)"), ACT.Square).then_inc(s_zsq, 1)
            norm(3)
            squares(4, lambda k: xT[:, k, :], lambda k: [(s_x, k + 1)])
            norm(4)
            for g in range(2):
                act_e.wait_ge(s_ad, 2 + g)
                act_e.activation(rowB[:, g * ADA:(g + 1) * ADA], banks(3 * g, ADA)[0:2], ACT.Copy).then_inc(s_row, 1)
            for half in range(2):
                p0 = half * FT
                sl = G_UP[half] % 2

                def conv(j, bs=(0, 1)):
                    for b in bs:
                        g = 2 * j + b
                        weight_high(g + (G_UP[half] + 1), (sl + b + 1) % 2, 0, parts_used("up", half, g, 0))
                        act_e.wait_ge(s_wu, 2 * g + (W_UP[half] + 2))
                        act_e.wait_ge(s_act, g + (p0 + 1))
                        for q in range(2):
                            t = 2 * j + (q * FT + b)
                            act_e.activation(convy[b][q], ps[:, 2 * b + q, :], ACT.Identity, bias=cols[:, bass.ds(t + COLS["conv_b"][0], 1)],
                                             scale=cols[:, bass.ds(t + (COLS["conv_w"][0] + 2 * 2 * FT), 1)]).then_inc(s_ua, 1)
                        weight_high(g + (G_UP[half] + 1), (sl + b + 1) % 2, 1, parts_used("up", half, g, 1))
                        act_e.wait_ge(s_uv, g + (p0 + 3))
                        act_e.activation(gelu[b], convy[b][0], ACT.Gelu_apprx_tanh).then_inc(s_gl, 1)
                conv(0, (0,))
                if half:
                    root(5)
                conv(0, (1,))
                if half:
                    spread(5)
                with act_e.Fori(1, FT // 2) as j:
                    conv(j)
                for q in range(2):
                    gated_high(half, q, q, parts_used("down", 0, FT // 2 - 1, q) if half else (s_S, U_ATT2))
                sl = G_DN[half] % 2
                with act_e.Fori(0, (FT // 2 - 1) // 2) as m:
                    for c in range(2):
                        for q in range(2):
                            g = 2 * m + c
                            weight_high(g + (G_DN[half] + 1), (sl + c + 1) % 2, q, parts_used("down", half, g, q))
                            gated_high(half, 2 * g + (2 + q), q, parts_used("down", half, g, q))
                nxt = (G_UP[1], G_IN2)[half]
                for q in range(2):
                    weight_high(nxt, nxt % 2, q, parts_used("down", half, FT // 2 - 1, q))
                if half:
                    squares(6, lambda k: ctxT[:, k, :], lambda k: [(s_cl, 16)])
                act_e.wait_ge(s_x, 8 + 8 * half)
                for t in range(1, KT, 2):
                    act_e.wait_ge(tps, 2 * (T_DN + 4 * half) + t + 1)
                    act_e.activation(yT[:, t, :], ps[:, t, :], ACT.Copy).then_inc(eva, 1)
                d = T_DN + 4 * half + 4
                squares(5 + 2 * half, lambda k: yT[:, k, :], lambda k: [(evv, d), (eva, d)])
            root(6)
            root(7)
            spread(6)
            spread(7)
            if STOP <= 1:
                return
            def shift(i, base, dst, row, b):
                for k in range(KT):
                    act_e.wait_ge(s_h, base + k + 1)
                    act_e.activation(dst[:, k, :], dst[:, k, :], ACT.Identity, bias=mod[:, row + k, b:b + 1]).then_inc(s_hb, 1)
            shift(6, 27, hcT, 0, 1)
            squares(8, lambda k: xT[:, k, :], lambda k: [(s_x, 17 + k)])
            act_e.wait_ge(s_cx, 1)
            act_e.activation(vc[:, :, :], ps[:, 5, 0:2 * P].rearrange("p (a b) -> p a b", a=2), ACT.Copy).then_inc(s_cxe, 1)
            norm(8)
            for i in range(2 * KT):
                hf, k = i // KT, i % KT
                act_e.wait_ge(s_h, 35 + i + 1)
                act_e.activation(g_hi[:, k, hf * HALF:(hf + 1) * HALF], sq[i % 2][:, 0:HALF], ACT.Identity, bias=mod[:, k, 0:1]).then_inc(s_hb, 1)
            def input_high(n):
                weight_high(G_IN2 + n // 2, (n // 2) % 2, n % 2, in2_used(n - 2))
            for t in range(4):
                g = T_V2[t]
                if t == 2:
                    input_high(2)
                    half1(T_K2, (k2[:, hi], ps[:, b1(T_K2), :])).then_inc(eva, 1)
                if t == 3:
                    input_high(3)
                half1(g, (v2[:, 2 * t + 1, :], ps[:, b1(g), 0:P])).then_inc(eva, 1)
            for t in range(1, 17):
                g = T_IN2 + t
                src = ps[:, b1(g), :]
                if t + 3 < 18:
                    input_high(t + 3)
                if t < 5:
                    half1(g, (q2[:, t - 1, hi], src), HD ** -0.5).then_inc(eva, 1)
                else:
                    act_e.wait_ge(evv, g + 1)
                    act_e.activation(apad[:, t - 5:t - 4], epst, ACT.Copy).then_inc(eva, 1)

            def att(g, nl):
                at = 512 - nl
                exps(8, g, lambda u: nl + CTX + 1, lambda u: banks(2 * (u % 2), 1024)[:, at:512 + CTX + 1], late_probs)
            att(U_ATT2, 2 * P)
            with act_e.Fori(1, NT - 1) as n:
                att(n * 8 + U_ATT2, 3 * P)
            att(U_ATT2 + 8 * (NT - 1), 2 * P)
            for k in range(4):
                half1(T_AT + k, (attT[:, k, hi], ps[:, b1(T_AT + k), :])).then_inc(eva, 1)
            with act_e.Fori(0, 4) as j:
                for b in range(2):
                    act_e.wait_ge(tps, 4 * j + (2 * (T_OUT2 + b) + 2))
                    act_e.wait_ge(s_x3, 2 * j + b + 1)
                    act_e.activation(gt1o[b], ps[:, b1(T_OUT2 + b), :], ACT.Copy, scale=mod[:, 2 * j + (16 + b), 0:1]).then_inc(eva, 1)
                    act_e.wait_ge(evv, 2 * j + (T_OUT2 + b + 1))
                    act_e.wait_ge(s_x3, 2 * j + b + 2)
                    act_e.wait_ge(s_zadd, 2 * j + (9 + b + 1))
                    act_e.activation(late_probs[b], xT[:, bass.ds(2 * j + b, 1), :].rearrange("p a b -> p (a b)"), ACT.Square).then_inc(s_zsq, 1)
            if STOP <= 2:
                return
            norm(9)
            shift(9, 51, hT, 24, 0)

            act_e.wait_ge(s_lgT, 1)
            act_e.activation(lgT, banks(0, S)[0:NE], ACT.Copy).then_inc(s_lgc, 1)
            act_e.wait_ge(s_rm, 1)
            act_e.activation(aff, aff, ACT.Exp).then_inc(s_re, 1)
            for i in range(2 * NT):
                g, dst = T_XR + i, tok[i % 2]
                act_e.wait_ge(tps, 2 * g + 2)
                if i >= 2:
                    act_e.wait_ge(s_tkst[i % 2], 16 * (i // 2))
                if i >= NT:
                    act_e.wait_ge(s_aff, 1)
                    act_e.activation(dst[:, D:ROW], aff[:, i - NT, :], ACT.Copy)
                act_e.activation(dst[:, 0:D], banks(2 * (g % 2), D), ACT.Copy).then_inc(eva, 1)
            def columns(e, b):
                act_e.wait_ge(s_xt, e + 1)
                act_e.activation(x_hi[:, b].rearrange("p a b -> p (a b)"), banks(4, D), ACT.Copy).then_inc(s_xhi, 1)

            def silu(e, used):
                act_e.wait_ge(s_eu, used)
                if not isinstance(e, int) or e:
                    act_e.wait_ge(s_ga, e)
                act_e.activation(sgate, banks(0, D), ACT.Silu).then_inc(s_sg, 1)

            def part_high(n, sl, a, e, first=False):
                act_e.wait_ge(wl[sl], e * 16 + 16 * (loads_before("expert", sl) + 1))
                if not first:
                    act_e.wait_ge(s_eu, n + (1 - RING))
                act_e.activation(e_hi[:, (2 * sl + a) % RING, :], slot[sl][:, a * D:(a + 1) * D], ACT.Copy).then_inc(s_ehi, 1)

            def expert(e, b, last=False):
                for i, sl, a, ee in expert_items(e, last):
                    if isinstance(e, int) and e == 0 and i == RING - 1:
                        silu(0, KT)
                    if not last and i == 4:
                        columns(e + 1, 1 - b)
                    if not last and i == 2 * KT + RING - 1:
                        silu(e + 1, expert_item(e, 2 * KT))
                    if i == (KT + 4 if last else 2 * KT):
                        act_e.wait_ge(s_at2, e + 1)
                        act_e.activation(t_hi.rearrange("p a b -> p (a b)"), banks(4, D), ACT.Copy).then_inc(s_thi, 1)
                    part_high(expert_item(e, i), sl, a, ee)

            for b in range(2):
                act_e.wait_ge(s_tkst[b], 16 * NT)
            columns(0, 0)
            for k in range(KT):
                part_high(k, k // 2, k % 2, 0, k < RING)
            expert(0, 0)
            with act_e.Fori(0, NE // 2 - 1) as q:
                for b in range(2):
                    expert(2 * q + (1 + b), 1 - b)
            expert(NE - 1, 1, last=True)
            for i in range(NT):
                act_e.wait_ge(s_fl[i], 16)
                ac.mark(act_e.activation(fsq, fin[i], ACT.Square, accum_out=fss[:, i:i + 1]))
                ac.need()
                act_e.activation(frs[:, i:i + 1], fss[:, i:i + 1], ACT.Sqrt, bias=epst, scale=1.0 / D).then_inc(s_frt, 1)

        @block.vector
        def _(v):
            vc_ = Chain(v, vch)
            done = [0, 0]

            def sums(i):
                sqs, sm, rs = NORM_AT[i]
                n = NORM_N[i]
                for k in range(1, NORM_K[i]):
                    v.wait_ge(s_sq, done[0] + k + 1)
                    if k > 1:
                        v.wait_ge(s_add, done[1] + k - 1)
                    v.tensor_tensor(sm[:, 0:n], sm[:, 0:n], sqs[k % 2][:, 0:n], ALU.add).then_inc(s_add, 1)
                done[0] += NORM_K[i]
                done[1] += NORM_K[i] - 1
                v.wait_ge(s_sq, done[0])
                if done[1]:
                    v.wait_ge(s_add, done[1])
                v.tensor_copy(rmax[:, 1:2], epst).then_inc(s_ssq, 1)

            def diagonal(i):
                v.wait_ge(s_rt, i + 1)
                nt = NORM_N[i] // P
                vc_.link(v.reciprocal(rms[i % 2][:, 0:nt], rms[i % 2][:, 0:nt]))
                v.scalar_tensor_tensor(NORM_AT[i][0][0][:, 0:nt * P].rearrange("p (t c) -> p t c", t=nt), rms[i % 2][:, 0:nt].unsqueeze(2).to_broadcast([P, nt, P]), float(D),
                                       ident.unsqueeze(1).to_broadcast([P, nt, P]), ALU.mult, ALU.mult).then_inc(s_dg, 1)

            def spread_ready(i):
                v.wait_ge(s_rs, i + 1)
                return NORM_AT[i][2][:, 0:NORM_N[i]]

            def inverse(i):
                diagonal(i)
                return spread_ready(i)

            vc_.mark(v.memset(epst, EPS))
            v.wait_ge(par, 16 * NPAR)
            vc_.mark(v.tensor_copy(identb, ident))
            vc_.mark(v.tensor_copy(causalb, con("causal")))
            vc_.mark(v.tensor_copy(leftb, con("left")))
            vc_.mark(v.tensor_scalar(sinkB, sinkB, float(D), None, ALU.mult))
            vc_.need()
            v.tensor_copy(rmax[:, 3:4], epst).then_inc(s_bf, 1)
            v.wait_ge(s_bl, 1)
            v.tensor_tensor(exts, ps[0:8, 4, 0:384], extm, ALU.add).then_inc(s_bls, 1)
            sums(0)
            rs = inverse(0)
            for k in range(KT):
                v.scalar_tensor_tensor(hT[:, k, :], xT[:, k, :], col("attn_pre", k), rs, ALU.mult, ALU.mult).then_inc(s_h, 1)

            def b0(t):
                return 2 * (t % 2)
            lo = slice(0, HALF)

            def half0(t, dst, src, scale=None):
                v.wait_ge(tps, 2 * t + 1)
                return v.tensor_scalar(dst, src, scale, None, ALU.mult) if scale else v.tensor_copy(dst, src)

            v.wait_ge(s_flip, 1)
            v.tensor_copy(swab.rearrange("p a b -> p (a b)"), banks(4, 2048))
            for t in range(4):
                g = T_V + t
                half0(g, swav[:, 2 * t, :], ps[:, b0(g), 0:P])
                v.tensor_copy(VH[:, 2 * t, 0:256], ps[:, b0(g), P:384]).then_inc(evv, 1)
            v.wait_ge(s_mod, 1)
            vc_.mark(v.tensor_copy(mod[:, 0:2 * KT, :], ps[:, 4, 0:4 * KT].rearrange("p (a b) -> p a b", b=2)))
            for t in range(13):
                g = T_IN + t
                src = ps[:, b0(g), :]
                if t < 4:
                    half0(g, swaq[:, t, lo], src, HD ** -0.5).then_inc(evv, 1)
                elif t == 4:
                    half0(g, swak[:, lo], src).then_inc(evv, 1)
                elif t < 9:
                    dst, h = (QH, 2 * (t - 5)) if t < 7 else (KH, 2 * (t - 7))
                    half0(g, dst[0:HD, h, lo], src[0:HD], HD ** -0.5 if t < 7 else None)
                    v.tensor_scalar(dst[0:HD, h + 1, lo], src[HD:P], HD ** -0.5 if t < 7 else 1.0, None, ALU.mult).then_inc(evv, 1)
                elif t < 11:
                    half0(g, cq[:, t - 9, lo], src).then_inc(evv, 1)
                elif t == 11:
                    half0(g, ckv[:, lo], src).then_inc(evv, 1)
                else:
                    half0(g, krope[64:96, lo], src[64:96])
                    v.tensor_scalar(flog[0:4, lo], src[0:4], fbias[0:4], None, ALU.add).then_inc(evv, 1)
            v.wait_ge(evv, T_UQ)
            v.wait_ge(eva, T_UQ)
            v.scalar_tensor_tensor(ftmp[0:4], flog[0:4], -1.0, flog[0:4], ALU.mult, ALU.max).then_inc(s_f, 1)
            v.wait_ge(s_fe, 1)
            vc_.link(v.tensor_scalar(flog[0:4], flog[0:4], 0.0, None, ALU.min))
            vc_.link(v.tensor_tensor(ftmp[0:4], flog[0:4], ftmp[0:4], ALU.subtract))
            vc_.link(v.tensor_tensor_scan(flog[0:4], ftmp[0:4], ftmp[0:4], 0.0, ALU.add, ALU.min))
            v.tensor_scalar(flog[0:4], flog[0:4], -1.0, None, ALU.mult).then_inc(s_fd, 1)
            sums(1)
            rs = inverse(1)
            for k in range(2):
                v.scalar_tensor_tensor(cq[:, k, :], cq[:, k, :], col("qlat", k), rs, ALU.mult, ALU.mult).then_inc(s_h, 1)
            sums(2)
            rs = inverse(2)
            v.scalar_tensor_tensor(ckv, ckv, col("kvlat"), rs, ALU.mult, ALU.mult).then_inc(s_h, 1)

            def rotate(i, x, c, s, tmp, r):
                v.wait_ge(s_sw, i + 1)
                vc_.mark(v.tensor_tensor(tmp[r], banks(4, S)[r], s[r], ALU.mult))
                vc_.link(v.tensor_tensor(x[r], x[r], c[r], ALU.mult))
                v.tensor_tensor(x[r], x[r], tmp[r], ALU.add).then_inc(s_rot, 1)

            r32 = slice(64, 96)
            v.wait_ge(s_rope, 16)
            rotate(0, krope, rope1[:, 0, :], rope1[:, 1, :], ropet, r32)
            for h in range(4):
                g = T_UQ + h
                half0(g, QH[0:QK, 4 + h, lo], ps[0:QK, b0(g), :], QK ** -0.5).then_inc(evv, 1)
                if h:
                    rotate(h, QH[:, 3 + h, :], rope1[:, 0, :], rope1[:, 1, :], ropet, r32)
            for h in range(4):
                g = T_UKV + h
                half0(g, KH[0:HD, 4 + h, lo], ps[0:HD, b0(g), :]).then_inc(evv, 1)
                if h == 0:
                    rotate(4, QH[:, 7, :], rope1[:, 0, :], rope1[:, 1, :], ropet, r32)
            for t in range(4):
                g = T_LV + t
                half0(g, VH[:, 2 * t, 256:512], ps[:, b0(g), 0:256]).then_inc(evv, 1)

            def units(g, now, before=None, probsT=probsT):
                def after(s, d, u, least):
                    if not isinstance(g, int) or g + u >= least:
                        v.wait_ge(s, g + (u + d))

                def group(w):
                    return now if w >= 0 else before
                for u in range(8 if now else 2):
                    if now:
                        c = u % 4
                        v.wait_ge(s_S, g + (u + 1))
                        v.tensor_reduce(nmax[:, c:c + 1], now[0](u), AX_X, ALU.max, negate=True).then_inc(s_max, 1)
                    w = u - 1
                    if (now or u == 0) and group(w):
                        v.wait_ge(s_T, g + (w + 1))
                        after(s_pv, -1, w, 2)
                        n = group(w)[1](w % 8)
                        v.tensor_copy(probsT[w % 2][:, 0:n], banks(4, n)).then_inc(s_pt, 1)
                    w = u - 2
                    if group(w):
                        c = w % 4
                        v.wait_ge(s_pv, g + (w + 1))
                        vc_.link(v.reciprocal(rec[:, c:c + 1], den[:, c:c + 1]))
                        v.tensor_scalar(group(w)[2](w % 8), ps[:, 6 + w % 2, 0:HD], rec[:, c:c + 1], None, ALU.mult).then_inc(s_o, 1)

            def hd(u):
                return (u // 2 + 4 * (u % 2)) * HD

            def swa(n):
                w = P if isinstance(n, int) and n == 0 else 2 * P
                return lambda u: ps[:, 2 * (u % 2), 0:w + 1], lambda u: w, lambda u: mixed[:, n, hd(u):hd(u) + HD]

            def dense(h):
                return lambda u: banks(2 * (u % 2), (u + 1) * P), lambda u: (u + 1) * P, lambda u: mixed[:, u, bass.ds(h * HD + 512, HD)]
            units(U_SWA, swa(0))
            units(8, swa(1), swa(0))
            with v.Fori(2, NT) as n:
                vc_.enter(n - 2, 8)
                units(n * 8, swa(n), swa(n - 1))
                vc_.leave(NT - 2)
            units(U_DENSE, dense(0), swa(NT - 1))
            with v.Fori(1, CH) as h:
                vc_.enter(h - 1, 8)
                units(h * 8 + U_DENSE, dense(h), dense(h - 1))
                vc_.leave(CH - 1)
            units(U_ATT2, None, dense(CH - 1))
            v.wait_ge(s_gq, 3)
            v.reciprocal(grs, grs).then_inc(s_gr, 1)
            v.wait_ge(s_gr, 1)
            for i in range(NT):
                for j, (c, w) in ((1, (512, 256)), (2, (768, 256))):
                    last = v.tensor_scalar(mixed[:, i, c:c + w], mixed[:, i, c:c + w], grs[:, i, j:j + 1], None, ALU.mult)
                last.then_inc(s_gn, 1)
            for k in range(KT):
                g = T_MT + k
                v.wait_ge(eva, g + 1)
                v.scalar_tensor_tensor(m_lo[:, k, :], banks(b0(g), S), col("group", k), m_hi[:, k, :].bitcast(F32), ALU.mult, ALU.subtract).then_inc(evv, 1)
            v.wait_ge(tps, 2 * T_OUT)
            v.memset(ssq, 0.0).then_inc(s_zadd, 1)
            with v.Fori(0, 4) as j:
                for b in range(2):
                    v.wait_ge(tps, 4 * j + (2 * (T_OUT + b) + 1))
                    v.tensor_copy(zT[:, 2 * j + b, lo], ps[:, b0(T_OUT + b), :]).then_inc(evv, 1)
                    v.wait_ge(s_zsq, 2 * j + (b + 1))
                    v.wait_ge(s_zadd, 2 * j + (b + 1))
                    v.tensor_tensor(ssq, ssq, sq[b], ALU.add).then_inc(s_zadd, 1)
            v.wait_ge(s_zadd, 9)
            v.memset(rmax[:, 1:2], 0.0).then_inc(s_ssq, 1)
            rs = inverse(3)
            for k in range(KT):
                v.scalar_tensor_tensor(zT[:, k, :], zT[:, k, :], col("attn_post", k), rs, ALU.mult, ALU.mult).then_inc(s_zn, 1)
            sums(4)
            rs = inverse(4)

            def split_input(half):
                hs = slice(half * HALF, (half + 1) * HALF)
                if half:
                    v.wait_ge(s_wu, W_DN[0])
                for k in range(KT):
                    tmp = sq[k % 2][:, 0:HALF]
                    vc_.link(v.scalar_tensor_tensor(tmp, xT[:, k, hs], col("ffn_pre", k), rstdB[:, hs], ALU.mult, ALU.mult))
                    v.tensor_copy(h_hi[:, k, :], tmp).then_inc(s_hhi, 1)
                    v.wait_ge(s_hhi, half * KT + k + 1)
                    v.tensor_tensor(h_lo[:, k, :], tmp, h_hi[:, k, :].bitcast(F32), ALU.subtract).then_inc(s_h, 1)
            split_input(0)
            v.memset(rmax[:, 0:1], 0.0).then_inc(s_uv, 1)
            v.memset(rmax[:, 1:2], 0.0).then_inc(s_uv, 1)
            v.memset(rmax[:, 2:3], 0.0).then_inc(s_act, 1)
            for half in range(2):
                p0 = half * FT

                def taps(j, bs=(0, 1)):
                    for b in bs:
                        g = 2 * j + (p0 + b)
                        w0, w1 = COLS["conv_w"][0], COLS["conv_w"][0] + 2 * FT
                        v.wait_ge(s_ua, 2 * g + 2)
                        for q in range(2):
                            t = 2 * j + (q * FT + b)
                            vc_.mark(v.scalar_tensor_tensor(convy[b][q][:, 1:HALF], ps[:, 2 * b + q, 0:HALF - 1], cols[:, bass.ds(t + w1, 1)],
                                                            convy[b][q][:, 1:HALF], ALU.mult, ALU.add))
                            if half:
                                vc_.mark(v.scalar_tensor_tensor(convy[b][q][:, 0:1], carry[:, bass.ds(t, 1), 1:2].rearrange("p a b -> p (a b)"), cols[:, bass.ds(t + w1, 1)],
                                                                convy[b][q][:, 0:1], ALU.mult, ALU.add))
                        vc_.need()
                        for q in range(2):
                            t = 2 * j + (q * FT + b)
                            two = carry[:, bass.ds(t, 1), :].rearrange("p a b -> p (a b)")
                            if half:
                                vc_.mark(v.scalar_tensor_tensor(convy[b][q][:, 0:2], two, cols[:, bass.ds(t + w0, 1)],
                                                                convy[b][q][:, 0:2], ALU.mult, ALU.add))
                            else:
                                vc_.mark(v.tensor_copy(two, ps[:, 2 * b + q, HALF - 2:HALF]))
                            last = v.scalar_tensor_tensor(convy[b][q][:, 2:HALF], ps[:, 2 * b + q, 0:HALF - 2], cols[:, bass.ds(t + w0, 1)],
                                                          convy[b][q][:, 2:HALF], ALU.mult, ALU.add)
                            if half:
                                vc_.mark(last) if q == 0 else last.then_inc(s_uv, 1)
                            elif q == 1:
                                last.then_inc(s_uv, 1)
                        if half:
                            vc_.mark(v.memset(rmax[:, 3:4], 0.0))
                        v.wait_ge(s_gl, g + 1)
                        v.tensor_tensor(act[:, bass.ds(2 * j + b, 1), :].rearrange("p a b -> p (a b)"), gelu[b], convy[b][1], ALU.mult).then_inc(s_act, 1)
                taps(0, (0,))
                if half:
                    diagonal(5)
                else:
                    v.wait_ge(s_mod, 2)
                    vc_.link(v.tensor_copy(mod[:, 2 * KT:5 * KT, :], ps[:, 4, 0:6 * KT].rearrange("p (a b) -> p a b", b=2)))
                    for b in range(2):
                        vc_.mark(v.tensor_tensor(mod[:, :, b], mod[:, :, b], col("b_ada", 0, 40), ALU.add))
                    vc_.need()
                    for i, (row, b, g) in enumerate(((8, 0, "g_mix"), (8, 1, "g_mix"), (32, 0, "g_ffn"))):
                        vc_.mark(v.scalar_tensor_tensor(gsc[:, i, :], mod[:, row:row + 8, b], 1.0, col(g, 0, 8), ALU.add, ALU.mult))
                    vc_.need()
                taps(0, (1,))
                if half:
                    rs = spread_ready(5)
                    for k in range(KT):
                        v.scalar_tensor_tensor(yT[:, k, :], yT[:, k, :], col("ffn_post", k), rs, ALU.mult, ALU.mult).then_inc(s_zn, 1)
                    for k in range(KT):
                        v.wait_ge(s_zn, KT + k + 1)
                        v.tensor_tensor(xT[:, k, lo], xT[:, k, lo], yT[:, k, :], ALU.add).then_inc(s_x, 1)
                with v.Fori(1, FT // 2) as j:
                    vc_.enter(j - 1, 16 if half else 8)
                    taps(j)
                    vc_.leave(FT // 2 - 1)
                if half == 0:
                    split_input(1)
                if half:
                    sums(6)
                for t in range(0, KT, 2):
                    v.wait_ge(tps, 2 * (T_DN + 4 * half) + t + 1)
                    v.tensor_copy(yT[:, t, :], ps[:, t, :]).then_inc(evv, 1)
                sums(5 + 2 * half)
            diagonal(6)
            diagonal(7)
            rs = spread_ready(6)
            for k in range(KT):
                v.scalar_tensor_tensor(hcT[:, k, :], ctxT[:, k, :], gsc[:, 1, k:k + 1], rs, ALU.mult, ALU.mult).then_inc(s_h, 1)
            rs = spread_ready(7)
            for k in range(KT):
                v.scalar_tensor_tensor(yT[:, k, :], yT[:, k, :], col("ffn_post", k), rs, ALU.mult, ALU.mult).then_inc(s_zn, 1)
            if STOP <= 1:
                return
            sums(8)
            v.wait_ge(s_cx, 1)
            v.tensor_copy(kc, ps[:, 4, 0:CTX]).then_inc(s_cxe, 1)
            rs = inverse(8)
            for i in range(2 * KT + 1):
                if 2 <= i < 2 * KT:
                    v.wait_ge(s_hhi, 2 * KT + i - 1)
                if i < 2 * KT:
                    k, hs = i % KT, slice(i // KT * HALF, (i // KT + 1) * HALF)
                    v.scalar_tensor_tensor(sq[i % 2][:, 0:HALF], xT[:, k, hs], gsc[:, 0, k:k + 1], rs[:, hs], ALU.mult, ALU.mult).then_inc(s_h, 1)
                if i:
                    k, hs = (i - 1) % KT, slice((i - 1) // KT * HALF, ((i - 1) // KT + 1) * HALF)
                    v.wait_ge(s_hb, KT + i)
                    v.scalar_tensor_tensor(g_lo[:, k, hs], sq[(i - 1) % 2][:, 0:HALF], mod[:, k, 0:1], g_hi[:, k, hs].bitcast(F32), ALU.add, ALU.subtract).then_inc(s_hhi, 1)
            v.wait_ge(s_rp, 16)
            for t in range(4):
                g = T_V2[t]
                half0(g, v2[:, 2 * t, :], ps[:, b0(g), 0:P]).then_inc(evv, 1)
                if t == 1:
                    half0(T_K2, k2[:, lo], ps[:, b0(T_K2), :]).then_inc(evv, 1)
                if t == 2:
                    rotate(5, k2, rope2[:, 0, :], rope2[:, 1, :], ropet2, slice(0, P))
            for t in range(1, 17):
                g = T_IN2 + t
                src = ps[:, b0(g), :]
                if t < 5:
                    half0(g, q2[:, t - 1, lo], src, HD ** -0.5).then_inc(evv, 1)
                    if t > 1:
                        rotate(4 + t, q2[:, t - 2, :], rope2[:, 0, :], rope2[:, 1, :], ropet2, slice(0, P))
                    continue
                c, part = (t - 5) // 3, (t - 5) % 3
                both = banks(b0(g), S)
                v.wait_ge(tps, 2 * g + 2)
                if part == 0:
                    if c:
                        v.wait_ge(s_cv, c)
                    v.tensor_copy(convu, both).then_inc(evv, 1)
                    v.wait_ge(evv, g + 1)
                    if c == 0:
                        rotate(9, q2[:, 3, :], rope2[:, 0, :], rope2[:, 1, :], ropet2, slice(0, P))
                elif part == 1:
                    vc_.need()
                    vc_.link(v.tensor_tensor(convu, both, convu, ALU.mult))
                    v.tensor_copy(rmax[:, 0:1], epst).then_inc(evv, 1)
                    vc_.link(v.tensor_scalar(convo, convu, col("conv2", 4 + c), None, ALU.mult))
                    vc_.link(v.scalar_tensor_tensor(convo[:, 1:S], convu[:, 0:S - 1], col("conv2", c), convo[:, 1:S], ALU.mult, ALU.add))
                    vc_.link(v.scalar_tensor_tensor(convo[:, 0:S - 1], convu[:, 1:S], col("conv2", 8 + c), convo[:, 0:S - 1], ALU.mult, ALU.add))
                else:
                    vc_.link(v.tensor_tensor(convm[:, c, :], both, convo, ALU.mult))
                    v.tensor_copy(rmax[:, 0:1], epst).then_inc(evv, 1)
                    v.tensor_copy(rmax[:, 1:2], epst).then_inc(s_cv, 1)

            def att(n, nl):
                at = 512 - nl
                return (lambda u: banks(2 * (u % 2), 1024)[:, at:512 + CTX + 1], lambda u: nl + CTX, lambda u: att2[:, n, hd(u):hd(u) + HD])
            def units2(g, now, before=None):
                units(g, now, before, late_probsT)
            units2(U_ATT2, att(0, 2 * P))
            units2(U_ATT2 + 8, att(1, 3 * P), att(0, 2 * P))
            with v.Fori(2, NT - 1) as n:
                vc_.enter(n - 2, 8)
                units2(n * 8 + U_ATT2, att(n, 3 * P), att(n - 1, 3 * P))
                vc_.leave(NT - 3)
            units2(U_END - 8, att(NT - 1, 2 * P), att(NT - 2, 3 * P))
            units2(U_END, None, att(NT - 1, 2 * P))
            for k in range(4):
                half0(T_AT + k, attT[:, k, lo], ps[:, b0(T_AT + k), :]).then_inc(evv, 1)
            v.wait_ge(tps, 2 * T_OUT2)
            v.memset(late_probsT[0], 0.0).then_inc(s_zadd, 1)
            with v.Fori(0, 4) as j:
                for b in range(2):
                    m = 2 * j + b
                    v.wait_ge(tps, 4 * j + (2 * (T_OUT2 + b) + 1))
                    v.scalar_tensor_tensor(xT[:, m, lo], ps[:, b0(T_OUT2 + b), :], mod[:, m + 16, 0:1], xT[:, m, lo], ALU.mult, ALU.add).then_inc(evv, 1)
                    v.wait_ge(s_zsq, 2 * j + (8 + b + 1))
                    v.wait_ge(s_zadd, 2 * j + (9 + b + 1))
                    v.tensor_tensor(late_probsT[0], late_probsT[0], late_probs[b], ALU.add).then_inc(s_zadd, 1)
            if STOP <= 2:
                return
            v.wait_ge(s_zadd, 18)
            v.memset(rmax[:, 1:2], 0.0).then_inc(s_ssq, 1)
            rs = inverse(9)
            for k in range(KT):
                v.scalar_tensor_tensor(hT[:, k, :], xT[:, k, :], gsc[:, 2, k:k + 1], rs, ALU.mult, ALU.mult).then_inc(s_h, 1)

            v.wait_ge(s_lg, 1)
            lg = ps[:, 4, 0:NT * NE].rearrange("p (a b) -> p a b", a=NT)
            vc_.link(v.tensor_reduce(rmx, lg, AX_X, ALU.max))
            v.tensor_tensor(aff, lg, rmx.unsqueeze(2).to_broadcast([P, NT, NE]), ALU.subtract).then_inc(s_rm, 1)
            v.wait_ge(s_re, 1)
            vc_.link(v.tensor_reduce(rsum, aff, AX_X, ALU.add))
            vc_.link(v.reciprocal(rsum, rsum))
            vc_.link(v.tensor_tensor(aff, aff, rsum.unsqueeze(2).to_broadcast([P, NT, NE]), ALU.mult))
            v.tensor_copy(rmax[:, 0:1], epst).then_inc(s_aff, 1)
            for k in range(KT):
                last = v.tensor_scalar(silu_b[:, k, :], con("mean"), scT[:, k, 0:1], float(D), ALU.mult, ALU.mult)
            last.then_inc(s_sb, 1)
            v.wait_ge(s_at, 1)
            vc_.link(v.tensor_copy(work, ps[0:NE, 5:7, :].rearrange("p a b -> p (a b)")))
            for _ in range(CAP // 8):
                vc_.link(v.max(top8[0:NE], work))
                vc_.link(v.match_replace(work, top8[0:NE], work, -1.0))
            vc_.link(v.tensor_scalar(work, work, 0.0, None, ALU.is_lt))
            vc_.link(v.tensor_tensor_scan(pos, work, work, 0.0, ALU.add, ALU.max))
            v.tensor_copy(posbf, pos).then_inc(s_pos, 1)
            v.wait_ge(s_g2, 1)
            v.wait_ge(s_late, 48)
            v.tensor_tensor(gt2B, banks(2, D), gt2B, ALU.add).then_inc(s_g2e, 1)
            for e in range(NE):
                if e:
                    v.wait_ge(s_cnt, e)
                v.wait_ge(s_pb, e + 1)
                v.tensor_scalar(cntj, banks(4 + 2 * (e % 2), S), con("slot"), None, ALU.is_le, ALU.add, accum_out=idxf[:, e:e + 1]).then_inc(s_cnt, 1)
                v.wait_ge(s_cnt, e + 1)
                v.tensor_copy(idxu[:, e:e + 1], idxf[:, e:e + 1]).then_inc(s_idx, 1)
            v.memset(rmax[:, 0:1], 0.0).then_inc(s_ys, 1)

            def columns_low(e, b):
                v.wait_ge(s_xhi, e + 1)
                v.tensor_tensor(x_lo[:, b].rearrange("p a b -> p (a b)"), banks(4, D), x_hi[:, b].rearrange("p a b -> p (a b)").bitcast(F32), ALU.subtract).then_inc(s_xe, 1)

            def part_low(n, sl, a):
                r = (2 * sl + a) % RING
                v.wait_ge(s_ehi, n + 1)
                v.tensor_tensor(e_lo[:, r, :], slot[sl][:, a * D:(a + 1) * D], e_hi[:, r, :].bitcast(F32), ALU.subtract).then_inc(s_elo, 1)

            def output(e, b, used):
                v.wait_ge(s_eu, used)
                v.wait_ge(s_gs, e + 1)
                v.wait_ge(s_yf, e + 1)
                v.scalar_tensor_tensor(yx[b], banks(6, D), gslot[b], gt2B, ALU.mult, ALU.mult).then_inc(s_ys, 1)

            def expert(e, b, last=False):
                v.wait_ge(s_gat[b], 8 * e + (16 - 8 * b))
                v.tensor_copy(gslot[b], xs[b][:, bass.ds(e + D, 1)]).then_inc(s_gs, 1)
                for i, sl, a, _ in expert_items(e, last):
                    if i == RING - 1 and not (isinstance(e, int) and e == 0):
                        output(e - 1, 1 - b, expert_item(e, 0))
                    if not last and i == 4:
                        columns_low(e + 1, 1 - b)
                    if i == KT + RING - 1:
                        v.wait_ge(s_sg, e + 1)
                        v.wait_ge(s_eu, expert_item(e, KT))
                        v.tensor_tensor(actx, banks(2, D), sgate, ALU.mult).then_inc(s_ga, 1)
                    if i == (KT + 4 if last else 2 * KT):
                        v.wait_ge(s_thi, e + 1)
                        v.tensor_tensor(t_lo.rearrange("p a b -> p (a b)"), banks(4, D), t_hi.rearrange("p a b -> p (a b)").bitcast(F32), ALU.subtract).then_inc(s_ae, 1)
                    part_low(expert_item(e, i), sl, a)

            columns_low(0, 0)
            for k in range(KT):
                part_low(k, k // 2, k % 2)
            expert(0, 0)
            with v.Fori(0, NE // 2 - 1) as q:
                for b in range(2):
                    expert(2 * q + (1 + b), 1 - b)
            expert(NE - 1, 1, last=True)
            output(NE - 1, 1, expert_item(NE - 1, 2 * KT))
            for i in range(NT):
                v.wait_ge(s_frt, i + 1)
                vc_.link(v.reciprocal(frs[:, i:i + 1], frs[:, i:i + 1]))
                v.scalar_tensor_tensor(fin[i], fin[i], frs[:, i:i + 1], g_fin, ALU.mult, ALU.mult).then_inc(s_fo, 1)

        @block.gpsimd
        def _(gp):
            gp.wait_ge(tps, 2 * T_IN)
            gp.memset(QH[64:96, 0:4, :], 1.0).then_inc(s_aug, 1)
            gp.wait_ge(s_h, 8)
            gp.memset(KH[64:96, 0:4, :], 0.0).then_inc(s_aug, 1)
            gp.wait_ge(s_aug, 2)
            gp.wait_ge(s_rot, 1)
            for h in range(4):
                last = gp.tensor_copy(KH[64:96, 4 + h, :], krope[64:96])
            last.then_inc(s_krc, 1)
            gp.wait_ge(s_krc, 1)
            gp.wait_ge(evv, T_MT)
            gp.wait_ge(eva, T_MT)
            gp.wait_ge(s_rot, 5)
            def stage_swa(q0, k0, w, b):
                gp.tensor_copy(qs[b], swaq[:, :, q0])
                gp.tensor_copy(ks[b][:, 0:w], swak[:, k0]).then_inc(s_stage, 1)
            stage_swa(slice(0, P), slice(0, P), P, 0)
            stage_swa(slice(P, 2 * P), slice(0, 2 * P), 2 * P, 1)
            with gp.Fori(1, NT // 2) as m:
                for b in range(2):
                    n = 2 * m + b
                    gp.wait_ge(s_S, m * 16 + 8 * (b - 1))
                    stage_swa(bass.ds(n * P, P), bass.ds(n * P - P, 2 * P), 2 * P, b)
            gp.wait_ge(s_frow, 16)
            for b in range(2):
                gp.wait_ge(s_S, 8 * (NT - 1 + b))
                gp.tensor_copy(qh[b][0:QK], QH[0:QK, b, :]).then_inc(s_stage, 1)
            with gp.Fori(1, CH // 2) as m:
                for b in range(2):
                    gp.wait_ge(s_S, m * 16 + (8 * (b - 1) + U_DENSE))
                    gp.tensor_copy(qh[b][0:QK], QH[0:QK, bass.ds(2 * m + b, 1), :].rearrange("p a c -> p (a c)")).then_inc(s_stage, 1)
            def weight_low(gg, c, q):
                gp.wait_ge(s_whi, 2 * gg + (q + 1))
                gp.tensor_tensor(w_lo[:, q, :], slot[c][:, q * D:(q + 1) * D], w_hi[:, q, :].bitcast(F32), ALU.subtract).then_inc(s_wlo, 1)

            def gated_low(half, k, q):
                gp.wait_ge(s_ahi, k + (half * FT + 1))
                gp.tensor_tensor(a_lo[:, q, :], act[:, k, :], a_hi[:, q, :].bitcast(F32), ALU.subtract).then_inc(s_alo, 1)

            for q in range(2):
                weight_low(G_OUT, 0, q)
            with gp.Fori(0, 2) as m:
                for c in range(2):
                    for q in range(2):
                        weight_low(2 * m + (G_OUT + c + 1), 1 - c, q)
            gp.wait_ge(xld, 16)
            for k in range(KT):
                gp.wait_ge(s_zn, k + 1)
                gp.tensor_tensor(xT[:, k, :], xT[:, k, :], zT[:, k, :], ALU.add).then_inc(s_x, 1)
            for half in range(2):
                sl = G_UP[half] % 2
                with gp.Fori(0, FT // 2) as j:
                    for b in range(2):
                        for q in range(2):
                            weight_low(2 * j + (G_UP[half] + b + 1), (sl + b + 1) % 2, q)
                for q in range(2):
                    gated_low(half, q, q)
                sl = G_DN[half] % 2
                with gp.Fori(0, (FT // 2 - 1) // 2) as m:
                    for c in range(2):
                        for q in range(2):
                            weight_low(2 * m + (G_DN[half] + c + 1), (sl + c + 1) % 2, q)
                            gated_low(half, 4 * m + (2 * c + 2 + q), q)
                for q in range(2):
                    weight_low((G_UP[1], G_IN2)[half], (G_UP[1], G_IN2)[half] % 2, q)
            for k in range(KT):
                gp.wait_ge(s_zn, 2 * KT + k + 1)
                gp.tensor_tensor(xT[:, k, HALF:S], xT[:, k, HALF:S], yT[:, k, :], ALU.add).then_inc(s_x, 1)
            if STOP <= 1:
                return
            for n in range(2, 18):
                weight_low(G_IN2 + n // 2, (n // 2) % 2, n % 2)
            gp.wait_ge(s_rot, 10)
            gp.wait_ge(s_cv, 4)
            n0 = NT + CH

            def stage(q0, k0, w, b):
                gp.tensor_copy(qs[b], q2[:, :, q0])
                gp.tensor_copy(ks[b][:, 0:w], k2[:, k0]).then_inc(s_stage, 1)
            stage(slice(0, P), slice(0, 2 * P), 2 * P, 0)
            stage(slice(P, 2 * P), slice(0, 3 * P), 3 * P, 1)
            with gp.Fori(1, NT // 2 - 1) as m:
                for b in range(2):
                    n = 2 * m + b
                    gp.wait_ge(s_S, m * 16 + (U_ATT2 + 8 * (b - 1)))
                    stage(bass.ds(n * P, P), bass.ds(n * P - P, 3 * P), 3 * P, b)
            gp.wait_ge(s_S, U_ATT2 + 8 * (NT - 3))
            stage(slice(S - 2 * P, S - P), slice(S - 3 * P, S), 3 * P, 0)
            gp.wait_ge(s_S, U_ATT2 + 8 * (NT - 2))
            stage(slice(S - P, S), slice(S - 2 * P, S), 2 * P, 1)
            gp.memset(gpad, 0.0).then_inc(s_x3, 1)
            with gp.Fori(0, 4) as j:
                for b in range(2):
                    m = 2 * j + b
                    gp.wait_ge(eva, 2 * j + (T_OUT2 + b + 1))
                    gp.tensor_tensor(xT[:, m, HALF:S], xT[:, m, HALF:S], gt1o[b], ALU.add).then_inc(s_x3, 1)
            if STOP <= 2:
                return
            gp.wait_ge(s_tkst[0], 16 * NT)
            gp.wait_ge(s_tkst[1], 16 * NT)
            gc = Chain(gp, gch)

            def gather(e):
                b = e % 2
                gp.wait_ge(s_idx, e + 1)
                gc.link(gp.tensor_copy(idxs[b], idxu[:, e:e + 1]))
                gp.indirect_dma_start(out=xs[b], out_offset=None, in_=h_d,
                                      in_offset=bass.IndirectOffsetOnAxis(ap=idxs[b], axis=0)).then_inc(s_gat[b], 16)
            for e in range(2):
                gather(e)
                gp.memset(gpad, 0.0).then_inc(s_yf, 1)
            for e in range(NE):
                b = e % 2
                if e + 2 < NE:
                    gp.wait_ge(s_gs, e + 1)
                    gp.wait_ge(s_xt, e + 1)
                    gather(e + 2)
                gc.link(gp.tensor_copy(odxs[b], idxu[:, e:e + 1]))
                gp.wait_ge(s_ys, e + 2)
                gp.indirect_dma_start(out=acc_d, out_offset=bass.IndirectOffsetOnAxis(ap=odxs[b], axis=0), in_=yx[b], in_offset=None,
                                      compute_op=ALU.add).then_inc(s_sc[b], 16)
                gp.wait_ge(s_sc[b], 16 * (e // 2 + 1))
                gp.memset(gpad, 0.0).then_inc(s_yf, 1)


def _tiles(w, tile=P):
    k, n = w.shape
    return w.reshape(k // P, P, n // tile, tile).transpose(1, 2, 0, 3).reshape(P, -1)


def _cols(v):
    return np.asarray(v).reshape(-1, P).T


def _constants():
    r = np.arange(P)
    c = np.zeros((P, NCONST), np.float32)

    def put(name, a):
        c[:, CONST[name][0]:CONST[name][0] + CONST[name][1]] = a
    put("ident", np.eye(P))
    put("causal", np.where(r[None, :] <= r[:, None], 0.0, NEG))
    put("left", np.where(r[None, :] >= r[:, None], 0.0, NEG))
    put("mean", np.full((P, P), 1.0 / D))
    s16 = np.zeros((P, QK))
    for i in range(32):
        s16[64 + i, 64 + (i + 16) % 32] = 1.0
    put("swap16", s16)
    s32 = np.zeros((P, P))
    for i in range(P):
        s32[i, i // 64 * 64 + (i + 32) % 64] = 1.0
    put("swap32", s32)
    put("flip", np.eye(P)[::-1])
    put("slot", r[:, None])
    pos = np.arange(S, dtype=np.float32)
    inv = (np.float32(10000.0) ** (-(np.arange(16, dtype=np.float32) * np.float32(2.0) / np.float32(32)))).astype(np.float32)
    ang = pos[None, :] * inv[:, None]
    rope1 = np.stack([np.concatenate([np.cos(ang)] * 2), np.concatenate([-np.sin(ang), np.sin(ang)])], 1)
    inv2 = (np.float32(10000.0) ** (-np.arange(16, dtype=np.float32) / np.float32(16))).astype(np.float32)
    grid = np.arange(S)
    ang2 = np.concatenate([(grid // 64).astype(np.float32)[None] * inv2[:, None], (grid % 64).astype(np.float32)[None] * inv2[:, None]])
    rope2 = np.stack([np.concatenate([np.cos(ang2)] * 4), np.concatenate([-np.sin(ang2), np.sin(ang2)] * 2)], 1)
    dist = 255 - np.arange(384)
    d = np.maximum(dist, 0)
    ratio = np.log(np.maximum(d, 1).astype(np.float32) / np.float32(16)) / np.float32(math.log(128 / 16))
    large = np.minimum(16 + (ratio * np.float32(16)).astype(np.int32), 31)
    bucket = np.where(d < 16, d, large)
    onehot = (np.arange(32)[:, None] == bucket[None, :]).astype(np.float32)
    extmask = np.broadcast_to(np.where((dist >= 0) & (dist < P), 0.0, NEG), (8, 384))
    f = lambda a: np.ascontiguousarray(a, np.float32)
    return {"const": c, "rope1": f(rope1), "rope2": f(rope2), "onehot": onehot, "extmask": f(extmask)}


def _layout(x):
    a = {k: np.asarray(v) for k, v in x.items()}
    w = a["w_in"][0]
    pair = np.concatenate([np.r_[t * HD:(t + 1) * HD, (t + 4) * HD:(t + 5) * HD] for t in range(4)])
    sw, fx, ml = 0, 768, 768 + 772
    rope = ml + 384 + np.arange(32)
    order = np.concatenate([pair, 512 + np.arange(128), fx + np.arange(512), ml + np.arange(384)])
    last = np.concatenate([fx + 768 + np.arange(4), rope, rope[:28], rope])
    w2 = a["w_in_2"][0]
    conv = np.concatenate([768 + np.arange(c * P, (c + 1) * P) + o for c in range(4) for o in (512, 1024, 0)])
    order2 = np.concatenate([512 + np.arange(256), pair, conv])
    wup = a["w_up"][0].reshape(KT, P, 2, FT, P).transpose(1, 3, 2, 0, 4).reshape(P, -1)
    wdn = a["w_down"][0].reshape(FT, P, D).transpose(1, 0, 2).reshape(P, -1)
    cols = np.concatenate([_cols(v) for v in (
        a["attn_pre_norm"], a["group_norm"], a["attn_post_norm"], a["ffn_pre_norm"], a["conv_w"], a["conv_b"], a["ffn_post_norm"],
        a["q_latent_norm"], a["kv_latent_norm"], a["c_2"], a["c_ctx_2"], a["b_ada_2"], a["g_mix_2"], a["conv_w_2"], a["g_ffn_2"])], 1)
    out = {
        "xT": a["x"][0].T.reshape(KT, P, S).transpose(1, 0, 2), "ctxT": a["ctx_2"][0].T.reshape(KT, P, CTX).transpose(1, 0, 2),
        "w_in": np.concatenate([_tiles(w[:, order]), _tiles(w[:, last], QK)], 1),
        "w_in_v": w[:, np.r_[640:768, fx + 512:fx + 768]].reshape(KT, P, 384).transpose(1, 0, 2),
        "w_uq": a["w_uq"][0].reshape(2, P, 4 * QK).transpose(1, 0, 2), "w_ukv": a["w_ukv"][0],
        "w_out": _tiles(a["w_out"][0]), "w_up": wup, "w_down": wdn,
        "w_in2": _tiles(w2[:, order2]), "w_out2": _tiles(a["w_out_2"][0]), "cols": cols,
    }
    for n in ("forget_bias", "swa_sinks", "sink_2", "rel_bias", "w_ada_2", "b_ada_2", "g_final_2", "w_router_2", "w_gate_2", "w_up_2", "w_down_2"):
        out[n] = a[n]
    return out


def kernel(**inputs):
    import concourse.bacc as bacc
    from concourse.bass_utils import run_bass_kernel_spmd as run

    nc = bacc.Bacc("TRN2", target_bir_lowering=False, num_devices=1)
    arrays, T = {}, {}
    for name, x in {**_layout(inputs), **_constants()}.items():
        x = np.ascontiguousarray(x)
        arrays["in_" + name] = x
        T[name] = nc.dram_tensor("in_" + name, x.shape, mybir.dt.from_np(x.dtype), kind="ExternalInput").ap()
    shape = (1, S, D) if STOP > 2 else (P, KT * S)
    T["out"] = nc.dram_tensor("out_rows", shape, F32, kind="ExternalOutput").ap()
    bass_two_blocks(nc, T)
    r = run(nc, [arrays], core_ids=[0])
    return r.results[0]["out_rows"]
```

```python
import math
from contextlib import ExitStack

import numpy as np
import concourse.bass as bass
from concourse import mybir

F32 = mybir.dt.float32
F32R = mybir.dt.float32r
BF16 = mybir.dt.bfloat16
U32 = mybir.dt.uint32
ALU = mybir.AluOpType
ACT = mybir.ActivationFunctionType
AX_X = mybir.AxisListType.X

P = 128
S = 1024
D = 1024
KT = D // P
NT = S // P
HALF = 512
HD = 64
EPS = 1e-6
NEG = -1e30
SWA_H = 8
CH = 8
QK = 96
FF = 2816
FT = FF // P
CTX = 256
NE = 16
CAP = 2 * S // NE
PARTS = 3 * KT
RING = 4
ROW = D + NE
ADA = 3 * D // 2
ITEM = 2048

COLS = {}
_at = 0
for _n, _w in (("attn_pre", 8), ("group", 8), ("attn_post", 8), ("ffn_pre", 8), ("conv_w", 3 * 2 * FT),
               ("conv_b", 2 * FT), ("ffn_post", 8), ("qlat", 2), ("kvlat", 1), ("cvec", 8), ("cctx", 8),
               ("b_ada", 48), ("g_mix", 8), ("conv2", 12), ("g_ffn", 8)):
    COLS[_n] = (_at, _w)
    _at += _w
NCOLS = _at
CONST = {}
_at = 0
for _n, _w in (("ident", P), ("causal", P), ("left", P), ("mean", P), ("swap16", QK), ("swap32", P), ("flip", P), ("slot", 1)):
    CONST[_n] = (_at, _w)
    _at += _w
NCONST = _at


def bass_two_blocks(nc, T):
    with ExitStack() as ctx:
        def sem(name):
            return ctx.enter_context(nc.semaphore(name))

        def split_views(*parts):
            out, at = [], 0
            with ExitStack() as early:
                for name, kb, shape in parts:
                    if kb * 256 > at:
                        early.enter_context(nc.sbuf_tensor(f"before_{name}", [P, kb * 256 - at], F32))
                    out.append(early.enter_context(nc.sbuf_tensor(name, [P] + shape, F32R)))
                    at = kb * 256 + int(np.prod(shape))
            return out

        w_hi, w_lo, h_hi, h_lo, a_hi, a_lo = split_views(("w_hi", 16, [2, D]), ("w_lo", 24, [2, D]), ("h_hi", 32, [KT, HALF]), ("h_lo", 48, [KT, HALF]),
                                                         ("a_hi", 192, [2, HALF]), ("a_lo", 196, [2, HALF]))
        g_hi, g_lo = split_views(("g_hi", 32, [KT, S]), ("g_lo", 64, [KT, S]))
        m_hi, m_lo = split_views(("m_hi", 64, [KT, S]), ("m_lo", 128, [KT, S]))
        x_hi, t_hi, x_lo, t_lo, e_hi, e_lo = split_views(("x_hi", 106, [2, KT, P]), ("t_hi", 122, [KT, P]), ("x_lo", 128, [2, KT, P]), ("t_lo", 136, [KT, P]),
                                                         ("e_hi", 168, [RING, D]), ("e_lo", 184, [RING, D]))
        o_hi, c_hi, o_lo, c_lo = split_views(("o_hi", 48, [4, S]), ("c_hi", 80, [4, S]), ("o_lo", 128, [4, S]), ("c_lo", 176, [4, S]))
        v_lo, n_lo0, n_lo1, v_hi = split_views(("v_lo", 64, [KT, 384]), ("n_lo0", 80, [4, S]), ("n_lo1", 112, [4, S]), ("v_hi", 144, [KT, 384]))
        n_hi, n_lo = g_hi, [n_lo0[:, k, :] for k in range(4)] + [n_lo1[:, k, :] for k in range(4)]
        arena = [ctx.enter_context(nc.sbuf_tensor(f"arena{i}", [P, n], F32)) for i, n in enumerate((96 * 256, 104 * 256))]
        cols = ctx.enter_context(nc.sbuf_tensor("cols", [P, NCOLS], F32))
        const = ctx.enter_context(nc.sbuf_tensor("const", [P, NCONST], F32))
        tiny = ctx.enter_context(nc.sbuf_tensor("tiny", [P, 480], F32))
        maskbf = ctx.enter_context(nc.sbuf_tensor("maskbf", [P, 3, P], BF16))
        ps = ctx.enter_context(nc.psum_tensor("ps", [P, 8, 512], F32))

        def view(kb, n):
            at = int(kb * 256)
            a = int(kb >= 96)
            return arena[a][:, at - a * 96 * 256:at - a * 96 * 256 + n]

        def view3(kb, a, b):
            return view(kb, a * b).rearrange("p (a b) -> p a b", a=a)

        def col(name, j=0, n=1):
            return cols[:, COLS[name][0] + j:COLS[name][0] + j + n]

        def con(name):
            return const[:, CONST[name][0]:CONST[name][0] + CONST[name][1]]

        def bank(b, n=512):
            return ps[:, b, 0:n]

        def banks(b, n):
            return ps[:, b:b + (n + 511) // 512, :].rearrange("p a b -> p (a b)")[:, 0:n]

        slot = [view(8 * s, ITEM) for s in range(12)]
        hT = view3(32, KT, S)
        mixed = view3(32, NT, D)
        QH = view3(64, CH, S)
        KH = view3(96, CH, S)
        xT = view3(96, KT, S)
        wv = view3(64, KT, 384)
        VH = view3(128, NT, 512)
        swaq = view3(144, 4, S)
        swak = view(160, S)
        swav = view3(164, NT, 128)
        swab = view3(168, SWA_H, 256)
        mflip = view3(184, SWA_H, 256)
        sq = [view(176, S), view(180, S)]
        ssq = view(184, S)
        rstdB = view(188, S)
        probs = [view(176, S), view(180, S)]
        probsT = [view(184, S), view(188, S)]
        cq = view3(176, 2, S)
        ckv = view(184, S)
        krope = view(188, S)
        rope1 = view3(192, 2, S)
        qs = [view3(192 + 4 * b, 4, P) for b in range(2)]
        ks = [view(194 + 4 * b, 384) for b in range(2)]
        qh = [view(192 + 4 * b, S) for b in range(2)]
        flog = view(8, S)
        ftmp = view(12, S)
        lat_sq = [view(144, S), view(148, S)]
        lat_ssq = view(152, S)
        lat_rstd = view(156, S)
        ropet = view(48, S)
        wuq = view3(3, 2, 4 * QK)
        wukv = view(6, 512)
        gsq = [view(160, 512), view(162, 512)]
        gsq_last = [view(164 + i, 256) for i in range(NT)]
        convm = view3(176, 4, S)
        late_probs = [view(64, S), view(68, S)]
        late_probsT = [view(72, S), view(76, S)]
        zT = view3(32, KT, S)
        act = view3(128, FT, HALF)
        yT = view3(64, KT, HALF)
        convy = [[view(80 + 4 * b + 2 * g, HALF) for g in range(2)] for b in range(2)]
        gelu = [view(88 + 2 * b, HALF) for b in range(2)]
        carry = view(92, 2 * FT * 2).rearrange("p (a b) -> p a b", b=2)
        adaA = [view(kb, 2 * D) for kb in (128, 136, 144, 152, 160, 168)]
        adaB = [view(kb, ADA) for kb in (160, 166, 192, 128, 134, 140, 146, 152)]
        rowA, rowB = view(176, 2 * D)[0:2], view(64, 2 * ADA)[0:2]
        ctxT = hcT = view3(80, KT, CTX)
        ctx_sq, ctx_ssq, ctx_rstd = [view(88, CTX), view(89, CTX)], view(93, CTX), view(94, CTX)
        q2 = view3(128, 4, S)
        k2 = view(144, S)
        v2 = view3(148, NT, 128)
        vT = view(152, S)
        kc = view(160, CTX)
        vc = view3(161, 2, 128)
        rope2 = view3(162, 2, S)
        ropet2 = view(170, S)
        convu = view(192, S)
        convo = view(196, S)
        gt1o = [view(196 + 2 * b, HALF) for b in range(2)]
        att2 = view3(32, NT, 512)
        tok = [view(176, ROW), view(180.5, ROW)]
        aff = tiny[:, 0:128].rearrange("p (a b) -> p a b", a=NT)
        work = view(132, S)[0:NE]
        lgT = view(128, S)[0:NE]
        pos = view(136, S)[0:NE]
        posbf = view(140, 512)[0:NE].bitcast(BF16)
        wr = view(142, KT * NE).rearrange("p (k e) -> p k e", k=KT)
        cntj = view(144, S)
        xs = [view(96, ROW), view(100.5, ROW)]
        sgate = view(114, S)
        actx = view(118, S)
        yx = [view(148, S), view(152, S)]
        gt2B = view(156, D)
        g_fin = view(160, D)
        silu_b = view3(164, KT, P)
        fin = [view(96 + 4 * i, D) for i in range(8)]
        fsq = view(176, D)
        mod = tiny[:, 128:208].rearrange("p (a b) -> p a b", b=2)
        scT = tiny[:, 208:224].rearrange("p (k b) -> p k b", b=2)
        gsc = tiny[:, 224:248].rearrange("p (a b) -> p a b", b=8)
        sinkB = tiny[:, 248:264].rearrange("p (a b) -> p a b", b=8)
        epst = tiny[:, 264:265]
        nmax = tiny[:, 266:270]
        den = tiny[:, 270:274]
        rec = tiny[:, 278:282]
        vpad = tiny[:, 282:286]
        gss = tiny[:, 286:310].rearrange("p (a b) -> p a b", b=3)
        grs = tiny[:, 310:334].rearrange("p (a b) -> p a b", b=3)
        fbias = tiny[:, 334:335]
        top8 = tiny[:, 336:344]
        rsum = tiny[:, 344:352]
        rmx = tiny[:, 352:360]
        idxf = tiny[:, 360:376]
        idxu = tiny[:, 376:392].bitcast(U32)
        idxs = [tiny[:, 392 + b:393 + b].bitcast(U32) for b in range(2)]
        odxs = [tiny[:, 440 + b:441 + b].bitcast(U32) for b in range(2)]
        gslot = [tiny[:, 396 + b:397 + b] for b in range(2)]
        fss = tiny[:, 400:408]
        apad = tiny[:, 442:454]
        rms = [tiny[:, 420 + 8 * b:428 + 8 * b] for b in range(2)]
        gpad = tiny[:, 417:418]
        frs = tiny[:, 408:416]
        relb = view(192, 8)[0:32]
        onehot = view(193, 384)[0:32]
        extm = view(195, 384)[0:8]
        exts = view(197, 384)[0:8]

        ident = con("ident")
        identb, causalb, leftb = maskbf[:, 0, :], maskbf[:, 1, :], maskbf[:, 2, :]

        ext_d = nc.dram_tensor("bias_line", (8, 384), F32, kind="Internal")
        h_d = nc.dram_tensor("routed_rows", (S, ROW), F32, kind="Internal").ap()
        acc_d = nc.dram_tensor("residual_rows", (S, D), F32, kind="Internal").ap()

        par = sem("params_loaded")
        xld = sem("x_loaded")
        wl = [sem(f"slot{s}_loaded") for s in range(12)]
        s_ehi = sem("expert_weight_high_ready")
        s_elo = sem("expert_weight_low_ready")
        s_eu = sem("expert_weight_used")
        s_xhi = sem("columns_high_ready")
        s_thi = sem("gated_columns_high_ready")
        extra = sem("extra_loaded")
        s_bf = sem("masks_cast")
        s_sq = sem("square_done")
        s_add = sem("square_added")
        s_ssq = sem("squares_summed")
        s_stat = sem("sum_broadcast")
        s_zsq = sem("branch_square_done")
        s_zadd = sem("branch_square_added")
        s_rt = sem("root_done")
        s_dg = sem("inverse_root_on_diagonal")
        s_bc = sem("inverse_root_broadcast")
        s_rs = sem("inverse_root_ready")
        s_h = sem("normalised")
        s_hb = sem("shifted")
        s_zn = sem("branch_scaled")
        s_x = sem("residual_added")
        tps = sem("tile_half_computed")
        evv = sem("tile_evacuated_dve")
        eva = sem("tile_evacuated_act")
        vch = sem("dve_chain")
        ach = sem("act_chain")
        gch = sem("pool_chain")
        s_f = sem("forget_abs_ready")
        s_fe = sem("forget_log_ready")
        s_fd = sem("forget_sum_ready")
        s_frow = sem("forget_row_placed")
        s_aug = sem("extra_rows_set")
        s_krc = sem("rope_key_copied")
        s_sw = sem("swapped_computed")
        s_rot = sem("rotated")
        s_bl = sem("bias_line_computed")
        s_bls = sem("bias_line_ready")
        s_bld = sem("bias_line_stored")
        s_bias = sem("bias_loaded")
        s_flip = sem("bias_in_order")
        s_rope = sem("rope1_loaded")
        s_lat = sem("latent_weights_loaded")
        s_stage = sem("query_staged")
        s_S = sem("scores_done")
        s_max = sem("max_done")
        s_exp = sem("exp_done")
        s_T = sem("probs_transposed")
        s_pt = sem("probs_evacuated")
        s_pv = sem("pv_done")
        s_o = sem("head_out_done")
        s_gq = sem("group_root")
        s_gr = sem("group_inverse_ready")
        s_gn = sem("group_normalised")
        s_gna = sem("window_group_normalised")
        s_wl = [sem("stream_slot0_loaded"), sem("stream_slot1_loaded")]
        s_whi = sem("weight_high_ready")
        s_wlo = sem("weight_low_ready")
        s_wu = sem("weight_parts_used")
        s_ahi = sem("gated_high_ready")
        s_alo = sem("gated_low_ready")
        s_hhi = sem("input_part_ready")
        s_n1 = sem("first_input_normalised")
        s_nhi = sem("first_input_high_ready")
        s_ihi = sem("input_weight_high_ready")
        s_ilo = sem("input_weight_low_ready")
        s_ua = sem("conv_started")
        s_uv = sem("conv_done")
        s_gl = sem("gelu_done")
        s_act = sem("gated")
        s_silu = sem("silu_done")
        s_al = [sem(f"modulation_loaded{i}") for i in range(6)]
        s_bl2 = [sem(f"later_modulation_loaded{i}") for i in range(8)]
        s_au = sem("modulation_weights_used")
        s_ad = sem("modulation_rows_computed")
        s_row = sem("modulation_rows_ready")
        s_mod = sem("modulation_columns_computed")
        xl = [sem(f"x_loaded{i}") for i in range(4)]
        s_cl = sem("context_loaded")
        s_cx = sem("context_proj")
        s_cxe = sem("context_evacuated")
        s_rp = sem("rope2_loaded")
        s_cv = sem("conv2_done")
        s_chi = sem("conv2_high_ready")
        s_clo = sem("conv2_low_ready")
        s_x3 = sem("gated_half_added")
        s_late = sem("late_params_loaded")
        s_lgT = sem("logits_computed")
        s_lgc = sem("logits_copied")
        s_lg = sem("logits_done")
        s_rm = sem("logits_shifted")
        s_re = sem("router_exp")
        s_aff = sem("affinity_done")
        s_tkst = [sem("rows_stored0"), sem("rows_stored1")]
        s_at = sem("affinity_transposed")
        s_pos = sem("positions_done")
        s_pb = sem("positions_broadcast")
        s_cnt = sem("positions_counted")
        s_idx = sem("indices_done")
        s_sb = sem("silu_columns_ready")
        s_g2 = sem("gate2_computed")
        s_g2e = sem("gate2_ready")
        s_gat = [sem("gathered0"), sem("gathered1")]
        s_yf = sem("expert_output_free")
        s_gs = sem("expert_affinity_kept")
        s_xt = sem("rows_to_columns")
        s_xe = sem("columns_evacuated")
        s_sg = sem("silu_gate_done")
        s_ga = sem("expert_gated")
        s_at2 = sem("gated_transposed")
        s_ae = sem("gated_evacuated")
        s_ys = sem("expert_out_scaled")
        s_sc = [sem("scattered0"), sem("scattered1")]
        s_fl = [sem(f"final_loaded{i}") for i in range(8)]
        s_frt = sem("final_root")
        s_fo = sem("final_ready")
        s_out = sem("stored")

        block = ctx.enter_context(nc.Block())

        NPAR = 8
        NORM_K = [8, 2, 1, 8, 8, 8, 8, 8, 8, 8]
        NORM_N = [S, S, S, S, S, HALF, CTX, HALF, S, S]
        NORM_PS = [6, 6, 6, 6, 6, 6, 5, 6, 6, 6]
        NORM_AT = [(sq, ssq, rstdB)] + [(lat_sq, lat_ssq, lat_rstd)] * 2 + [(sq, ssq, rstdB)] * 3 + [(ctx_sq, ctx_ssq, ctx_rstd)] + [(sq, ssq, rstdB)] * 2 + [(late_probs, late_probsT[0], late_probsT[1])]

        class Chain:
            def __init__(self, eng, s):
                self.eng, self.s, self.base, self.k = eng, s, 0, 0

            def mark(self, ins):
                ins.then_inc(self.s, 1)
                self.k += 1

            def need(self):
                self.eng.wait_ge(self.s, self.base + self.k)

            def link(self, ins):
                self.mark(ins)
                self.need()

            def enter(self, it, per):
                self.static, self.per = self.base + self.k, per
                self.base, self.k = it * per + self.static, 0

            def leave(self, n):
                assert self.k == self.per, (self.k, self.per)
                self.base, self.k = self.static + n * self.per, 0

        PH = ["w_in", "gate2", "expert"]
        USE = {"w_in": [4, 3, 0, 0], "gate2": [1, 1, 1, 1], "expert": [NE] * 12}

        def loads_before(ph, s):
            return sum(USE[p][s] if s < len(USE[p]) else 0 for p in PH[:PH.index(ph)])

        U_SWA, U_DENSE, U_ATT2, U_END = 0, 64, 128, 192
        T_V, T_IN, T_UQ, T_UKV, T_LV, T_MT, T_OUT, T_DN = 0, 4, 17, 21, 25, 29, 37, 45
        T_VT, T_K2, T_V2, T_IN2, T_AT, T_OUT2, T_XR, T_HR = 53, 54, 55, 55, 72, 76, 84, 92

        G_OUT, G_UP, G_DN, G_IN2, G_OUT2 = 0, (4, 37), (26, 59), 70, 79
        W_UP, W_DN = (0, 2 * FT + FT - 1), (2 * FT, 4 * FT + FT - 1)

        def in2_used(n):
            return tps, 2 * (T_K2 + 1 if n < 2 else T_IN2 + n)

        def parts_used(ph, half, g, q):
            if ph == "out":
                return tps, 4 * g + (2 * (T_OUT + q) + 2)
            if ph == "down" and isinstance(g, int) and g == FT // 2 - 1 and q == 1:
                return tps, 2 * (T_DN + 4 * half) + 8
            return s_wu, 2 * g + ((W_UP if ph == "up" else W_DN)[half] + q + 1)

        def expert_item(e, i):
            return PARTS * e + (KT + i)

        def expert_items(e, last):
            turn = [(1, e), (2, e)] if last else [(1, e), (0, e + 1), (2, e)]
            return [(j * KT + k, 4 * n + k // 2, k % 2, ee) for j, (n, ee) in enumerate(turn) for k in range(KT)]

        @block.sync
        def _(sp):
            sp.dma_start(cols[:], T["cols"]).then_inc(par, 16)
            sp.dma_start(const[:], T["const"]).then_inc(par, 16)
            sp.dma_start(fbias[0:4], T["forget_bias"].rearrange("a (h o) -> (a h) o", o=1)).then_inc(par, 16)
            sp.dma_start(sinkB[:, 0, :], T["swa_sinks"].to_broadcast([P, 8])).then_inc(par, 16)
            sp.dma_start(sinkB[:, 1, :], T["sink_2"].to_broadcast([P, 8])).then_inc(par, 16)
            sp.dma_start(relb, T["rel_bias"]).then_inc(par, 16)
            sp.dma_start(onehot, T["onehot"]).then_inc(par, 16)
            sp.dma_start(extm, T["extmask"]).then_inc(par, 16)
            for i in range(4):
                sp.dma_start(xT[:, 2 * i:2 * i + 2, :], T["xT"][:, 2 * i:2 * i + 2, :]).then_inc(xl[i], 16)
            ada = T["w_ada_2"].rearrange("l (k p) n -> (l k) p n", p=P)
            for k in range(6):
                sp.dma_start(adaA[k], ada[k, :, 0:2 * D]).then_inc(s_al[k], 16)
            sp.dma_start(wv, T["w_in_v"]).then_inc(extra, 16)

            for i in range(7):
                if i == 2:
                    for k in range(6, KT):
                        sp.wait_ge(s_au, k - 5)
                        sp.dma_start(adaA[k - 6], ada[k, :, 0:2 * D]).then_inc(s_al[k - 6], 16)
                    sp.wait_ge(s_bls, 1)
                    sp.dma_start(ext_d.ap(), exts).then_inc(s_bld, 16)
                    sp.wait_ge(s_bld, 16)
                    sp.wait_ge(s_h, KT)
                    sp.dma_start(mflip, bass.AP(ext_d, 0, [[1, P], [384, 8], [1, 256]])).then_inc(s_bias, 16)
                    sp.dma_start(rope1[64:96], T["rope1"]).then_inc(s_rope, 16)
                if i >= 2:
                    sp.wait_ge(s_ilo, 1 + 2 * (i - 1))
                n = ITEM if i < 6 else KT * QK
                sp.dma_start(slot[i % 2][:, 0:n], T["w_in"][:, i * ITEM:i * ITEM + n]).then_inc(wl[i % 2], 16)
            sp.dma_start(wuq, T["w_uq"]).then_inc(s_lat, 16)
            sp.dma_start(wukv, T["w_ukv"]).then_inc(s_lat, 16)
            sp.wait_ge(s_fd, 1)
            sp.wait_ge(s_aug, 2)
            sp.dma_start(KH[64:65, 0:4, :], flog[0:4, :]).then_inc(s_frow, 16)
            sp.wait_ge(s_frow, 16)
            sp.wait_ge(tps, 2 * T_MT)

            def stream(g0, n, src):
                if g0 < 2:
                    for g in range(2):
                        sp.dma_start(slot[g], src[:, g, :]).then_inc(s_wl[g], 16)
                    stream(g0 + 2, n - 2, src[:, 2:, :])
                    return
                two = src[:, 0:n // 2 * 2, :].rearrange("p (m c) n -> p m c n", c=2)
                with sp.Fori(0, n // 2) as m:
                    for c in range(2):
                        sp.wait_ge(s_wlo, 4 * m + 2 * (g0 + c) - 2)
                        sp.dma_start(slot[(g0 + c) % 2], two[:, m, c, :]).then_inc(s_wl[(g0 + c) % 2], 16)
                if n % 2:
                    sp.wait_ge(s_wlo, 2 * (g0 + n - 1) - 2)
                    sp.dma_start(slot[(g0 + n - 1) % 2], src[:, n - 1, :]).then_inc(s_wl[(g0 + n - 1) % 2], 16)

            stream(G_OUT, KT // 2, T["w_out"].rearrange("p (g n) -> p g n", n=ITEM))
            sp.wait_ge(s_S, U_ATT2)
            sp.dma_start(xT, T["xT"]).then_inc(xld, 16)
            up0 = T["w_up"].rearrange("p (g n) -> p g n", n=ITEM)
            for g in range(2):
                sp.wait_ge(s_wlo, 2 * (G_UP[0] + g) - 2)
                sp.dma_start(slot[g], up0[:, g, :]).then_inc(s_wl[g], 16)
            for g in range(2):
                for k in range(KT):
                    if g == 0 and k == 3:
                        sp.wait_ge(tps, 2 * T_DN)
                    if g:
                        sp.wait_ge(s_au, KT - 1 + k + 1) if k < KT - 1 else sp.wait_ge(s_ad, 2)
                    sp.dma_start(adaB[k], ada[k, :, 2 * D + g * ADA:2 * D + (g + 1) * ADA]).then_inc(s_bl2[k], 16)
            for half in range(2):
                if half:
                    stream(G_UP[1], FT, up0)
                else:
                    stream(G_UP[0] + 2, FT - 2, up0[:, 2:, :])
                stream(G_DN[half], FT // 2, T["w_down"].rearrange("p (g n) -> p g n", n=ITEM))
            sp.wait_ge(s_act, 2 * FT + 1)
            sp.dma_start(ctxT, T["ctxT"]).then_inc(s_cl, 16)
            in2 = T["w_in2"].rearrange("p (g n) -> p g n", n=ITEM)
            for g in range(9):
                sp.wait_ge(s_wlo, 2 * (G_IN2 + g) - 2)
                if g == 2:
                    sp.wait_ge(s_cx, 1)
                    sp.dma_start(rope2, T["rope2"]).then_inc(s_rp, 16)
                sp.dma_start(slot[g % 2], in2[:, g, :]).then_inc(s_wl[g % 2], 16)
            out2 = T["w_out2"].rearrange("p (g n) -> p g n", n=ITEM)
            for g in range(KT // 2):
                sp.wait_ge(s_wlo, 2 * (G_OUT2 + g) - 2)
                sp.dma_start(slot[(G_OUT2 + g) % 2], out2[:, g, :]).then_inc(s_wl[(G_OUT2 + g) % 2], 16)
            wga = T["w_ada_2"].rearrange("l (k a p) n -> l k p a n", a=2, p=P)[0]
            sp.wait_ge(tps, 2 * (T_OUT2 + 8))
            for i in range(4):
                sp.dma_start(slot[i].rearrange("p (a n) -> p a n", a=2), wga[i][:, :, 5 * D:6 * D]).then_inc(wl[i], 16)
            sp.wait_ge(evv, T_OUT2 + 8)
            sp.dma_start(gt2B, T["b_ada_2"][:, 5 * D:6 * D].to_broadcast([P, D])).then_inc(s_late, 16)
            sp.dma_start(g_fin, T["g_final_2"].rearrange("(a d) -> a d", a=1).to_broadcast([P, D])).then_inc(s_late, 16)
            sp.dma_start(wr, T["w_router_2"][0].rearrange("(k p) e -> p k e", p=P)).then_inc(s_late, 16)
            for i in range(2 * NT):
                sp.wait_ge(eva, T_XR + i + 1)
                dst, n, t = (acc_d, D, i) if i < NT else (h_d, ROW, i - NT)
                sp.dma_start(dst[t * P:(t + 1) * P, :], tok[i % 2][:, 0:n]).then_inc(s_tkst[i % 2], 16)
            wx = [T[n].rearrange("l e (j a p) n -> (l e) j p a n", a=2, p=P) for n in ("w_gate_2", "w_up_2", "w_down_2")]
            sp.wait_ge(tps, 2 * (T_HR + 8))
            sp.wait_ge(s_g2, 1)
            def expert_weights(n, e, used=None):
                for j in range(4):
                    if used is not None:
                        sp.wait_ge(s_elo, used + (2 * j + 2))
                    src = wx[n][e, j] if isinstance(e, int) else wx[n][bass.ds(e, 1), j].rearrange("o p a n -> p (o a) n")
                    sp.dma_start(slot[4 * n + j].rearrange("p (a n) -> p a n", a=2), src).then_inc(wl[4 * n + j], 16)
            for n in range(3):
                expert_weights(n, 0)
            expert_weights(0, 1, 0)
            with sp.Fori(0, NE - 2) as e:
                expert_weights(1, e + 1, expert_item(e, 0))
                expert_weights(0, e + 2, expert_item(e, KT))
                expert_weights(2, e + 1, expert_item(e, 2 * KT))
            for n in (1, 2):
                expert_weights(n, NE - 1, expert_item(NE - 2, (n - 1) * 2 * KT))
            for b in range(2):
                sp.wait_ge(s_sc[b], 16 * NE // 2)
            for i in range(NT):
                sp.dma_start(fin[i], acc_d[i * P:(i + 1) * P, :]).then_inc(s_fl[i], 16)
            for i in range(NT):
                sp.wait_ge(s_fo, i + 1)
                sp.dma_start(T["out"][0, i * P:(i + 1) * P, :], fin[i]).then_inc(s_out, 16)
            sp.wait_ge(s_out, 16 * NT)

        @block.tensor
        def _(pe):
            def keep_clock(n):
                for _ in range(n):
                    pe.matmul(ps[:, 7, :], con("mean"), const[:, 0:512], start=True, stop=True)

            def mean(i):
                pe.wait_ge(s_ssq, i + 1)
                for t in range(NORM_N[i] // P):
                    m = pe.matmul(ps[:, NORM_PS[i], t:t + 1], NORM_AT[i][1][:, t * P:(t + 1) * P], con("mean")[:, 0:1], start=True, stop=True)
                m.then_inc(s_stat, 1)

            def spread(i):
                pe.wait_ge(s_dg, i + 1)
                for t in range(NORM_N[i] // P):
                    m = pe.matmul(ps[:, NORM_PS[i] + t // 4, (t % 4) * P:(t % 4 + 1) * P], con("mean"), NORM_AT[i][0][0][:, t * P:(t + 1) * P], start=True, stop=True)
                m.then_inc(s_bc, 1)

            def stat(i):
                mean(i)
                spread(i)

            def tile_free(t, h):
                if not isinstance(t, int) or t >= 2:
                    pe.wait_ge(evv if h == 0 else eva, t - 1)

            def tile(t, b, lhs, rhs, nk, m=P, n=512):
                for h in range(2):
                    tile_free(t, h)
                    for k in range(nk):
                        i = pe.matmul(ps[0:m, 2 * b + h, 0:n], lhs(k, h), rhs(k, h), start=(k == 0), stop=(k == nk - 1))
                    i.then_inc(tps, 1)

            def turn(t, src, n=2):
                for h in range(2):
                    pe.wait_ge(evv if h == 0 else eva, t - n + 1)
                    for j in range(4):
                        i = pe.transpose(ps[:, 2 * (t % n) + h, j * P:(j + 1) * P], src(h, j), ident)
                    i.then_inc(tps, 1)

            def loaded(ph, s, j):
                pe.wait_ge(wl[s], j * 16 + 16 * (loads_before(ph, s) + 1))

            def wtile(s, a):
                return lambda k, h: slot[s][:, (a * KT + k) * P:(a * KT + k + 1) * P]

            def tokens(src):
                return lambda k, h: src[:, k, h * HALF:(h + 1) * HALF]

            def units(g, now, before=None, probs=probs, probsT=probsT):
                def after(s, v, u, least):
                    if not isinstance(g, int) or g + u >= least:
                        pe.wait_ge(s, g + (u + v))

                def group(w):
                    return now if w >= 0 else before
                for u in range(8 if now else 2):
                    if now:
                        after(s_exp, -1, u, 2)
                        now[0](u).then_inc(s_S, 1)
                    w = u - 1
                    if (now or u == 0) and group(w):
                        pe.wait_ge(s_exp, g + (w + 1))
                        after(s_pt, 0, w, 1)
                        for j in range(group(w)[1](w % 8) // P):
                            i = pe.transpose(ps[:, 4 + j // 4, (j % 4) * P:(j % 4 + 1) * P], probs[w % 2][:, j * P:(j + 1) * P], ident)
                        i.then_inc(s_T, 1)
                    w = u - 2
                    if group(w):
                        pe.wait_ge(s_pt, g + (w + 1))
                        after(s_o, -1, w, 2)
                        nb = group(w)[1](w % 8) // P
                        for j in range(nb):
                            i = pe.matmul(ps[:, 6 + w % 2, 0:HD], probsT[w % 2][:, j * P:(j + 1) * P], group(w)[2](w % 8, j),
                                          start=(j == 0), stop=(j == nb - 1))
                        i.then_inc(s_pv, 1)

            pe.wait_ge(par, 16 * NPAR)
            pe.matmul(ps[0:8, 4, 0:384], relb, onehot, start=True, stop=True).then_inc(s_bl, 1)

            def modulation(k, w, load, b, n):
                pe.wait_ge(*load)
                for c in range(n):
                    m = pe.matmul(ps[0:2, b + c, :], scT[:, k, :], w[:, c * 512:(c + 1) * 512], start=(k == 0), stop=(k == KT - 1))
                return m

            def columns(row, n, rows):
                pe.wait_ge(s_row, rows)
                for t in range(n):
                    m = pe.transpose(ps[:, 4, 2 * t:2 * t + 2], row[:, t * P:(t + 1) * P], ident[0:2, 0:2])
                m.then_inc(s_mod, 1)

            stat(0)
            pe.wait_ge(s_silu, 1)
            for k in range(KT):
                modulation(k, adaA[k % 6], (s_al[k % 6], 16 * (k // 6 + 1)), 0, 4).then_inc(s_au if k < KT - 1 else s_ad, 1)
            pe.wait_ge(s_row, 1)
            pe.wait_ge(s_h, 8)
            pe.wait_ge(extra, 16)
            pe.wait_ge(s_bias, 16)
            for c in range(4):
                m = pe.matmul(ps[:, 4 + c, :], con("flip"), mflip.rearrange("p a b -> p (a b)")[:, c * 512:(c + 1) * 512], start=True, stop=True)
            m.then_inc(s_flip, 1)
            pe.wait_ge(s_ilo, 1)
            for t in range(4):
                for h in range(2):
                    tile_free(T_V + t, h)
                    out, rows = ps[:, 2 * (t % 2) + h, 0:384], slice((2 * t + h) * P, (2 * t + h + 1) * P)
                    for k in range(KT):
                        pe.matmul(out, n_hi[:, k, rows], v_hi[:, k, :], start=(k == 0), stop=False)
                        pe.matmul(out, n_hi[:, k, rows], v_lo[:, k, :], start=False, stop=False)
                        m = pe.matmul(out, n_lo[k][:, rows], v_hi[:, k, :], start=False, stop=(k == KT - 1))
                    m.then_inc(tps, 1)
            pe.wait_ge(evv, T_IN)
            columns(rowA, 2 * KT, 1)
            for t in range(13):
                w = P if t < 12 else QK
                pe.wait_ge(s_ilo, 1 + t + 1)
                for h in range(2):
                    tile_free(T_IN + t, h)
                    out, hs = ps[0:w, 2 * ((T_IN + t) % 2) + h, :], slice(h * HALF, (h + 1) * HALF)
                    for k in range(KT):
                        part = slice(k * w, (k + 1) * w)
                        pe.matmul(out, w_hi[:, t % 2, part], n_hi[:, k, hs], start=(k == 0), stop=False)
                        pe.matmul(out, w_hi[:, t % 2, part], n_lo[k][:, hs], start=False, stop=False)
                        m = pe.matmul(out, w_lo[:, t % 2, part], n_hi[:, k, hs], start=False, stop=(k == KT - 1))
                    m.then_inc(tps, 1)
                if t in (3, 5):
                    mean(1 if t == 3 else 2)
                if t in (4, 6):
                    spread(1 if t == 4 else 2)

            def swapped(i, src):
                if i:
                    pe.wait_ge(s_rot, i)
                for h in range(2):
                    m = pe.matmul(ps[0:QK, 4 + h, :], con("swap16")[64:96], src[64:96, h * HALF:(h + 1) * HALF], start=True, stop=True)
                m.then_inc(s_sw, 1)

            def swap_query(h):
                pe.wait_ge(evv, T_UQ + h + 1)
                pe.wait_ge(eva, T_UQ + h + 1)
                swapped(1 + h, QH[:, 4 + h, :])

            pe.wait_ge(eva, T_UQ)
            pe.wait_ge(evv, T_UQ)
            pe.wait_ge(s_bls, 1)
            swapped(0, krope)
            pe.wait_ge(s_lat, 32)
            pe.wait_ge(s_h, 8 + 2 + 1)
            for h in range(4):
                tile(T_UQ + h, (T_UQ + h) % 2, lambda k, hf: wuq[:, k, h * QK:(h + 1) * QK], tokens(cq), 2, QK)
                if h:
                    swap_query(h - 1)
            for h in range(4):
                tile(T_UKV + h, (T_UKV + h) % 2, lambda k, hf: wukv[:, h * P:h * P + HD],
                     lambda k, hf: ckv[:, hf * HALF:(hf + 1) * HALF], 1, HD)
                if h == 0:
                    swap_query(3)
            wuv = wukv.rearrange("p (h c) -> p h c", c=P)[:, :, HD:P]
            for t in range(4):
                tile(T_LV + t, (T_LV + t) % 2, lambda k, h: ckv[:, (2 * t + h) * P:(2 * t + h + 1) * P], lambda k, h: wuv, 1, P, 256)

            keep_clock(6)
            pe.wait_ge(evv, T_MT)
            pe.wait_ge(eva, T_MT)
            pe.wait_ge(s_rot, 5)
            pe.wait_ge(s_krc, 1)
            pe.wait_ge(s_frow, 16)

            def sink(u, layer, b, at):
                return pe.matmul(ps[:, b, at:at + 1], con("mean")[0:1, :], sinkB[0:1, layer, u // 2 + 4 * (u % 2):u // 2 + 4 * (u % 2) + 1], start=True, stop=True)

            def swa(n, par):
                nk = P if isinstance(n, int) and n == 0 else 2 * P

                def scores(u):
                    r = HD * (u % 2)
                    if u == 0:
                        pe.wait_ge(s_stage, n + 1)
                    pe.matmul(ps[:, 2 * (u % 2), 0:nk], qs[par][r:r + HD, u // 2, :], ks[par][r:r + HD, 0:nk], start=True, stop=False)
                    pe.matmul(ps[:, 2 * (u % 2), 0:nk], ident, swab[:, u // 2 + 4 * (u % 2), 256 - nk:256], start=False, stop=True)
                    return sink(u, 0, 2 * (u % 2), nk)

                def values(u, j):
                    c = HD * (u % 2)
                    if nk == P:
                        return swav[:, 0, c:c + HD]
                    return swav[:, bass.ds(n + (j - 1), 1), c:c + HD].rearrange("p a c -> p (a c)")
                return scores, lambda u: nk, values

            def dense(h, par):
                def scores(u):
                    if u == 0:
                        pe.wait_ge(s_stage, h + (NT + 1))
                    n = (u + 1) * P
                    for c in range((n + 511) // 512):
                        m = min(512, n - c * 512)
                        pe.matmul(ps[:, 2 * (u % 2) + c, 0:m], qh[par][0:QK, u * P:(u + 1) * P],
                                  KH[0:QK, bass.ds(h, 1), c * 512:c * 512 + m].rearrange("p a c -> p (a c)"), start=True, stop=(c * 512 + m < n))
                    return pe.matmul(ps[:, 2 * (u % 2) + u // 4, (u % 4) * P:(u % 4 + 1) * P], identb, causalb, start=False, stop=True)

                def values(u, j):
                    return VH[:, j, bass.ds(h * HD, HD)]
                return scores, lambda u: (u + 1) * P, values

            units(U_SWA, swa(0, 0))
            units(8, swa(1, 1), swa(0, 0))
            with pe.Fori(1, NT // 2) as m:
                for b in range(2):
                    units(m * 16 + 8 * b, swa(2 * m + b, b), swa(2 * m + (b - 1), 1 - b))
            units(U_DENSE, dense(0, 0), swa(NT - 1, 1))
            with pe.Fori(0, CH // 2 - 1) as m:
                for b in range(2):
                    units(m * 16 + (U_DENSE + 8 * (b + 1)), dense(2 * m + (b + 1), 1 - b), dense(2 * m + b, b))
            units(U_ATT2 - 8, dense(CH - 1, 1), dense(CH - 2, 0))
            units(U_ATT2, None, dense(CH - 1, 1))

            pe.wait_ge(s_gn, 8)
            pe.wait_ge(s_gna, 8)
            for k in range(KT):
                turn(T_MT + k, lambda h, j: mixed[:, 4 * h + j, k * P:(k + 1) * P], 4)
            pe.wait_ge(evv, T_OUT)
            pe.wait_ge(eva, T_OUT)
            def passes(out, q, t, hi, lo, start, stop):
                w = slice(t * P, (t + 1) * P)
                pe.matmul(out, w_hi[:, q, w], hi, start=start, stop=False)
                pe.matmul(out, w_hi[:, q, w], lo, start=False, stop=False)
                return pe.matmul(out, w_lo[:, q, w], hi, start=False, stop=stop)

            with pe.Fori(0, 2) as m:
                for c in range(2):
                    for q in range(2):
                        g = 2 * m + c
                        pe.wait_ge(s_wlo, 2 * g + (2 * G_OUT + q + 1))
                        for h in range(2):
                            tile_free(4 * m + (T_OUT + 2 * c + q), h)
                            for k in range(KT):
                                i = passes(ps[:, 2 * ((T_OUT + q) % 2) + h, :], q, k, m_hi[:, k, h * HALF:(h + 1) * HALF], m_lo[:, k, h * HALF:(h + 1) * HALF],
                                           k == 0, k == KT - 1)
                            i.then_inc(tps, 1)
            def parts(g, ks):
                for k in ks:
                    modulation(k, adaB[k], (s_bl2[k], 16 * (g + 1)), 3 * g, 3).then_inc(s_au if k < KT - 1 else s_ad, 1)
            pe.wait_ge(evv, T_DN)
            pe.wait_ge(eva, T_DN)
            mean(3)
            parts(0, range(2))
            spread(3)
            parts(0, range(2, KT))
            mean(4)
            parts(1, range(2))
            spread(4)
            parts(1, range(2, KT))
            pe.wait_ge(s_row, 2)

            def up(half, g, b):
                for q in range(2):
                    pe.wait_ge(s_wlo, 2 * g + (2 * G_UP[half] + q + 1))
                    if q == 0:
                        pe.wait_ge(s_uv, g + (half * FT + 1))
                    for k in range(KT):
                        i = passes(ps[:, 2 * b + q, :], q, k, h_hi[:, k, :], h_lo[:, k, :], k == 0, k == KT - 1)
                    i.then_inc(s_wu, 1)

            def down(half, g, q, last=False):
                pe.wait_ge(s_wlo, 2 * g + (2 * G_DN[half] + q + 1))
                pe.wait_ge(s_alo, 2 * g + (half * FT + q + 1))
                for t in range(KT):
                    i = passes(ps[:, t, :], q, t, a_hi[:, q, :], a_lo[:, q, :], False, last)
                    if last:
                        i.then_inc(tps, 1)
                if not last:
                    i.then_inc(s_wu, 1)

            def first_down(half):
                for ts in (range(4, KT), range(4)):
                    for q in range(2):
                        if ts[0]:
                            pe.wait_ge(s_wlo, 2 * G_DN[half] + q + 1)
                            pe.wait_ge(s_alo, half * FT + q + 1)
                        elif q == 0:
                            pe.wait_ge(s_uv, half * FT + FT + 2)
                        for t in ts:
                            i = passes(ps[:, t, :], q, t, a_hi[:, q, :], a_lo[:, q, :], q == 0, False)
                        if ts[0] == 0:
                            i.then_inc(s_wu, 1)

            for half in range(2):
                pe.wait_ge(s_h, 8 + 2 + 1 + 8 + 8 * half)
                pe.wait_ge(evv, T_DN + 4 * half)
                pe.wait_ge(eva, T_DN + 4 * half)
                up(half, 0, 0)
                if half:
                    mean(5)
                else:
                    columns(rowB, 3 * KT, 3)
                up(half, 1, 1)
                if half:
                    spread(5)
                with pe.Fori(1, FT // 2) as j:
                    for b in range(2):
                        up(half, 2 * j + b, b)
                first_down(half)
                with pe.Fori(1, FT // 2 - 1) as g:
                    for q in range(2):
                        down(half, g, q)
                down(half, FT // 2 - 1, 0)
                down(half, FT // 2 - 1, 1, last=True)
            pe.wait_ge(evv, T_VT)
            pe.wait_ge(eva, T_VT)
            mean(6)
            mean(7)
            spread(6)
            spread(7)
            pe.wait_ge(s_wl[0], 8 * G_IN2 + 16)
            pe.wait_ge(s_hb, KT)
            for k in range(KT):
                pe.matmul(ps[:, 4, 0:CTX], wtile(0, 0)(k, 0), hcT[:, k, :], start=(k == 0), stop=(k == KT - 1))
            for t in range(2):
                for k in range(KT):
                    i = pe.matmul(ps[:, 5, t * P:(t + 1) * P], hcT[:, k, t * P:(t + 1) * P], wtile(0, 1)(k, 0), start=(k == 0), stop=(k == KT - 1))
            i.then_inc(s_cx, 1)
            stat(8)

            def swapped2(i, src):
                pe.wait_ge(s_rot, 5 + i)
                for h in range(2):
                    m = pe.matmul(ps[:, 4 + h, :], con("swap32"), src[:, h * HALF:(h + 1) * HALF], start=True, stop=True)
                m.then_inc(s_sw, 1)

            def input_tile(t, n):
                pe.wait_ge(s_wlo, 2 * G_IN2 + n + 1)
                for h in range(2):
                    tile_free(t, h)
                    hs = slice(h * HALF, (h + 1) * HALF)
                    for k in range(KT):
                        i = passes(ps[:, 2 * (t % 2) + h, :], n % 2, k, g_hi[:, k, hs], g_lo[:, k, hs], k == 0, k == KT - 1)
                    i.then_inc(tps, 1)

            pe.wait_ge(s_cxe, 2)
            pe.wait_ge(s_wlo, 2 * G_IN2 + 2)
            for h in range(2):
                pe.wait_ge(s_hhi, (3 + h) * KT)
                hs = slice(h * HALF, (h + 1) * HALF)
                for t, n in ((T_VT, 1), (T_K2, 0)):
                    for k in range(KT):
                        i = passes(ps[:, 2 * (t % 2) + h, :], n, k, g_hi[:, k, hs], g_lo[:, k, hs], k == 0, k == KT - 1)
                    i.then_inc(tps, 1)
            turn(T_V2, lambda h, j: vT[:, h * HALF + j * P:h * HALF + (j + 1) * P])
            pe.wait_ge(evv, T_K2 + 1)
            pe.wait_ge(eva, T_K2 + 1)
            swapped2(0, k2)
            for t in range(1, 17):
                input_tile(T_IN2 + t, t + 1)
                if 2 <= t <= 5:
                    pe.wait_ge(evv, T_IN2 + t)
                    pe.wait_ge(eva, T_IN2 + t)
                    swapped2(t - 1, q2[:, t - 2, :])
            keep_clock(6)
            pe.wait_ge(s_rot, 10)
            pe.wait_ge(s_cv, 4)

            def att(n, lo, hi, it, par):
                nl = (hi - lo + 1) * P
                at = 512 - nl

                def scores(u):
                    r, b = HD * (u % 2), 2 * (u % 2)
                    if u == 0:
                        pe.wait_ge(s_stage, it + (NT + CH + 1))
                    pe.matmul(ps[:, b, at:512], qs[par][r:r + HD, u // 2, :], ks[par][r:r + HD, 0:nl], start=True, stop=False)
                    if lo < 0:
                        pe.matmul(ps[:, b, at:at + P], identb, leftb, start=False, stop=(hi < 1))
                    if hi > 0:
                        pe.matmul(ps[:, b, 512 - P:512], identb, causalb, start=False, stop=True)
                    pe.matmul(ps[:, b + 1, 0:CTX], qs[par][r:r + HD, u // 2, :], kc[r:r + HD, :], start=True, stop=True)
                    return sink(u, 1, b + 1, CTX)

                def values(u, j):
                    c = HD * (u % 2)
                    if j >= nl // P:
                        return vc[:, j - nl // P, c:c + HD]
                    return v2[:, n + (lo + j), c:c + HD]
                return scores, lambda u: nl + CTX, values

            def units2(g, now, before=None):
                units(g, now, before, late_probs, late_probsT)
            units2(U_ATT2, att(0, 0, 1, 0, 0))
            units2(U_ATT2 + 8, att(1, -1, 1, 1, 1), att(0, 0, 1, 0, 0))
            with pe.Fori(1, NT // 2 - 1) as m:
                for b in range(2):
                    n = 2 * m + b
                    units2(m * 16 + (U_ATT2 + 8 * b), att(n, -1, 1, n, b), att(n - 1, -1, 1, n - 1, 1 - b))
            units2(U_END - 16, att(NT - 2, -1, 1, NT - 2, 0), att(NT - 3, -1, 1, NT - 3, 1))
            units2(U_END - 8, att(NT - 1, -1, 0, NT - 1, 1), att(NT - 2, -1, 1, NT - 2, 0))
            units2(U_END, None, att(NT - 1, -1, 0, NT - 1, 1))
            pe.wait_ge(s_o, U_END)
            for k in range(4):
                turn(T_AT + k, lambda h, j: att2[:, 4 * h + j, k * P:(k + 1) * P], 4)
            pe.wait_ge(evv, T_OUT2)
            pe.wait_ge(eva, T_OUT2)
            pe.wait_ge(s_clo, 4)
            with pe.Fori(0, 4) as j:
                for b in range(2):
                    pe.wait_ge(s_wlo, 2 * j + (2 * G_OUT2 + b + 1))
                    for h in range(2):
                        tile_free(2 * j + (T_OUT2 + b), h)
                        for k in range(KT):
                            hi, lo = (o_hi, o_lo) if k < 4 else (c_hi, c_lo)
                            hs = slice(h * HALF, (h + 1) * HALF)
                            i = passes(ps[:, 2 * ((T_OUT2 + b) % 2) + h, :], b, k, hi[:, k % 4, hs], lo[:, k % 4, hs], k == 0, k == KT - 1)
                        i.then_inc(tps, 1)
            stat(9)
            pe.wait_ge(s_late, 48)
            for k in range(KT):
                pe.wait_ge(s_hb, 3 * KT + k + 1)
                for c in range(2):
                    m = pe.matmul(ps[0:NE, c, :], wr[:, k, :], hT[:, k, c * HALF:(c + 1) * HALF], start=(k == 0), stop=(k == KT - 1))
            m.then_inc(s_lgT, 1)
            pe.wait_ge(s_lgc, 1)
            for i in range(NT):
                m = pe.transpose(ps[:, 4, i * NE:(i + 1) * NE], lgT[:, i * P:(i + 1) * P], ident[0:NE, 0:NE])
            m.then_inc(s_lg, 1)
            pe.wait_ge(s_aff, 1)
            for i in range(NT):
                m = pe.transpose(ps[0:NE, 5 + i // 4, (i % 4) * P:(i % 4 + 1) * P], aff[:, i, :], ident)
            m.then_inc(s_at, 1)
            for i in range(2 * NT):
                src, t, g = (xT, i, T_XR + i) if i < NT else (hT, i - NT, T_XR + i)
                pe.wait_ge(eva, g - 1)
                for k in range(KT):
                    m = pe.transpose(ps[:, 2 * (g % 2) + k // 4, (k % 4) * P:(k % 4 + 1) * P], src[:, k, t * P:(t + 1) * P], ident)
                    if k % 4 == 3:
                        m.then_inc(tps, 1)
            pe.wait_ge(s_sb, 1)
            pe.wait_ge(eva, T_HR + 8)
            for k in range(KT):
                if k % 2 == 0:
                    loaded("gate2", k // 2, 0)
                for c in range(2):
                    m = pe.matmul(ps[:, 2 + c, :], silu_b[:, k, :], slot[k // 2][:, (k % 2) * D + c * 512:(k % 2) * D + (c + 1) * 512],
                                  start=(k == 0), stop=(k == KT - 1))
            m.then_inc(s_g2, 1)
            pe.wait_ge(s_pos, 1)
            for e in range(NE):
                if e >= 2:
                    pe.wait_ge(s_cnt, e - 1)
                for c in range(2):
                    b = 4 + 2 * (e % 2) + c
                    m = pe.matmul(ps[:, b, :], identb[0:NE, e:e + 1].to_broadcast([NE, P]), posbf[:, c * 512:(c + 1) * 512], start=True, stop=True)
                m.then_inc(s_pb, 1)
            pe.wait_ge(s_cnt, NE)
            pe.wait_ge(s_g2e, 1)
            def item(n, k, hi, lo, bank):
                r = k % RING
                pe.wait_ge(s_elo, n + 1)
                for c in range(2):
                    w, out = slice(c * 512, (c + 1) * 512), ps[:, bank + c, :]
                    pe.matmul(out, hi[:, k, :], e_hi[:, r, w], start=(k == 0), stop=False)
                    pe.matmul(out, lo[:, k, :], e_hi[:, r, w], start=False, stop=False)
                    m = pe.matmul(out, hi[:, k, :], e_lo[:, r, w], start=False, stop=(k == KT - 1))
                m.then_inc(s_eu, 1)

            def turn_rows(e, b):
                pe.wait_ge(s_gat[b], 8 * e + (16 - 8 * b))
                for k in range(KT):
                    m = pe.transpose(ps[:, 4 + k // 4, (k % 4) * P:(k % 4 + 1) * P], xs[b][:, k * P:(k + 1) * P], ident)
                m.then_inc(s_xt, 1)

            def gate(n, b, ks):
                for k in ks:
                    item(n + k, k, x_hi[:, b], x_lo[:, b], 0)

            def expert(e, b, last=False):
                if not last:
                    turn_rows(e + 1, 1 - b)
                for k in range(KT):
                    item(expert_item(e, k), k, x_hi[:, b], x_lo[:, b], 2)
                if not last:
                    pe.wait_ge(s_xe, e + 2)
                    pe.wait_ge(s_sg, e + 1)
                    gate(expert_item(e, KT), 1 - b, range(4))
                pe.wait_ge(s_ga, e + 1)
                for k in range(KT):
                    m = pe.transpose(ps[:, 4 + k // 4, (k % 4) * P:(k % 4 + 1) * P], actx[:, k * P:(k + 1) * P], ident)
                m.then_inc(s_at2, 1)
                if not last:
                    gate(expert_item(e, KT), 1 - b, range(4, KT))
                pe.wait_ge(s_ae, e + 1)
                pe.wait_ge(s_ys, e + 1)
                for k in range(KT):
                    item(expert_item(e, (1 if last else 2) * KT + k), k, t_hi, t_lo, 6)

            turn_rows(0, 0)
            pe.wait_ge(s_xe, 1)
            gate(0, 0, range(KT))
            expert(0, 0)
            with pe.Fori(0, NE // 2 - 1) as q:
                for b in range(2):
                    expert(2 * q + (1 + b), 1 - b)
            expert(NE - 1, 1, last=True)

        @block.scalar
        def _(act_e):
            ac = Chain(act_e, ach)
            sqn = [0, 0]

            def squares(i, src, ready):
                sqs, sm, _ = NORM_AT[i]
                n = NORM_N[i]
                for k in range(NORM_K[i]):
                    for w in (ready(k) or ()):
                        act_e.wait_ge(*w)
                    if k >= 3:
                        act_e.wait_ge(s_add, sqn[1] + k - 2)
                    act_e.activation(sm[:, 0:n] if k == 0 else sqs[k % 2][:, 0:n], src(k), ACT.Square).then_inc(s_sq, 1)
                sqn[1] += NORM_K[i] - 1

            def root(i):
                act_e.wait_ge(s_stat, i + 1)
                nt = NORM_N[i] // P
                act_e.activation(rms[i % 2][:, 0:nt], ps[:, NORM_PS[i], 0:nt], ACT.Sqrt, bias=epst, scale=KT / NORM_K[i]).then_inc(s_rt, 1)

            def spread(i):
                act_e.wait_ge(s_bc, i + 1)
                act_e.activation(NORM_AT[i][2][:, 0:NORM_N[i]], banks(NORM_PS[i], NORM_N[i]), ACT.Copy).then_inc(s_rs, 1)

            def norm(i):
                root(i)
                spread(i)

            act_e.wait_ge(par, 16 * NPAR)
            act_e.wait_ge(s_bf, 1)
            act_e.activation(scT[:, :, 0:1], col("cvec", 0, 8), ACT.Silu)
            act_e.activation(scT[:, :, 1:2], col("cctx", 0, 8), ACT.Silu).then_inc(s_silu, 1)
            squares(0, lambda k: xT[:, k, :], lambda k: [(xl[k // 2], 16)])
            norm(0)
            for k in range(KT):
                act_e.wait_ge(s_n1, k + 1)
                act_e.activation(n_hi[:, k, :], xT[:, k, :], ACT.Copy).then_inc(s_nhi, 1)

            def first_high(n):
                w = KT * (P if n < 12 else QK)
                act_e.wait_ge(wl[n // 2 % 2], 16 * (n // 4 + 1))
                if n >= 2:
                    act_e.wait_ge(tps, 2 * (T_IN + n - 2) + 2)
                act_e.activation(w_hi[:, n % 2, 0:w], slot[n // 2 % 2][:, n % 2 * D:n % 2 * D + w], ACT.Copy).then_inc(s_ihi, 1)

            act_e.wait_ge(extra, 16)
            act_e.wait_ge(s_ad, 1)
            act_e.activation(v_hi[:], wv, ACT.Copy).then_inc(s_ihi, 1)
            for n in range(2):
                first_high(n)
            act_e.activation(rowA, banks(0, 2 * D)[0:2], ACT.Copy).then_inc(s_row, 1)

            def half1(t, out, scale=None):
                act_e.wait_ge(tps, 2 * t + 2)
                return act_e.activation(out[0], out[1], ACT.Copy, scale=scale) if scale else act_e.activation(out[0], out[1], ACT.Copy)

            def b1(t):
                return 2 * (t % 2) + 1
            hi = slice(HALF, S)
            for t in range(4):
                g = T_V + t
                half1(g, (swav[:, 2 * t + 1, :], ps[:, b1(g), 0:P]))
                act_e.activation(VH[:, 2 * t + 1, 0:256], ps[:, b1(g), P:384], ACT.Copy).then_inc(eva, 1)
            for t in range(13):
                g = T_IN + t
                src = ps[:, b1(g), :]
                if t < 2:
                    half1(g, (cq[:, t, hi], src)).then_inc(eva, 1)
                elif t == 2:
                    half1(g, (ckv[:, hi], src)).then_inc(eva, 1)
                elif t < 7:
                    dst, h = (QH, 2 * (t - 3)) if t < 5 else (KH, 2 * (t - 5))
                    half1(g, (dst[0:HD, h, hi], src[0:HD]), HD ** -0.5 if t < 5 else None)
                    act_e.activation(dst[0:HD, h + 1, hi], src[HD:P], ACT.Copy, scale=HD ** -0.5 if t < 5 else 1.0).then_inc(eva, 1)
                elif t == 7:
                    half1(g, (swak[:, hi], src)).then_inc(eva, 1)
                elif t < 12:
                    act_e.wait_ge(s_h, KT + 2 + 1)
                    half1(g, (swaq[:, t - 8, hi], src), HD ** -0.5).then_inc(eva, 1)
                else:
                    half1(g, (krope[64:96, hi], src[64:96]))
                    act_e.activation(flog[0:4, hi], src[0:4], ACT.Identity, bias=fbias[0:4]).then_inc(eva, 1)
                if t + 2 < 13:
                    first_high(t + 2)
                if t == 2:
                    squares(1, lambda k: cq[:, k, :], lambda k: [(evv, T_IN + 2), (eva, T_IN + 2)])
                if t in (3, 5):
                    root(1 if t == 3 else 2)
                if t in (4, 6):
                    spread(1 if t == 4 else 2)
                if t == 4:
                    squares(2, lambda k: ckv, lambda k: [(s_h, KT + 2), (evv, T_IN + 3), (eva, T_IN + 3)])
            act_e.wait_ge(s_f, 1)
            ac.link(act_e.activation(ftmp[0:4], ftmp[0:4], ACT.Exp, scale=-1.0))
            act_e.activation(ftmp[0:4], ftmp[0:4], ACT.Ln, bias=1.0).then_inc(s_fe, 1)
            for h in range(4):
                g = T_UQ + h
                half1(g, (QH[0:QK, 4 + h, hi], ps[0:QK, b1(g), :]), QK ** -0.5).then_inc(eva, 1)
            for h in range(4):
                g = T_UKV + h
                half1(g, (KH[0:HD, 4 + h, hi], ps[0:HD, b1(g), :])).then_inc(eva, 1)
            for t in range(4):
                g = T_LV + t
                half1(g, (VH[:, 2 * t + 1, 256:512], ps[:, b1(g), 0:256])).then_inc(eva, 1)

            def exps(n, g, cols_of, src, probs=probs):
                for u in range(n):
                    act_e.wait_ge(s_max, g + (u + 1))
                    if not isinstance(g, int) or g + u >= 2:
                        act_e.wait_ge(s_T, g + (u - 1))
                    w, c = cols_of(u), u % 4
                    act_e.activation(probs[u % 2][:, 0:w], src(u), ACT.Exp, bias=nmax[:, c:c + 1], accum_out=den[:, c:c + 1]).then_inc(s_exp, 1)

            def swa(n, g):
                w = P if isinstance(n, int) else 2 * P
                exps(8, g, lambda u: w + 1, lambda u: ps[:, 2 * (u % 2), 0:w + 1])
            swa(0, 0)
            with act_e.Fori(1, NT) as n:
                swa(n, n * 8)
            groups = ((0, 512), (512, 256), (768, 256))
            for j in range(2):
                c, w = groups[j]
                with act_e.Fori(0, CH // 2) as m:
                    exps(8, m * 8 + (U_DENSE + 32 * j), lambda u: (u + 1) * P, lambda u: banks(2 * (u % 2), (u + 1) * P))
                    act_e.wait_ge(s_o, U_DENSE + 32 * j)
                    for i in range(2):
                        act_e.activation(gsq[i][:, 0:w], mixed[:, bass.ds(2 * m + i, 1), c:c + w].rearrange("p a c -> p (a c)"), ACT.Square,
                                         accum_out=gss[:, bass.ds(2 * m + i, 1), j:j + 1].rearrange("p a c -> p (a c)"))
            c, w = groups[2]
            for i in range(NT):
                act_e.wait_ge(s_o, U_ATT2 - NT + i + 1)
                ac.mark(act_e.activation(gsq_last[i], mixed[:, i, c:c + w], ACT.Square, accum_out=gss[:, i, 2:3]))

            def weight_high(gg, c, q, free):
                act_e.wait_ge(s_wl[c], 8 * gg + (16 - 8 * c))
                act_e.wait_ge(*free)
                act_e.activation(w_hi[:, q, :], slot[c][:, q * D:(q + 1) * D], ACT.Copy).then_inc(s_whi, 1)

            def gated_high(half, k, q, free):
                act_e.wait_ge(s_act, k + (half * FT + 2))
                act_e.wait_ge(*free)
                act_e.activation(a_hi[:, q, :], act[:, k, :], ACT.Copy).then_inc(s_ahi, 1)

            for q in range(2):
                weight_high(G_OUT, 0, q, (tps, 2 * T_UQ))
            ac.need()
            for j, (c, w) in enumerate(groups):
                act_e.activation(grs[:, :, j:j + 1], gss[:, :, j:j + 1], ACT.Sqrt, bias=epst, scale=1.0 / w).then_inc(s_gq, 1)
            act_e.wait_ge(s_gr, 1)
            for i in range(NT):
                act_e.activation(mixed[:, i, 0:512], mixed[:, i, 0:512], ACT.Copy, scale=grs[:, i, 0:1]).then_inc(s_gna, 1)
            for k in range(KT):
                g = T_MT + k
                act_e.wait_ge(tps, 2 * g + 2)
                act_e.activation(m_hi[:, k, :], banks(2 * (g % 4), S), ACT.Copy, scale=col("group", k)).then_inc(eva, 1)
            act_e.wait_ge(tps, 2 * T_OUT)
            with act_e.Fori(0, 2) as m:
                for c in range(2):
                    for q in range(2):
                        g = 2 * m + c
                        act_e.wait_ge(tps, 4 * g + (2 * (T_OUT + q) + 2))
                        weight_high(g + (G_OUT + 1), 1 - c, q, parts_used("out", 0, g, q))
                        act_e.activation(zT[:, 2 * g + q, hi], ps[:, b1(T_OUT + q), :], ACT.Copy).then_inc(eva, 1)
                        act_e.wait_ge(evv, 2 * g + (T_OUT + q + 1))
                        act_e.wait_ge(eva, 2 * g + (T_OUT + q + 1))
                        act_e.wait_ge(s_zadd, 2 * g + (q + 1))
                        act_e.activation(sq[q], zT[:, bass.ds(2 * g + q, 1), :].rearrange("p a b -> p (a b)"), ACT.Square).then_inc(s_zsq, 1)
            norm(3)
            squares(4, lambda k: xT[:, k, :], lambda k: [(s_x, k + 1)])
            norm(4)
            for g in range(2):
                act_e.wait_ge(s_ad, 2 + g)
                act_e.activation(rowB[:, g * ADA:(g + 1) * ADA], banks(3 * g, ADA)[0:2], ACT.Copy).then_inc(s_row, 1)
            for half in range(2):
                p0 = half * FT
                sl = G_UP[half] % 2

                def conv(j, bs=(0, 1)):
                    for b in bs:
                        g = 2 * j + b
                        weight_high(g + (G_UP[half] + 1), (sl + b + 1) % 2, 0, parts_used("up", half, g, 0))
                        act_e.wait_ge(s_wu, 2 * g + (W_UP[half] + 2))
                        act_e.wait_ge(s_act, g + (p0 + 1))
                        for q in range(2):
                            t = 2 * j + (q * FT + b)
                            act_e.activation(convy[b][q], ps[:, 2 * b + q, :], ACT.Identity, bias=cols[:, bass.ds(t + COLS["conv_b"][0], 1)],
                                             scale=cols[:, bass.ds(t + (COLS["conv_w"][0] + 2 * 2 * FT), 1)]).then_inc(s_ua, 1)
                        weight_high(g + (G_UP[half] + 1), (sl + b + 1) % 2, 1, parts_used("up", half, g, 1))
                        act_e.wait_ge(s_uv, g + (p0 + 3))
                        act_e.activation(gelu[b], convy[b][0], ACT.Gelu_apprx_tanh).then_inc(s_gl, 1)
                conv(0, (0,))
                if half:
                    root(5)
                conv(0, (1,))
                if half:
                    spread(5)
                with act_e.Fori(1, FT // 2 - 1) as j:
                    conv(j)
                for q in range(2):
                    gated_high(half, q, q, parts_used("down", 0, FT // 2 - 1, q) if half else (s_S, U_ATT2))
                conv(FT // 2 - 1)
                sl = G_DN[half] % 2
                with act_e.Fori(0, (FT // 2 - 1) // 2) as m:
                    for c in range(2):
                        for q in range(2):
                            g = 2 * m + c
                            weight_high(g + (G_DN[half] + 1), (sl + c + 1) % 2, q, parts_used("down", half, g, q))
                            gated_high(half, 2 * g + (2 + q), q, parts_used("down", half, g, q))
                nxt = (G_UP[1], G_IN2)[half]
                for q in range(2):
                    weight_high(nxt, nxt % 2, q, parts_used("down", half, FT // 2 - 1, q))
                if half:
                    squares(6, lambda k: ctxT[:, k, :], lambda k: [(s_cl, 16)])
                act_e.wait_ge(s_x, 8 + 8 * half)
                for t in range(1, KT, 2):
                    act_e.wait_ge(tps, 2 * (T_DN + 4 * half) + t + 1)
                    act_e.activation(yT[:, t, :], ps[:, t, :], ACT.Copy).then_inc(eva, 1)
                d = T_DN + 4 * half + 4
                squares(5 + 2 * half, lambda k: yT[:, k, :], lambda k: [(evv, d), (eva, d)])
            root(6)
            root(7)
            spread(6)
            spread(7)
            def shift(i, base, dst, row, b):
                for k in range(KT):
                    act_e.wait_ge(s_h, base + k + 1)
                    act_e.activation(dst[:, k, :], dst[:, k, :], ACT.Identity, bias=mod[:, row + k, b:b + 1]).then_inc(s_hb, 1)
            shift(6, 27, hcT, 0, 1)
            squares(8, lambda k: xT[:, k, :], lambda k: [(s_x, 17 + k)])
            act_e.wait_ge(s_cx, 1)
            act_e.activation(vc[:, :, :], ps[:, 5, 0:2 * P].rearrange("p (a b) -> p a b", a=2), ACT.Copy).then_inc(s_cxe, 1)
            norm(8)
            for i in range(2 * KT):
                hf, k = i // KT, i % KT
                act_e.wait_ge(s_h, 35 + i + 1)
                act_e.activation(g_hi[:, k, hf * HALF:(hf + 1) * HALF], sq[i % 2][:, 0:HALF], ACT.Identity, bias=mod[:, k, 0:1]).then_inc(s_hb, 1)
            def input_high(n):
                weight_high(G_IN2 + n // 2, (n // 2) % 2, n % 2, in2_used(n - 2))
            act_e.wait_ge(tps, 2 * T_VT + 3)
            act_e.activation(vT[:, hi], ps[:, b1(T_VT), :], ACT.Copy).then_inc(eva, 1)
            act_e.wait_ge(tps, 2 * T_VT + 4)
            act_e.activation(k2[:, hi], ps[:, b1(T_K2), :], ACT.Copy).then_inc(eva, 1)
            for n in (2, 3):
                input_high(n)
            half1(T_V2, (v2[:, NT // 2:NT, :].rearrange("p a c -> p (a c)"), ps[:, b1(T_V2), :])).then_inc(eva, 1)
            for t in range(1, 17):
                g = T_IN2 + t
                src = ps[:, b1(g), :]
                input_high(t + 3)
                if t < 5:
                    half1(g, (q2[:, t - 1, hi], src), HD ** -0.5).then_inc(eva, 1)
                else:
                    act_e.wait_ge(evv, g + 1)
                    act_e.activation(apad[:, t - 5:t - 4], epst, ACT.Copy).then_inc(eva, 1)

            def att(g, nl):
                at = 512 - nl
                exps(8, g, lambda u: nl + CTX + 1, lambda u: banks(2 * (u % 2), 1024)[:, at:512 + CTX + 1], late_probs)
            att(U_ATT2, 2 * P)
            with act_e.Fori(1, NT - 1) as n:
                att(n * 8 + U_ATT2, 3 * P)
            att(U_ATT2 + 8 * (NT - 1), 2 * P)
            for k in range(4):
                g = T_AT + k
                act_e.wait_ge(tps, 2 * g + 2)
                act_e.activation(o_hi[:, k, :], banks(2 * (g % 4), S), ACT.Copy).then_inc(eva, 1)
            for m in range(KT):
                b, g = m % 2, T_OUT2 + m
                act_e.wait_ge(tps, 2 * g + 2)
                if m + 2 < KT:
                    weight_high(G_OUT2 + m // 2 + 1, (G_OUT2 + m // 2 + 1) % 2, b, (tps, 2 * g + 2))
                act_e.wait_ge(s_x3, m + 1)
                act_e.activation(gt1o[b], ps[:, b1(g), :], ACT.Copy, scale=mod[:, 16 + m, 0:1]).then_inc(eva, 1)
                act_e.wait_ge(evv, g + 1)
                act_e.wait_ge(s_x3, m + 2)
                act_e.wait_ge(s_zadd, 9 + m + 1)
                act_e.activation(late_probs[b], xT[:, m, :], ACT.Square).then_inc(s_zsq, 1)
            norm(9)
            shift(9, 51, hT, 24, 0)

            act_e.wait_ge(s_lgT, 1)
            act_e.activation(lgT, banks(0, S)[0:NE], ACT.Copy).then_inc(s_lgc, 1)
            act_e.wait_ge(s_rm, 1)
            act_e.activation(aff, aff, ACT.Exp).then_inc(s_re, 1)
            for i in range(2 * NT):
                g, dst = T_XR + i, tok[i % 2]
                act_e.wait_ge(tps, 2 * g + 2)
                if i >= 2:
                    act_e.wait_ge(s_tkst[i % 2], 16 * (i // 2))
                if i >= NT:
                    act_e.wait_ge(s_aff, 1)
                    act_e.activation(dst[:, D:ROW], aff[:, i - NT, :], ACT.Copy)
                act_e.activation(dst[:, 0:D], banks(2 * (g % 2), D), ACT.Copy).then_inc(eva, 1)
            def columns(e, b):
                act_e.wait_ge(s_xt, e + 1)
                act_e.activation(x_hi[:, b].rearrange("p a b -> p (a b)"), banks(4, D), ACT.Copy).then_inc(s_xhi, 1)

            def silu(e, used):
                act_e.wait_ge(s_eu, used)
                if not isinstance(e, int) or e:
                    act_e.wait_ge(s_ga, e)
                act_e.activation(sgate, banks(0, D), ACT.Silu).then_inc(s_sg, 1)

            def part_high(n, sl, a, e, first=False):
                act_e.wait_ge(wl[sl], e * 16 + 16 * (loads_before("expert", sl) + 1))
                if not first:
                    act_e.wait_ge(s_eu, n + (1 - RING))
                act_e.activation(e_hi[:, (2 * sl + a) % RING, :], slot[sl][:, a * D:(a + 1) * D], ACT.Copy).then_inc(s_ehi, 1)

            def expert(e, b, last=False):
                for i, sl, a, ee in expert_items(e, last):
                    if isinstance(e, int) and e == 0 and i == RING - 1:
                        silu(0, KT)
                    if not last and i == 4:
                        columns(e + 1, 1 - b)
                    if not last and i == 2 * KT + RING - 1:
                        silu(e + 1, expert_item(e, 2 * KT))
                    if i == (KT + 4 if last else 2 * KT):
                        act_e.wait_ge(s_at2, e + 1)
                        act_e.activation(t_hi.rearrange("p a b -> p (a b)"), banks(4, D), ACT.Copy).then_inc(s_thi, 1)
                    part_high(expert_item(e, i), sl, a, ee)

            for b in range(2):
                act_e.wait_ge(s_tkst[b], 16 * NT)
            columns(0, 0)
            for k in range(KT):
                part_high(k, k // 2, k % 2, 0, k < RING)
            expert(0, 0)
            with act_e.Fori(0, NE // 2 - 1) as q:
                for b in range(2):
                    expert(2 * q + (1 + b), 1 - b)
            expert(NE - 1, 1, last=True)
            for i in range(NT):
                act_e.wait_ge(s_fl[i], 16)
                ac.mark(act_e.activation(fsq, fin[i], ACT.Square, accum_out=fss[:, i:i + 1]))
                ac.need()
                act_e.activation(frs[:, i:i + 1], fss[:, i:i + 1], ACT.Sqrt, bias=epst, scale=1.0 / D).then_inc(s_frt, 1)

        @block.vector
        def _(v):
            vc_ = Chain(v, vch)
            done = [0, 0]

            def sums(i):
                sqs, sm, rs = NORM_AT[i]
                n = NORM_N[i]
                for k in range(1, NORM_K[i]):
                    v.wait_ge(s_sq, done[0] + k + 1)
                    if k > 1:
                        v.wait_ge(s_add, done[1] + k - 1)
                    v.tensor_tensor(sm[:, 0:n], sm[:, 0:n], sqs[k % 2][:, 0:n], ALU.add).then_inc(s_add, 1)
                done[0] += NORM_K[i]
                done[1] += NORM_K[i] - 1
                v.wait_ge(s_sq, done[0])
                if done[1]:
                    v.wait_ge(s_add, done[1])
                v.tensor_copy(vpad[:, 1:2], epst).then_inc(s_ssq, 1)

            def diagonal(i):
                v.wait_ge(s_rt, i + 1)
                nt = NORM_N[i] // P
                vc_.link(v.reciprocal(rms[i % 2][:, 0:nt], rms[i % 2][:, 0:nt]))
                v.scalar_tensor_tensor(NORM_AT[i][0][0][:, 0:nt * P].rearrange("p (t c) -> p t c", t=nt), rms[i % 2][:, 0:nt].unsqueeze(2).to_broadcast([P, nt, P]), float(D),
                                       ident.unsqueeze(1).to_broadcast([P, nt, P]), ALU.mult, ALU.mult).then_inc(s_dg, 1)

            def spread_ready(i):
                v.wait_ge(s_rs, i + 1)
                return NORM_AT[i][2][:, 0:NORM_N[i]]

            def inverse(i):
                diagonal(i)
                return spread_ready(i)

            vc_.mark(v.memset(epst, EPS))
            v.wait_ge(par, 16 * NPAR)
            vc_.mark(v.tensor_copy(identb, ident))
            vc_.mark(v.tensor_copy(causalb, con("causal")))
            vc_.mark(v.tensor_copy(leftb, con("left")))
            vc_.mark(v.tensor_scalar(sinkB, sinkB, float(D), None, ALU.mult))
            vc_.need()
            v.tensor_copy(vpad[:, 3:4], epst).then_inc(s_bf, 1)
            v.wait_ge(s_bl, 1)
            v.tensor_tensor(exts, ps[0:8, 4, 0:384], extm, ALU.add).then_inc(s_bls, 1)
            sums(0)
            rs = inverse(0)
            for k in range(KT):
                v.scalar_tensor_tensor(xT[:, k, :], xT[:, k, :], col("attn_pre", k), rs, ALU.mult, ALU.mult).then_inc(s_n1, 1)
            for k in range(KT):
                v.wait_ge(s_nhi, k + 1)
                v.tensor_tensor(n_lo[k], xT[:, k, :], n_hi[:, k, :].bitcast(F32), ALU.subtract).then_inc(s_h, 1)

            def b0(t):
                return 2 * (t % 2)
            lo = slice(0, HALF)

            def half0(t, dst, src, scale=None):
                v.wait_ge(tps, 2 * t + 1)
                return v.tensor_scalar(dst, src, scale, None, ALU.mult) if scale else v.tensor_copy(dst, src)

            v.wait_ge(s_flip, 1)
            v.tensor_copy(swab.rearrange("p a b -> p (a b)"), banks(4, 2048))
            for t in range(4):
                g = T_V + t
                half0(g, swav[:, 2 * t, :], ps[:, b0(g), 0:P])
                v.tensor_copy(VH[:, 2 * t, 0:256], ps[:, b0(g), P:384]).then_inc(evv, 1)
            v.wait_ge(s_mod, 1)
            vc_.mark(v.tensor_copy(mod[:, 0:2 * KT, :], ps[:, 4, 0:4 * KT].rearrange("p (a b) -> p a b", b=2)))
            for t in range(13):
                g = T_IN + t
                src = ps[:, b0(g), :]
                if t < 2:
                    half0(g, cq[:, t, lo], src).then_inc(evv, 1)
                elif t == 2:
                    half0(g, ckv[:, lo], src).then_inc(evv, 1)
                elif t < 7:
                    dst, h = (QH, 2 * (t - 3)) if t < 5 else (KH, 2 * (t - 5))
                    half0(g, dst[0:HD, h, lo], src[0:HD], HD ** -0.5 if t < 5 else None)
                    v.tensor_scalar(dst[0:HD, h + 1, lo], src[HD:P], HD ** -0.5 if t < 5 else 1.0, None, ALU.mult).then_inc(evv, 1)
                elif t == 7:
                    half0(g, swak[:, lo], src).then_inc(evv, 1)
                elif t < 12:
                    v.wait_ge(s_h, KT + 2 + 1)
                    half0(g, swaq[:, t - 8, lo], src, HD ** -0.5).then_inc(evv, 1)
                else:
                    half0(g, krope[64:96, lo], src[64:96])
                    v.tensor_scalar(flog[0:4, lo], src[0:4], fbias[0:4], None, ALU.add).then_inc(evv, 1)
                if t == 3:
                    sums(1)
                    diagonal(1)
                if t == 4:
                    rs = spread_ready(1)
                    for k in range(2):
                        v.scalar_tensor_tensor(cq[:, k, :], cq[:, k, :], col("qlat", k), rs, ALU.mult, ALU.mult).then_inc(s_h, 1)
                    sums(2)
                if t == 5:
                    diagonal(2)
                if t == 6:
                    rs = spread_ready(2)
                    v.scalar_tensor_tensor(ckv, ckv, col("kvlat"), rs, ALU.mult, ALU.mult).then_inc(s_h, 1)
            v.wait_ge(evv, T_UQ)
            v.wait_ge(eva, T_UQ)
            v.scalar_tensor_tensor(ftmp[0:4], flog[0:4], -1.0, flog[0:4], ALU.mult, ALU.max).then_inc(s_f, 1)
            v.wait_ge(s_fe, 1)
            vc_.link(v.tensor_scalar(flog[0:4], flog[0:4], 0.0, None, ALU.min))
            vc_.link(v.tensor_tensor(ftmp[0:4], flog[0:4], ftmp[0:4], ALU.subtract))
            vc_.link(v.tensor_tensor_scan(flog[0:4], ftmp[0:4], ftmp[0:4], 0.0, ALU.add, ALU.min))
            v.tensor_scalar(flog[0:4], flog[0:4], -1.0, None, ALU.mult).then_inc(s_fd, 1)
            def rotate(i, x, c, s, tmp, r):
                v.wait_ge(s_sw, i + 1)
                vc_.mark(v.tensor_tensor(tmp[r], banks(4, S)[r], s[r], ALU.mult))
                vc_.link(v.tensor_tensor(x[r], x[r], c[r], ALU.mult))
                v.tensor_tensor(x[r], x[r], tmp[r], ALU.add).then_inc(s_rot, 1)

            r32 = slice(64, 96)
            v.wait_ge(s_rope, 16)
            rotate(0, krope, rope1[:, 0, :], rope1[:, 1, :], ropet, r32)
            for h in range(4):
                g = T_UQ + h
                half0(g, QH[0:QK, 4 + h, lo], ps[0:QK, b0(g), :], QK ** -0.5).then_inc(evv, 1)
                if h:
                    rotate(h, QH[:, 3 + h, :], rope1[:, 0, :], rope1[:, 1, :], ropet, r32)
            for h in range(4):
                g = T_UKV + h
                half0(g, KH[0:HD, 4 + h, lo], ps[0:HD, b0(g), :]).then_inc(evv, 1)
                if h == 0:
                    rotate(4, QH[:, 7, :], rope1[:, 0, :], rope1[:, 1, :], ropet, r32)
            for t in range(4):
                g = T_LV + t
                half0(g, VH[:, 2 * t, 256:512], ps[:, b0(g), 0:256]).then_inc(evv, 1)

            def units(g, now, before=None, probsT=probsT):
                def after(s, d, u, least):
                    if not isinstance(g, int) or g + u >= least:
                        v.wait_ge(s, g + (u + d))

                def group(w):
                    return now if w >= 0 else before
                for u in range(8 if now else 2):
                    if now:
                        c = u % 4
                        v.wait_ge(s_S, g + (u + 1))
                        v.tensor_reduce(nmax[:, c:c + 1], now[0](u), AX_X, ALU.max, negate=True).then_inc(s_max, 1)
                    w = u - 1
                    if (now or u == 0) and group(w):
                        v.wait_ge(s_T, g + (w + 1))
                        after(s_pv, -1, w, 2)
                        n = group(w)[1](w % 8)
                        v.tensor_copy(probsT[w % 2][:, 0:n], banks(4, n)).then_inc(s_pt, 1)
                    w = u - 2
                    if group(w):
                        c = w % 4
                        v.wait_ge(s_pv, g + (w + 1))
                        vc_.link(v.reciprocal(rec[:, c:c + 1], den[:, c:c + 1]))
                        v.tensor_scalar(group(w)[2](w % 8), ps[:, 6 + w % 2, 0:HD], rec[:, c:c + 1], None, ALU.mult).then_inc(s_o, 1)

            def hd(u):
                return (u // 2 + 4 * (u % 2)) * HD

            def swa(n):
                w = P if isinstance(n, int) and n == 0 else 2 * P
                return lambda u: ps[:, 2 * (u % 2), 0:w + 1], lambda u: w, lambda u: mixed[:, n, hd(u):hd(u) + HD]

            def dense(h):
                return lambda u: banks(2 * (u % 2), (u + 1) * P), lambda u: (u + 1) * P, lambda u: mixed[:, u, bass.ds(h * HD + 512, HD)]
            units(U_SWA, swa(0))
            units(8, swa(1), swa(0))
            with v.Fori(2, NT) as n:
                vc_.enter(n - 2, 8)
                units(n * 8, swa(n), swa(n - 1))
                vc_.leave(NT - 2)
            units(U_DENSE, dense(0), swa(NT - 1))
            with v.Fori(1, CH) as h:
                vc_.enter(h - 1, 8)
                units(h * 8 + U_DENSE, dense(h), dense(h - 1))
                vc_.leave(CH - 1)
            units(U_ATT2, None, dense(CH - 1))
            v.wait_ge(s_gq, 3)
            v.reciprocal(grs, grs).then_inc(s_gr, 1)
            v.wait_ge(s_gr, 1)
            for i in range(NT):
                for j, (c, w) in ((1, (512, 256)), (2, (768, 256))):
                    last = v.tensor_scalar(mixed[:, i, c:c + w], mixed[:, i, c:c + w], grs[:, i, j:j + 1], None, ALU.mult)
                last.then_inc(s_gn, 1)
            for k in range(KT):
                g = T_MT + k
                v.wait_ge(eva, g + 1)
                v.scalar_tensor_tensor(m_lo[:, k, :], banks(2 * (g % 4), S), col("group", k), m_hi[:, k, :].bitcast(F32), ALU.mult, ALU.subtract).then_inc(evv, 1)
            v.wait_ge(tps, 2 * T_OUT)
            v.memset(ssq, 0.0).then_inc(s_zadd, 1)
            with v.Fori(0, 4) as j:
                for b in range(2):
                    v.wait_ge(tps, 4 * j + (2 * (T_OUT + b) + 1))
                    v.tensor_copy(zT[:, 2 * j + b, lo], ps[:, b0(T_OUT + b), :]).then_inc(evv, 1)
                    v.wait_ge(s_zsq, 2 * j + (b + 1))
                    v.wait_ge(s_zadd, 2 * j + (b + 1))
                    v.tensor_tensor(ssq, ssq, sq[b], ALU.add).then_inc(s_zadd, 1)
            v.wait_ge(s_zadd, 9)
            v.memset(vpad[:, 1:2], 0.0).then_inc(s_ssq, 1)
            rs = inverse(3)
            for k in range(KT):
                v.scalar_tensor_tensor(zT[:, k, :], zT[:, k, :], col("attn_post", k), rs, ALU.mult, ALU.mult).then_inc(s_zn, 1)
            sums(4)
            inverse(4)

            def split_input(half):
                hs = slice(half * HALF, (half + 1) * HALF)
                if half:
                    v.wait_ge(s_wu, W_DN[0])
                for k in range(KT):
                    tmp = sq[k % 2][:, 0:HALF]
                    vc_.link(v.scalar_tensor_tensor(tmp, xT[:, k, hs], col("ffn_pre", k), rstdB[:, hs], ALU.mult, ALU.mult))
                    v.tensor_copy(h_hi[:, k, :], tmp).then_inc(s_hhi, 1)
                    v.wait_ge(s_hhi, half * KT + k + 1)
                    v.tensor_tensor(h_lo[:, k, :], tmp, h_hi[:, k, :].bitcast(F32), ALU.subtract).then_inc(s_h, 1)
            split_input(0)
            v.memset(vpad[:, 0:1], 0.0).then_inc(s_uv, 1)
            v.memset(vpad[:, 1:2], 0.0).then_inc(s_uv, 1)
            v.memset(vpad[:, 2:3], 0.0).then_inc(s_act, 1)
            for half in range(2):
                p0 = half * FT

                def taps(j, bs=(0, 1)):
                    for b in bs:
                        g = 2 * j + (p0 + b)
                        w0, w1 = COLS["conv_w"][0], COLS["conv_w"][0] + 2 * FT
                        v.wait_ge(s_ua, 2 * g + 2)
                        for q in range(2):
                            t = 2 * j + (q * FT + b)
                            vc_.mark(v.scalar_tensor_tensor(convy[b][q][:, 1:HALF], ps[:, 2 * b + q, 0:HALF - 1], cols[:, bass.ds(t + w1, 1)],
                                                            convy[b][q][:, 1:HALF], ALU.mult, ALU.add))
                            if half:
                                vc_.mark(v.scalar_tensor_tensor(convy[b][q][:, 0:1], carry[:, bass.ds(t, 1), 1:2].rearrange("p a b -> p (a b)"), cols[:, bass.ds(t + w1, 1)],
                                                                convy[b][q][:, 0:1], ALU.mult, ALU.add))
                        vc_.need()
                        for q in range(2):
                            t = 2 * j + (q * FT + b)
                            two = carry[:, bass.ds(t, 1), :].rearrange("p a b -> p (a b)")
                            if half:
                                vc_.mark(v.scalar_tensor_tensor(convy[b][q][:, 0:2], two, cols[:, bass.ds(t + w0, 1)],
                                                                convy[b][q][:, 0:2], ALU.mult, ALU.add))
                            else:
                                vc_.mark(v.tensor_copy(two, ps[:, 2 * b + q, HALF - 2:HALF]))
                            last = v.scalar_tensor_tensor(convy[b][q][:, 2:HALF], ps[:, 2 * b + q, 0:HALF - 2], cols[:, bass.ds(t + w0, 1)],
                                                          convy[b][q][:, 2:HALF], ALU.mult, ALU.add)
                            if half:
                                vc_.mark(last) if q == 0 else last.then_inc(s_uv, 1)
                            elif q == 1:
                                last.then_inc(s_uv, 1)
                        if half:
                            vc_.mark(v.memset(vpad[:, 3:4], 0.0))
                        v.wait_ge(s_gl, g + 1)
                        v.tensor_tensor(act[:, bass.ds(2 * j + b, 1), :].rearrange("p a b -> p (a b)"), gelu[b], convy[b][1], ALU.mult).then_inc(s_act, 1)
                taps(0, (0,))
                if half:
                    diagonal(5)
                else:
                    v.wait_ge(s_mod, 2)
                    vc_.link(v.tensor_copy(mod[:, 2 * KT:5 * KT, :], ps[:, 4, 0:6 * KT].rearrange("p (a b) -> p a b", b=2)))
                    for b in range(2):
                        vc_.mark(v.tensor_tensor(mod[:, :, b], mod[:, :, b], col("b_ada", 0, 40), ALU.add))
                    vc_.need()
                    for i, (row, b, g) in enumerate(((8, 0, "g_mix"), (8, 1, "g_mix"), (32, 0, "g_ffn"))):
                        vc_.mark(v.scalar_tensor_tensor(gsc[:, i, :], mod[:, row:row + 8, b], 1.0, col(g, 0, 8), ALU.add, ALU.mult))
                    vc_.need()
                taps(0, (1,))
                if half:
                    rs = spread_ready(5)
                    for k in range(KT):
                        v.scalar_tensor_tensor(yT[:, k, :], yT[:, k, :], col("ffn_post", k), rs, ALU.mult, ALU.mult).then_inc(s_zn, 1)
                    for k in range(KT):
                        v.wait_ge(s_zn, KT + k + 1)
                        v.tensor_tensor(xT[:, k, lo], xT[:, k, lo], yT[:, k, :], ALU.add).then_inc(s_x, 1)
                with v.Fori(1, FT // 2) as j:
                    vc_.enter(j - 1, 16 if half else 8)
                    taps(j)
                    vc_.leave(FT // 2 - 1)
                if half == 0:
                    split_input(1)
                if half:
                    sums(6)
                for t in range(0, KT, 2):
                    v.wait_ge(tps, 2 * (T_DN + 4 * half) + t + 1)
                    v.tensor_copy(yT[:, t, :], ps[:, t, :]).then_inc(evv, 1)
                sums(5 + 2 * half)
            diagonal(6)
            diagonal(7)
            rs = spread_ready(6)
            for k in range(KT):
                v.scalar_tensor_tensor(hcT[:, k, :], ctxT[:, k, :], gsc[:, 1, k:k + 1], rs, ALU.mult, ALU.mult).then_inc(s_h, 1)
            rs = spread_ready(7)
            for k in range(KT):
                v.scalar_tensor_tensor(yT[:, k, :], yT[:, k, :], col("ffn_post", k), rs, ALU.mult, ALU.mult).then_inc(s_zn, 1)
            sums(8)
            v.wait_ge(s_cx, 1)
            v.tensor_copy(kc, ps[:, 4, 0:CTX]).then_inc(s_cxe, 1)
            rs = inverse(8)
            for i in range(2 * KT + 1):
                if 2 <= i < 2 * KT:
                    v.wait_ge(s_hhi, 2 * KT + i - 1)
                if i < 2 * KT:
                    k, hs = i % KT, slice(i // KT * HALF, (i // KT + 1) * HALF)
                    v.scalar_tensor_tensor(sq[i % 2][:, 0:HALF], xT[:, k, hs], gsc[:, 0, k:k + 1], rs[:, hs], ALU.mult, ALU.mult).then_inc(s_h, 1)
                if i:
                    k, hs = (i - 1) % KT, slice((i - 1) // KT * HALF, ((i - 1) // KT + 1) * HALF)
                    v.wait_ge(s_hb, KT + i)
                    v.scalar_tensor_tensor(g_lo[:, k, hs], sq[(i - 1) % 2][:, 0:HALF], mod[:, k, 0:1], g_hi[:, k, hs].bitcast(F32), ALU.add, ALU.subtract).then_inc(s_hhi, 1)
            v.wait_ge(s_rp, 16)
            v.wait_ge(tps, 2 * T_VT + 1)
            v.tensor_copy(vT[:, lo], ps[:, b0(T_VT), :]).then_inc(evv, 1)
            v.wait_ge(tps, 2 * T_VT + 2)
            v.tensor_copy(k2[:, lo], ps[:, b0(T_K2), :]).then_inc(evv, 1)
            half0(T_V2, v2[:, 0:NT // 2, :].rearrange("p a c -> p (a c)"), ps[:, b0(T_V2), :]).then_inc(evv, 1)
            rotate(5, k2, rope2[:, 0, :], rope2[:, 1, :], ropet2, slice(0, P))
            for t in range(1, 17):
                g = T_IN2 + t
                src = ps[:, b0(g), :]
                if t < 5:
                    half0(g, q2[:, t - 1, lo], src, HD ** -0.5).then_inc(evv, 1)
                    if t > 1:
                        rotate(4 + t, q2[:, t - 2, :], rope2[:, 0, :], rope2[:, 1, :], ropet2, slice(0, P))
                    continue
                c, part = (t - 5) // 3, (t - 5) % 3
                both = banks(b0(g), S)
                v.wait_ge(tps, 2 * g + 2)
                if part == 0:
                    if c:
                        v.wait_ge(s_cv, c)
                    v.tensor_copy(convu, both).then_inc(evv, 1)
                    v.wait_ge(evv, g + 1)
                    if c == 0:
                        rotate(9, q2[:, 3, :], rope2[:, 0, :], rope2[:, 1, :], ropet2, slice(0, P))
                elif part == 1:
                    vc_.need()
                    vc_.link(v.tensor_tensor(convu, both, convu, ALU.mult))
                    v.tensor_copy(vpad[:, 0:1], epst).then_inc(evv, 1)
                    vc_.link(v.tensor_scalar(convo, convu, col("conv2", 4 + c), None, ALU.mult))
                    vc_.link(v.scalar_tensor_tensor(convo[:, 1:S], convu[:, 0:S - 1], col("conv2", c), convo[:, 1:S], ALU.mult, ALU.add))
                    vc_.link(v.scalar_tensor_tensor(convo[:, 0:S - 1], convu[:, 1:S], col("conv2", 8 + c), convo[:, 0:S - 1], ALU.mult, ALU.add))
                else:
                    vc_.link(v.tensor_tensor(convm[:, c, :], both, convo, ALU.mult))
                    v.tensor_copy(vpad[:, 0:1], epst).then_inc(evv, 1)
                    v.tensor_copy(vpad[:, 1:2], epst).then_inc(s_cv, 1)

            def att(n, nl):
                at = 512 - nl
                return (lambda u: banks(2 * (u % 2), 1024)[:, at:512 + CTX + 1], lambda u: nl + CTX, lambda u: att2[:, n, hd(u):hd(u) + HD])
            def units2(g, now, before=None):
                units(g, now, before, late_probsT)
            units2(U_ATT2, att(0, 2 * P))
            units2(U_ATT2 + 8, att(1, 3 * P), att(0, 2 * P))
            with v.Fori(2, NT - 1) as n:
                vc_.enter(n - 2, 8)
                units2(n * 8 + U_ATT2, att(n, 3 * P), att(n - 1, 3 * P))
                vc_.leave(NT - 3)
            units2(U_END - 8, att(NT - 1, 2 * P), att(NT - 2, 3 * P))
            units2(U_END, None, att(NT - 1, 2 * P))
            for k in range(4):
                g = T_AT + k
                v.wait_ge(eva, g + 1)
                v.tensor_tensor(o_lo[:, k, :], banks(2 * (g % 4), S), o_hi[:, k, :].bitcast(F32), ALU.subtract).then_inc(evv, 1)
            v.wait_ge(tps, 2 * T_OUT2)
            v.memset(late_probsT[0], 0.0).then_inc(s_zadd, 1)
            with v.Fori(0, 4) as j:
                for b in range(2):
                    m = 2 * j + b
                    v.wait_ge(tps, 4 * j + (2 * (T_OUT2 + b) + 1))
                    v.scalar_tensor_tensor(xT[:, m, lo], ps[:, b0(T_OUT2 + b), :], mod[:, m + 16, 0:1], xT[:, m, lo], ALU.mult, ALU.add).then_inc(evv, 1)
                    v.wait_ge(s_zsq, 2 * j + (8 + b + 1))
                    v.wait_ge(s_zadd, 2 * j + (9 + b + 1))
                    v.tensor_tensor(late_probsT[0], late_probsT[0], late_probs[b], ALU.add).then_inc(s_zadd, 1)
            v.wait_ge(s_zadd, 18)
            v.memset(vpad[:, 1:2], 0.0).then_inc(s_ssq, 1)
            rs = inverse(9)
            for k in range(KT):
                v.scalar_tensor_tensor(hT[:, k, :], xT[:, k, :], gsc[:, 2, k:k + 1], rs, ALU.mult, ALU.mult).then_inc(s_h, 1)

            v.wait_ge(s_lg, 1)
            lg = ps[:, 4, 0:NT * NE].rearrange("p (a b) -> p a b", a=NT)
            vc_.link(v.tensor_reduce(rmx, lg, AX_X, ALU.max))
            v.tensor_tensor(aff, lg, rmx.unsqueeze(2).to_broadcast([P, NT, NE]), ALU.subtract).then_inc(s_rm, 1)
            v.wait_ge(s_re, 1)
            vc_.link(v.tensor_reduce(rsum, aff, AX_X, ALU.add))
            vc_.link(v.reciprocal(rsum, rsum))
            vc_.link(v.tensor_tensor(aff, aff, rsum.unsqueeze(2).to_broadcast([P, NT, NE]), ALU.mult))
            v.tensor_copy(vpad[:, 0:1], epst).then_inc(s_aff, 1)
            for k in range(KT):
                last = v.tensor_scalar(silu_b[:, k, :], con("mean"), scT[:, k, 0:1], float(D), ALU.mult, ALU.mult)
            last.then_inc(s_sb, 1)
            v.wait_ge(s_at, 1)
            vc_.link(v.tensor_copy(work, ps[0:NE, 5:7, :].rearrange("p a b -> p (a b)")))
            for _ in range(CAP // 8):
                vc_.link(v.max(top8[0:NE], work))
                vc_.link(v.match_replace(work, top8[0:NE], work, -1.0))
            vc_.link(v.tensor_scalar(work, work, 0.0, None, ALU.is_lt))
            vc_.link(v.tensor_tensor_scan(pos, work, work, 0.0, ALU.add, ALU.max))
            v.tensor_copy(posbf, pos).then_inc(s_pos, 1)
            v.wait_ge(s_g2, 1)
            v.wait_ge(s_late, 48)
            v.tensor_tensor(gt2B, banks(2, D), gt2B, ALU.add).then_inc(s_g2e, 1)
            for e in range(NE):
                if e:
                    v.wait_ge(s_cnt, e)
                v.wait_ge(s_pb, e + 1)
                v.tensor_scalar(cntj, banks(4 + 2 * (e % 2), S), con("slot"), None, ALU.is_le, ALU.add, accum_out=idxf[:, e:e + 1]).then_inc(s_cnt, 1)
                v.wait_ge(s_cnt, e + 1)
                v.tensor_copy(idxu[:, e:e + 1], idxf[:, e:e + 1]).then_inc(s_idx, 1)
            v.memset(vpad[:, 0:1], 0.0).then_inc(s_ys, 1)

            def columns_low(e, b):
                v.wait_ge(s_xhi, e + 1)
                v.tensor_tensor(x_lo[:, b].rearrange("p a b -> p (a b)"), banks(4, D), x_hi[:, b].rearrange("p a b -> p (a b)").bitcast(F32), ALU.subtract).then_inc(s_xe, 1)

            def part_low(n, sl, a):
                r = (2 * sl + a) % RING
                v.wait_ge(s_ehi, n + 1)
                v.tensor_tensor(e_lo[:, r, :], slot[sl][:, a * D:(a + 1) * D], e_hi[:, r, :].bitcast(F32), ALU.subtract).then_inc(s_elo, 1)

            def output(e, b, used):
                v.wait_ge(s_eu, used)
                v.wait_ge(s_gs, e + 1)
                v.wait_ge(s_yf, e + 1)
                v.scalar_tensor_tensor(yx[b], banks(6, D), gslot[b], gt2B, ALU.mult, ALU.mult).then_inc(s_ys, 1)

            def expert(e, b, last=False):
                v.wait_ge(s_gat[b], 8 * e + (16 - 8 * b))
                v.tensor_copy(gslot[b], xs[b][:, bass.ds(e + D, 1)]).then_inc(s_gs, 1)
                for i, sl, a, _ in expert_items(e, last):
                    if i == RING - 1 and not (isinstance(e, int) and e == 0):
                        output(e - 1, 1 - b, expert_item(e, 0))
                    if not last and i == 4:
                        columns_low(e + 1, 1 - b)
                    if i == KT + RING - 1:
                        v.wait_ge(s_sg, e + 1)
                        v.wait_ge(s_eu, expert_item(e, KT))
                        v.tensor_tensor(actx, banks(2, D), sgate, ALU.mult).then_inc(s_ga, 1)
                    if i == (KT + 4 if last else 2 * KT):
                        v.wait_ge(s_thi, e + 1)
                        v.tensor_tensor(t_lo.rearrange("p a b -> p (a b)"), banks(4, D), t_hi.rearrange("p a b -> p (a b)").bitcast(F32), ALU.subtract).then_inc(s_ae, 1)
                    part_low(expert_item(e, i), sl, a)

            columns_low(0, 0)
            for k in range(KT):
                part_low(k, k // 2, k % 2)
            expert(0, 0)
            with v.Fori(0, NE // 2 - 1) as q:
                for b in range(2):
                    expert(2 * q + (1 + b), 1 - b)
            expert(NE - 1, 1, last=True)
            output(NE - 1, 1, expert_item(NE - 1, 2 * KT))
            for i in range(NT):
                v.wait_ge(s_frt, i + 1)
                vc_.link(v.reciprocal(frs[:, i:i + 1], frs[:, i:i + 1]))
                v.scalar_tensor_tensor(fin[i], fin[i], frs[:, i:i + 1], g_fin, ALU.mult, ALU.mult).then_inc(s_fo, 1)

        @block.gpsimd
        def _(gp):
            def first_low(n):
                w = KT * (P if n < 12 else QK)
                gp.wait_ge(s_ihi, 1 + n + 1)
                gp.tensor_tensor(w_lo[:, n % 2, 0:w], slot[n // 2 % 2][:, n % 2 * D:n % 2 * D + w], w_hi[:, n % 2, 0:w].bitcast(F32), ALU.subtract).then_inc(s_ilo, 1)

            gp.wait_ge(s_ihi, 1)
            gp.tensor_tensor(v_lo[:], wv, v_hi[:].bitcast(F32), ALU.subtract).then_inc(s_ilo, 1)
            for n in range(2):
                first_low(n)
            gp.wait_ge(s_ilo, 3)
            gp.wait_ge(tps, 2 * T_IN)
            gp.memset(QH[64:96, 0:4, :], 1.0).then_inc(s_aug, 1)
            gp.wait_ge(s_h, 8)
            gp.memset(KH[64:96, 0:4, :], 0.0).then_inc(s_aug, 1)
            gp.wait_ge(s_aug, 2)
            for n in range(2, 13):
                first_low(n)
            gp.wait_ge(s_ilo, 14)
            gp.wait_ge(s_rot, 1)
            for h in range(4):
                last = gp.tensor_copy(KH[64:96, 4 + h, :], krope[64:96])
            last.then_inc(s_krc, 1)
            gp.wait_ge(s_krc, 1)
            gp.wait_ge(evv, T_MT)
            gp.wait_ge(eva, T_MT)
            gp.wait_ge(s_rot, 5)
            def stage_swa(q0, k0, w, b):
                gp.tensor_copy(qs[b], swaq[:, :, q0])
                gp.tensor_copy(ks[b][:, 0:w], swak[:, k0]).then_inc(s_stage, 1)
            stage_swa(slice(0, P), slice(0, P), P, 0)
            stage_swa(slice(P, 2 * P), slice(0, 2 * P), 2 * P, 1)
            with gp.Fori(1, NT // 2) as m:
                for b in range(2):
                    n = 2 * m + b
                    gp.wait_ge(s_S, m * 16 + 8 * (b - 1))
                    stage_swa(bass.ds(n * P, P), bass.ds(n * P - P, 2 * P), 2 * P, b)
            gp.wait_ge(s_frow, 16)
            for b in range(2):
                gp.wait_ge(s_S, 8 * (NT - 1 + b))
                gp.tensor_copy(qh[b][0:QK], QH[0:QK, b, :]).then_inc(s_stage, 1)
            with gp.Fori(1, CH // 2) as m:
                for b in range(2):
                    gp.wait_ge(s_S, m * 16 + (8 * (b - 1) + U_DENSE))
                    gp.tensor_copy(qh[b][0:QK], QH[0:QK, bass.ds(2 * m + b, 1), :].rearrange("p a c -> p (a c)")).then_inc(s_stage, 1)
            def weight_low(gg, c, q):
                gp.wait_ge(s_whi, 2 * gg + (q + 1))
                gp.tensor_tensor(w_lo[:, q, :], slot[c][:, q * D:(q + 1) * D], w_hi[:, q, :].bitcast(F32), ALU.subtract).then_inc(s_wlo, 1)

            def gated_low(half, k, q):
                gp.wait_ge(s_ahi, k + (half * FT + 1))
                gp.tensor_tensor(a_lo[:, q, :], act[:, k, :], a_hi[:, q, :].bitcast(F32), ALU.subtract).then_inc(s_alo, 1)

            for q in range(2):
                weight_low(G_OUT, 0, q)
            with gp.Fori(0, 2) as m:
                for c in range(2):
                    for q in range(2):
                        weight_low(2 * m + (G_OUT + c + 1), 1 - c, q)
            gp.wait_ge(xld, 16)
            for k in range(KT):
                gp.wait_ge(s_zn, k + 1)
                gp.tensor_tensor(xT[:, k, :], xT[:, k, :], zT[:, k, :], ALU.add).then_inc(s_x, 1)
            for half in range(2):
                sl = G_UP[half] % 2
                def up_low(j):
                    for b in range(2):
                        for q in range(2):
                            weight_low(2 * j + (G_UP[half] + b + 1), (sl + b + 1) % 2, q)
                with gp.Fori(0, FT // 2 - 1) as j:
                    up_low(j)
                for q in range(2):
                    gated_low(half, q, q)
                up_low(FT // 2 - 1)
                sl = G_DN[half] % 2
                with gp.Fori(0, (FT // 2 - 1) // 2) as m:
                    for c in range(2):
                        for q in range(2):
                            weight_low(2 * m + (G_DN[half] + c + 1), (sl + c + 1) % 2, q)
                            gated_low(half, 4 * m + (2 * c + 2 + q), q)
                for q in range(2):
                    weight_low((G_UP[1], G_IN2)[half], (G_UP[1], G_IN2)[half] % 2, q)
            for k in range(KT):
                gp.wait_ge(s_zn, 2 * KT + k + 1)
                gp.tensor_tensor(xT[:, k, HALF:S], xT[:, k, HALF:S], yT[:, k, :], ALU.add).then_inc(s_x, 1)
            for n in range(2, 18):
                weight_low(G_IN2 + n // 2, (n // 2) % 2, n % 2)
            gp.wait_ge(s_rot, 10)
            gp.wait_ge(s_cv, 4)

            def stage(q0, k0, w, b):
                gp.tensor_copy(qs[b], q2[:, :, q0])
                gp.tensor_copy(ks[b][:, 0:w], k2[:, k0]).then_inc(s_stage, 1)
            stage(slice(0, P), slice(0, 2 * P), 2 * P, 0)
            stage(slice(P, 2 * P), slice(0, 3 * P), 3 * P, 1)
            for n in range(2):
                weight_low(G_OUT2, G_OUT2 % 2, n)
            gp.wait_ge(tps, 2 * T_AT)
            for c in range(4):
                gp.tensor_copy(c_hi[:, c, :], convm[:, c, :]).then_inc(s_chi, 1)
            for c in range(4):
                gp.wait_ge(s_chi, c + 1)
                gp.tensor_tensor(c_lo[:, c, :], convm[:, c, :], c_hi[:, c, :].bitcast(F32), ALU.subtract).then_inc(s_clo, 1)
            with gp.Fori(1, NT // 2 - 1) as m:
                for b in range(2):
                    n = 2 * m + b
                    gp.wait_ge(s_S, m * 16 + (U_ATT2 + 8 * (b - 1)))
                    stage(bass.ds(n * P, P), bass.ds(n * P - P, 3 * P), 3 * P, b)
            gp.wait_ge(s_S, U_ATT2 + 8 * (NT - 3))
            stage(slice(S - 2 * P, S - P), slice(S - 3 * P, S), 3 * P, 0)
            gp.wait_ge(s_S, U_ATT2 + 8 * (NT - 2))
            stage(slice(S - P, S), slice(S - 2 * P, S), 2 * P, 1)
            gp.memset(gpad, 0.0).then_inc(s_x3, 1)
            for m in range(KT):
                if m + 2 < KT:
                    weight_low(G_OUT2 + m // 2 + 1, (G_OUT2 + m // 2 + 1) % 2, m % 2)
                gp.wait_ge(eva, T_OUT2 + m + 1)
                gp.tensor_tensor(xT[:, m, HALF:S], xT[:, m, HALF:S], gt1o[m % 2], ALU.add).then_inc(s_x3, 1)
            gp.wait_ge(s_tkst[0], 16 * NT)
            gp.wait_ge(s_tkst[1], 16 * NT)
            gc = Chain(gp, gch)

            def gather(e):
                b = e % 2
                gp.wait_ge(s_idx, e + 1)
                gc.link(gp.tensor_copy(idxs[b], idxu[:, e:e + 1]))
                gp.indirect_dma_start(out=xs[b], out_offset=None, in_=h_d,
                                      in_offset=bass.IndirectOffsetOnAxis(ap=idxs[b], axis=0)).then_inc(s_gat[b], 16)
            for e in range(2):
                gather(e)
                gp.memset(gpad, 0.0).then_inc(s_yf, 1)
            for e in range(NE):
                b = e % 2
                if e + 2 < NE:
                    gp.wait_ge(s_gs, e + 1)
                    gp.wait_ge(s_xt, e + 1)
                    gather(e + 2)
                gc.link(gp.tensor_copy(odxs[b], idxu[:, e:e + 1]))
                gp.wait_ge(s_ys, e + 2)
                gp.indirect_dma_start(out=acc_d, out_offset=bass.IndirectOffsetOnAxis(ap=odxs[b], axis=0), in_=yx[b], in_offset=None,
                                      compute_op=ALU.add).then_inc(s_sc[b], 16)
                gp.wait_ge(s_sc[b], 16 * (e // 2 + 1))
                gp.memset(gpad, 0.0).then_inc(s_yf, 1)


def _tiles(w, tile=P):
    k, n = w.shape
    return w.reshape(k // P, P, n // tile, tile).transpose(1, 2, 0, 3).reshape(P, -1)


def _cols(v):
    return np.asarray(v).reshape(-1, P).T


def _constants():
    r = np.arange(P)
    c = np.zeros((P, NCONST), np.float32)

    def put(name, a):
        c[:, CONST[name][0]:CONST[name][0] + CONST[name][1]] = a
    put("ident", np.eye(P))
    put("causal", np.where(r[None, :] <= r[:, None], 0.0, NEG))
    put("left", np.where(r[None, :] >= r[:, None], 0.0, NEG))
    put("mean", np.full((P, P), 1.0 / D))
    s16 = np.zeros((P, QK))
    for i in range(32):
        s16[64 + i, 64 + (i + 16) % 32] = 1.0
    put("swap16", s16)
    s32 = np.zeros((P, P))
    for i in range(P):
        s32[i, i // 64 * 64 + (i + 32) % 64] = 1.0
    put("swap32", s32)
    put("flip", np.eye(P)[::-1])
    put("slot", r[:, None])
    pos = np.arange(S, dtype=np.float32)
    inv = (np.float32(10000.0) ** (-(np.arange(16, dtype=np.float32) * np.float32(2.0) / np.float32(32)))).astype(np.float32)
    ang = pos[None, :] * inv[:, None]
    rope1 = np.stack([np.concatenate([np.cos(ang)] * 2), np.concatenate([-np.sin(ang), np.sin(ang)])], 1)
    inv2 = (np.float32(10000.0) ** (-np.arange(16, dtype=np.float32) / np.float32(16))).astype(np.float32)
    grid = np.arange(S)
    ang2 = np.concatenate([(grid // 64).astype(np.float32)[None] * inv2[:, None], (grid % 64).astype(np.float32)[None] * inv2[:, None]])
    rope2 = np.stack([np.concatenate([np.cos(ang2)] * 4), np.concatenate([-np.sin(ang2), np.sin(ang2)] * 2)], 1)
    dist = 255 - np.arange(384)
    d = np.maximum(dist, 0)
    ratio = np.log(np.maximum(d, 1).astype(np.float32) / np.float32(16)) / np.float32(math.log(128 / 16))
    large = np.minimum(16 + (ratio * np.float32(16)).astype(np.int32), 31)
    bucket = np.where(d < 16, d, large)
    onehot = (np.arange(32)[:, None] == bucket[None, :]).astype(np.float32)
    extmask = np.broadcast_to(np.where((dist >= 0) & (dist < P), 0.0, NEG), (8, 384))
    f = lambda a: np.ascontiguousarray(a, np.float32)
    return {"const": c, "rope1": f(rope1), "rope2": f(rope2), "onehot": onehot, "extmask": f(extmask)}


def _layout(x):
    a = {k: np.asarray(v) for k, v in x.items()}
    w = a["w_in"][0]
    pair = np.concatenate([np.r_[t * HD:(t + 1) * HD, (t + 4) * HD:(t + 5) * HD] for t in range(4)])
    fx, ml = 768, 768 + 772
    rope = ml + 384 + np.arange(32)
    order = np.concatenate([ml + np.arange(384), fx + np.arange(512), 512 + np.arange(128), pair])
    last = np.concatenate([fx + 768 + np.arange(4), rope, rope[:28], rope])
    w2 = a["w_in_2"][0]
    conv = np.concatenate([768 + np.arange(c * P, (c + 1) * P) + o for c in range(4) for o in (512, 1024, 0)])
    order2 = np.concatenate([512 + np.arange(256), pair, conv])
    wup = a["w_up"][0].reshape(KT, P, 2, FT, P).transpose(1, 3, 2, 0, 4).reshape(P, -1)
    wdn = a["w_down"][0].reshape(FT, P, D).transpose(1, 0, 2).reshape(P, -1)
    cols = np.concatenate([_cols(v) for v in (
        a["attn_pre_norm"], a["group_norm"], a["attn_post_norm"], a["ffn_pre_norm"], a["conv_w"], a["conv_b"], a["ffn_post_norm"],
        a["q_latent_norm"], a["kv_latent_norm"], a["c_2"], a["c_ctx_2"], a["b_ada_2"], a["g_mix_2"], a["conv_w_2"], a["g_ffn_2"])], 1)
    out = {
        "xT": a["x"][0].T.reshape(KT, P, S).transpose(1, 0, 2), "ctxT": a["ctx_2"][0].T.reshape(KT, P, CTX).transpose(1, 0, 2),
        "w_in": np.concatenate([_tiles(w[:, order]), _tiles(w[:, last], QK)], 1),
        "w_in_v": w[:, np.r_[640:768, fx + 512:fx + 768]].reshape(KT, P, 384).transpose(1, 0, 2),
        "w_uq": a["w_uq"][0].reshape(2, P, 4 * QK).transpose(1, 0, 2), "w_ukv": a["w_ukv"][0],
        "w_out": _tiles(a["w_out"][0]), "w_up": wup, "w_down": wdn,
        "w_in2": _tiles(w2[:, order2]), "w_out2": _tiles(a["w_out_2"][0]), "cols": cols,
    }
    for n in ("forget_bias", "swa_sinks", "sink_2", "rel_bias", "w_ada_2", "b_ada_2", "g_final_2", "w_router_2", "w_gate_2", "w_up_2", "w_down_2"):
        out[n] = a[n]
    return out


def kernel(**inputs):
    import concourse.bacc as bacc
    from concourse.bass_utils import run_bass_kernel_spmd as run

    nc = bacc.Bacc("TRN2", target_bir_lowering=False, num_devices=1)
    arrays, T = {}, {}
    for name, x in {**_layout(inputs), **_constants()}.items():
        x = np.ascontiguousarray(x)
        arrays["in_" + name] = x
        T[name] = nc.dram_tensor("in_" + name, x.shape, mybir.dt.from_np(x.dtype), kind="ExternalInput").ap()
    T["out"] = nc.dram_tensor("out_rows", (1, S, D), F32, kind="ExternalOutput").ap()
    bass_two_blocks(nc, T)
    r = run(nc, [arrays], core_ids=[0])
    return r.results[0]["out_rows"]
```
